# Optimizing a Trainium2 kernel written in Bass

```python
import math
import jax, jax.numpy as jnp
from jax import lax
import numpy as np

D_MODEL = 1024
BATCH = 1
SEQ = 512
DEPTH = 1
DEC_BATCH = 8
DEC_SEQ = 4
PAST_LEN = 2048
PAGE_SIZE = 128

MLA_HEADS = 8
Q_LORA = 384
KV_LORA = 256
NOPE_DIM = 128
ROPE_DIM = 64
V_DIM = 128
ROPE_THETA = 10000.0
Q_BLOCK = 128
SSM_HEADS = 32
SSM_HEAD_DIM = 64
D_INNER = SSM_HEADS * SSM_HEAD_DIM
SSM_GROUPS = 4
HEADS_PER_GROUP = SSM_HEADS // SSM_GROUPS
D_STATE = 128
CONV_W = 4
CONV_DIM = D_INNER + 2 * SSM_GROUPS * D_STATE
SSD_BLOCK = 128
N_MEM = 256
MEM_HEADS = 4
MEM_HEAD_DIM = 256
MEM_WIDTH = MEM_HEADS * MEM_HEAD_DIM
D_FF = 4 * D_MODEL
N_BRANCH = 3
ALPHA = (2 * DEPTH) ** 0.25
BETA = (8 * DEPTH) ** -0.25
LN_EPS = 1e-5
RMS_EPS = 1e-6
IN_SIZES = (Q_LORA, KV_LORA, ROPE_DIM, D_INNER, CONV_DIM, SSM_HEADS, MEM_WIDTH, N_BRANCH * D_MODEL)
D_IN = Q_LORA + KV_LORA + ROPE_DIM + D_INNER + CONV_DIM + SSM_HEADS + MEM_WIDTH + N_BRANCH * D_MODEL

kernel_name = "hybrid_mla_ssd_mem_decoder_step"

F32 = jnp.float32

def _split_in(proj):
    idx = np.cumsum(IN_SIZES)[:-1].tolist()
    return jnp.split(proj, idx, axis=-1)

def _rms_norm(x, g):
    xf = x.astype(F32)
    y = xf * lax.rsqrt(jnp.mean(xf * xf, -1, keepdims=True) + RMS_EPS)
    return (y * g.astype(F32)).astype(x.dtype)

def _layer_norm(x, g, b):
    xf = x.astype(F32)
    mu = jnp.mean(xf, -1, keepdims=True)
    var = jnp.mean(jnp.square(xf - mu), -1, keepdims=True)
    return ((xf - mu) * lax.rsqrt(var + LN_EPS) * g.astype(F32) + b.astype(F32)).astype(x.dtype)

def _rope(x, pos):
    half = ROPE_DIM // 2
    inv = ROPE_THETA ** (-jnp.arange(half, dtype=F32) / half)
    ang = pos.astype(F32)[:, None] * inv[None, :]
    ang = ang.reshape((1, pos.shape[0]) + (1,) * (x.ndim - 3) + (half,))
    cos, sin = jnp.cos(ang), jnp.sin(ang)
    xf = x.astype(F32)
    x1, x2 = xf[..., :half], xf[..., half:]
    return jnp.concatenate([x1 * cos - x2 * sin, x1 * sin + x2 * cos], -1).astype(x.dtype)

def _mla_queries(cq, q_norm_g, w_uq, w_uk, pos):
    q = jnp.einsum('blr,rhd->blhd', _rms_norm(cq, q_norm_g), w_uq)
    q_nope, q_rope = q[..., :NOPE_DIM], q[..., NOPE_DIM:]
    q_lat = jnp.einsum('blhd,chd->blhc', q_nope, w_uk)
    return q_lat, _rope(q_rope, pos)

def _mla_scores(q_lat, q_rope, ckv, krope):
    s = jnp.einsum('bqhc,bkc->bhqk', q_lat, ckv) + jnp.einsum('bqhr,bkr->bhqk', q_rope, krope)
    return s.astype(F32) * ((NOPE_DIM + ROPE_DIM) ** -0.5)

def _mla_prompt_attend(q_lat, q_rope, ckv, krope):
    b, L = q_lat.shape[:2]
    qb = min(Q_BLOCK, L)
    nblk = L // qb
    ql = q_lat.reshape(b, nblk, qb, MLA_HEADS, KV_LORA).swapaxes(0, 1)
    qr = q_rope.reshape(b, nblk, qb, MLA_HEADS, ROPE_DIM).swapaxes(0, 1)
    kpos = jnp.arange(L)

    def block(args):
        i, qlb, qrb = args
        s = _mla_scores(qlb, qrb, ckv, krope)
        qpos = i * qb + jnp.arange(qb)
        s = jnp.where(kpos[None, :] <= qpos[:, None], s, -jnp.inf)
        p = jax.nn.softmax(s, axis=-1).astype(ckv.dtype)
        return jnp.einsum('bhqk,bkc->bqhc', p, ckv)

    o = lax.map(block, (jnp.arange(nblk), ql, qr))
    return o.swapaxes(0, 1).reshape(b, L, MLA_HEADS, KV_LORA)

def _mla_sample_attend(q_lat, q_rope, ckv_new, krope_new, ckv_past, krope_past):
    T = q_lat.shape[1]
    s_past = _mla_scores(q_lat, q_rope, ckv_past, krope_past)
    s_new = _mla_scores(q_lat, q_rope, ckv_new, krope_new)
    s_new = jnp.where(jnp.tril(jnp.ones((T, T), bool)), s_new, -jnp.inf)
    p = jax.nn.softmax(jnp.concatenate([s_past, s_new], -1), axis=-1).astype(ckv_new.dtype)
    P = ckv_past.shape[1]
    return (jnp.einsum('bhqk,bkc->bqhc', p[..., :P], ckv_past)
            + jnp.einsum('bhqk,bkc->bqhc', p[..., P:], ckv_new))

def _mla_out(o_lat, w_uv):
    b, L = o_lat.shape[:2]
    return jnp.einsum('bqhc,chv->bqhv', o_lat, w_uv).reshape(b, L, MLA_HEADS * V_DIM)

def _causal_conv(xbc_ext, conv_w, conv_b, L):
    out = conv_b.astype(F32) + sum(conv_w[k].astype(F32) * xbc_ext[:, k:k + L].astype(F32) for k in range(CONV_W))
    return jax.nn.silu(out)

def _ssd(x, dt, a_coef, Bm, Cm, s0):
    b, L = x.shape[:2]
    q = math.gcd(L, SSD_BLOCK)
    nc = L // q

    def chunks(t):
        return t.reshape((b, nc, q) + t.shape[2:]).swapaxes(0, 1)

    tri = jnp.tril(jnp.ones((q, q), bool))[None, :, :, None, None]

    def step(S, inp):
        xc, dtc, Bc, Cc = inp
        cum = jnp.cumsum(dtc * a_coef, axis=1)
        seg = cum[:, :, None] - cum[:, None, :]
        decay = jnp.exp(jnp.where(tri, seg, -jnp.inf))
        cb = jnp.einsum('bign,bjgn->bijg', Cc, Bc)
        w = cb[..., None] * decay * dtc[:, None]
        y = jnp.einsum('bijgh,bjghp->bighp', w, xc)
        y = y + jnp.einsum('bign,bghpn->bighp', Cc, S) * jnp.exp(cum)[..., None]
        last = cum[:, -1]
        wb = dtc * jnp.exp(last[:, None] - cum)
        S = S * jnp.exp(last)[..., None, None] + jnp.einsum('bjgh,bjgn,bjghp->bghpn', wb, Bc, xc)
        return S, y

    S, ys = lax.scan(step, s0, (chunks(x), chunks(dt), chunks(Bm), chunks(Cm)))
    return ys.swapaxes(0, 1).reshape(x.shape), S

def _mamba(z, xbc_ext, dt_raw, s0, conv_w, conv_b, dt_bias, a_log, d_skip, ssm_norm_g):
    b, L = z.shape[:2]
    xbc = _causal_conv(xbc_ext, conv_w, conv_b, L)
    xs, Bm, Cm = jnp.split(xbc, [D_INNER, D_INNER + SSM_GROUPS * D_STATE], axis=-1)
    xs = xs.reshape(b, L, SSM_GROUPS, HEADS_PER_GROUP, SSM_HEAD_DIM)
    Bm = Bm.reshape(b, L, SSM_GROUPS, D_STATE)
    Cm = Cm.reshape(b, L, SSM_GROUPS, D_STATE)
    dt = jax.nn.softplus(dt_raw.astype(F32) + dt_bias.astype(F32)).reshape(b, L, SSM_GROUPS, HEADS_PER_GROUP)
    a_coef = -jnp.exp(a_log.astype(F32)).reshape(SSM_GROUPS, HEADS_PER_GROUP)
    y, S = _ssd(xs, dt, a_coef, Bm, Cm, s0)
    y = y + d_skip.astype(F32).reshape(SSM_GROUPS, HEADS_PER_GROUP)[..., None] * xs
    y = y.reshape(b, L, D_INNER) * jax.nn.silu(z.astype(F32))
    yg = y.reshape(b, L, SSM_GROUPS, D_INNER // SSM_GROUPS)
    yg = yg * lax.rsqrt(jnp.mean(yg * yg, -1, keepdims=True) + RMS_EPS)
    y = yg.reshape(b, L, D_INNER) * ssm_norm_g.astype(F32)
    return y.astype(z.dtype), S.reshape(b, SSM_HEADS, SSM_HEAD_DIM, D_STATE).astype(z.dtype)

def _mem_kv(mem, w_mem_k, w_mem_v):
    return jnp.einsum('bmd,dhe->bmhe', mem, w_mem_k), jnp.einsum('bmd,dhe->bmhe', mem, w_mem_v)

def _mem_attend(mq, mem_k, mem_v):
    b, L = mq.shape[:2]
    q = mq.reshape(b, L, MEM_HEADS, MEM_HEAD_DIM)
    s = jnp.einsum('blhe,bmhe->bhlm', q, mem_k).astype(F32) * (MEM_HEAD_DIM ** -0.5)
    p = jax.nn.softmax(s, axis=-1).astype(mem_v.dtype)
    return jnp.einsum('bhlm,bmhe->blhe', p, mem_v).reshape(b, L, MEM_WIDTH)

def _merge_ffn(x, o_mla, o_ssm, o_mem, g_raw, b_gate, w_o_mla, w_o_ssm, w_o_mem, w_out,
               ln1_g, ln1_b, w_up, b_up, w_down, b_down, ln2_g, ln2_b):
    g = jax.nn.sigmoid((g_raw + b_gate).astype(F32)).astype(x.dtype)
    g_a, g_b, g_m = jnp.split(g, N_BRANCH, axis=-1)
    m = g_a * (o_mla @ w_o_mla) + g_b * (o_ssm @ w_o_ssm) + g_m * (o_mem @ w_o_mem)
    x1 = _layer_norm(ALPHA * x + m @ w_out, ln1_g, ln1_b)
    h = jnp.square(jax.nn.relu(x1 @ w_up + b_up))
    return _layer_norm(ALPHA * x1 + h @ w_down + b_down, ln2_g, ln2_b)

def _normal(k, shape, scale):
    return jax.random.normal(k, shape, F32) * scale

def setup_inputs(seed: int = 0) -> dict:
    key = jax.random.key(seed)
    ks = jax.random.split(key, 40)
    n_pages = PAST_LEN // PAGE_SIZE
    n_used = DEC_BATCH * n_pages
    n_pool = n_used + n_used // 4
    page_table = jax.random.permutation(ks[0], n_pool)[:n_used].reshape(DEC_BATCH, n_pages).astype(jnp.int32)
    dt0 = jnp.exp(jax.random.uniform(ks[1], (SSM_HEADS,), F32, math.log(1e-3), math.log(1e-1)))
    return {
        "x_prompt": _normal(ks[2], (BATCH, SEQ, D_MODEL), 1.0),
        "x_sample": _normal(ks[3], (DEC_BATCH, DEC_SEQ, D_MODEL), 1.0),
        "mem_prompt": _normal(ks[4], (BATCH, N_MEM, D_MODEL), 1.0),
        "cache_ckv": _normal(ks[5], (n_pool, PAGE_SIZE, KV_LORA), 1.0),
        "cache_krope": _normal(ks[6], (n_pool, PAGE_SIZE, ROPE_DIM), 1.0),
        "page_table": page_table,
        "cache_mem_k": _normal(ks[7], (DEC_BATCH, N_MEM, MEM_HEADS, MEM_HEAD_DIM), 1.0),
        "cache_mem_v": _normal(ks[8], (DEC_BATCH, N_MEM, MEM_HEADS, MEM_HEAD_DIM), 1.0),
        "state_ssm": _normal(ks[9], (DEC_BATCH, SSM_HEADS, SSM_HEAD_DIM, D_STATE), 0.1),
        "state_conv": _normal(ks[10], (DEC_BATCH, CONV_W - 1, CONV_DIM), 1.0),
        "w_in": _normal(ks[11], (D_MODEL, D_IN), D_MODEL ** -0.5),
        "q_norm_g": 1.0 + _normal(ks[12], (Q_LORA,), 0.02),
        "w_uq": _normal(ks[13], (Q_LORA, MLA_HEADS, NOPE_DIM + ROPE_DIM), Q_LORA ** -0.5),
        "kv_norm_g": 1.0 + _normal(ks[14], (KV_LORA,), 0.02),
        "w_uk": _normal(ks[15], (KV_LORA, MLA_HEADS, NOPE_DIM), KV_LORA ** -0.5),
        "w_uv": _normal(ks[16], (KV_LORA, MLA_HEADS, V_DIM), KV_LORA ** -0.5),
        "conv_w": _normal(ks[17], (CONV_W, CONV_DIM), CONV_W ** -0.5),
        "conv_b": _normal(ks[18], (CONV_DIM,), 0.02),
        "dt_bias": dt0 + jnp.log(-jnp.expm1(-dt0)),
        "a_log": jnp.log(jax.random.uniform(ks[19], (SSM_HEADS,), F32, 1.0, 16.0)),
        "d_skip": 1.0 + _normal(ks[20], (SSM_HEADS,), 0.1),
        "ssm_norm_g": 1.0 + _normal(ks[21], (D_INNER,), 0.02),
        "w_mem_k": _normal(ks[22], (D_MODEL, MEM_HEADS, MEM_HEAD_DIM), D_MODEL ** -0.5),
        "w_mem_v": _normal(ks[23], (D_MODEL, MEM_HEADS, MEM_HEAD_DIM), D_MODEL ** -0.5),
        "b_gate": _normal(ks[24], (N_BRANCH * D_MODEL,), 0.02),
        "w_o_mla": _normal(ks[25], (MLA_HEADS * V_DIM, D_MODEL), (MLA_HEADS * V_DIM) ** -0.5),
        "w_o_ssm": _normal(ks[26], (D_INNER, D_MODEL), D_INNER ** -0.5),
        "w_o_mem": _normal(ks[27], (MEM_WIDTH, D_MODEL), MEM_WIDTH ** -0.5),
        "w_out": _normal(ks[28], (D_MODEL, D_MODEL), BETA * D_MODEL ** -0.5),
        "ln1_g": 1.0 + _normal(ks[29], (D_MODEL,), 0.02),
        "ln1_b": _normal(ks[30], (D_MODEL,), 0.02),
        "w_up": _normal(ks[31], (D_MODEL, D_FF), D_MODEL ** -0.5),
        "b_up": _normal(ks[32], (D_FF,), 0.02),
        "w_down": _normal(ks[33], (D_FF, D_MODEL), BETA * D_FF ** -0.5),
        "b_down": _normal(ks[34], (D_MODEL,), 0.02),
        "ln2_g": 1.0 + _normal(ks[35], (D_MODEL,), 0.02),
        "ln2_b": _normal(ks[36], (D_MODEL,), 0.02),
    }

def reference(x_prompt, x_sample, mem_prompt, cache_ckv, cache_krope, page_table, cache_mem_k, cache_mem_v,
              state_ssm, state_conv, w_in, q_norm_g, w_uq, kv_norm_g, w_uk, w_uv, conv_w, conv_b, dt_bias,
              a_log, d_skip, ssm_norm_g, w_mem_k, w_mem_v, b_gate, w_o_mla, w_o_ssm, w_o_mem, w_out,
              ln1_g, ln1_b, w_up, b_up, w_down, b_down, ln2_g, ln2_b):
    ssm_w = (conv_w, conv_b, dt_bias, a_log, d_skip, ssm_norm_g)
    merge_w = (b_gate, w_o_mla, w_o_ssm, w_o_mem, w_out, ln1_g, ln1_b, w_up, b_up, w_down, b_down, ln2_g, ln2_b)

    bp, L = x_prompt.shape[:2]
    pos_p = jnp.arange(L)
    cq, ckv_raw, kr_raw, z, xbc, dt_raw, mq, g_raw = _split_in(x_prompt @ w_in)
    ckv_p = _rms_norm(ckv_raw, kv_norm_g)
    krope_p = _rope(kr_raw, pos_p)
    q_lat, q_rope = _mla_queries(cq, q_norm_g, w_uq, w_uk, pos_p)
    o_mla = _mla_out(_mla_prompt_attend(q_lat, q_rope, ckv_p, krope_p), w_uv)
    xbc_ext = jnp.concatenate([jnp.zeros((bp, CONV_W - 1, CONV_DIM), xbc.dtype), xbc], axis=1)
    s0 = jnp.zeros((bp, SSM_GROUPS, HEADS_PER_GROUP, SSM_HEAD_DIM, D_STATE), F32)
    o_ssm, ssm_p = _mamba(z, xbc_ext, dt_raw, s0, *ssm_w)
    conv_p = xbc_ext[:, -(CONV_W - 1):]
    mem_k_p, mem_v_p = _mem_kv(mem_prompt, w_mem_k, w_mem_v)
    o_mem = _mem_attend(mq, mem_k_p, mem_v_p)
    y_prompt = _merge_ffn(x_prompt, o_mla, o_ssm, o_mem, g_raw, *merge_w)

    bs, T = x_sample.shape[:2]
    past = page_table.shape[1] * PAGE_SIZE
    pos_s = past + jnp.arange(T)
    cq, ckv_raw, kr_raw, z, xbc, dt_raw, mq, g_raw = _split_in(x_sample @ w_in)
    ckv_s = _rms_norm(ckv_raw, kv_norm_g)
    krope_s = _rope(kr_raw, pos_s)
    q_lat, q_rope = _mla_queries(cq, q_norm_g, w_uq, w_uk, pos_s)
    ckv_past = cache_ckv[page_table].reshape(bs, past, KV_LORA)
    krope_past = cache_krope[page_table].reshape(bs, past, ROPE_DIM)
    o_mla = _mla_out(_mla_sample_attend(q_lat, q_rope, ckv_s, krope_s, ckv_past, krope_past), w_uv)
    xbc_ext = jnp.concatenate([state_conv.astype(xbc.dtype), xbc], axis=1)
    s0 = state_ssm.astype(F32).reshape(bs, SSM_GROUPS, HEADS_PER_GROUP, SSM_HEAD_DIM, D_STATE)
    o_ssm, ssm_s = _mamba(z, xbc_ext, dt_raw, s0, *ssm_w)
    conv_s = xbc_ext[:, -(CONV_W - 1):]
    o_mem = _mem_attend(mq, cache_mem_k, cache_mem_v)
    y_sample = _merge_ffn(x_sample, o_mla, o_ssm, o_mem, g_raw, *merge_w)

    return (y_prompt, y_sample, ckv_p, krope_p, mem_k_p, mem_v_p, ssm_p, conv_p, ckv_s, krope_s, ssm_s, conv_s)


_drawn_inputs = setup_inputs


def setup_inputs(seed=0):
    import zlib

    import numpy as np

    out = dict(_drawn_inputs(seed))
    spreads = {}
    factors = {'cache_ckv': 5.577,
     'cache_krope': 8.0,
     'q_norm_g': 8.0,
     'kv_norm_g': 8.551,
     'd_skip': 2.849,
     'ssm_norm_g': 22.772,
     'b_gate': 8.0,
     'ln1_g': 2.812,
     'ln1_b': 2.679,
     'b_up': 4.549,
     'b_down': 19.042,
     'ln2_g': 24.626,
     'ln2_b': 22.843,
     'cache_mem_k': 6.431,
     'cache_mem_v': 5.183,
     'w_o_mem': 4.357}
    for name, (base, spread) in spreads.items():
        noise = np.random.default_rng([zlib.crc32(name.encode()), seed]).standard_normal(out[name].shape)
        drawn = base * np.exp(spread * noise) if base else spread * noise
        out[name] = __import__('jax').numpy.asarray(drawn.astype(out[name].dtype))
    for name, factor in factors.items():
        out[name] = (out[name] * factor).astype(out[name].dtype)
    return out
```

```python
import numpy as np
from contextlib import ExitStack, contextmanager

P = 128
D_MODEL, SEQ, DEC_BATCH, DEC_SEQ = 1024, 512, 8, 4
PAGE, N_PAGES, N_POOL = 128, 16, 160
MLA_HEADS, Q_LORA, KV_LORA, NOPE, ROPE, V_DIM = 8, 384, 256, 128, 64, 128
SSM_HEADS, HEAD_DIM, GROUPS, D_STATE, CONV_W = 32, 64, 4, 128, 4
D_INNER = SSM_HEADS * HEAD_DIM
CONV_DIM = D_INNER + 2 * GROUPS * D_STATE
N_MEM, MEM_HEADS, MEM_DIM = 256, 4, 256
D_FF = 4 * D_MODEL
ALPHA = 2 ** 0.25
LN_EPS, RMS_EPS = 1e-5, 1e-6
THETA = 10000.0

NS = DEC_BATCH * DEC_SEQ
T = SEQ + NS
HT = T // 2
KC = D_MODEL // P
NB = SEQ // P
HG = SSM_HEADS // GROUPS
GW = HG * HEAD_DIM
GC = GW // P
QC = GC + 2
NC = CONV_DIM // P
EXT_P = CONV_W - 1 + SEQ
EXT_S = CONV_W - 1 + DEC_SEQ
EXT = EXT_P + DEC_BATCH * EXT_S
CL = EXT - (CONV_W - 1)
FC = D_FF // P
RING = 4
BLOCK = 1024
NEG = -1e30

_C = {}
def _const_layout():
    at = 0
    for name, n in (("ident", P), ("tri", P), ("last", P), ("ones", P), ("causal", P), ("fold", P),
                    ("tri_s", NS), ("last_s", NS), ("lastcol", DEC_BATCH), ("ofbatch", DEC_BATCH),
                    ("newmask", 2 * NS), ("sel", HG * P), ("selpair", HG // 2 * P),
                    ("rope", T), ("scanmask", T), ("half", 1), ("bmask", DEC_BATCH * NS)):
        _C[name] = (at, n)
        at += n
    return at
CW = _const_layout()

_V = {}
def _vec_layout():
    at = 0
    for name, n in (("qg", Q_LORA // P), ("kvg", KV_LORA // P), ("convw", NC * CONV_W), ("convb", NC),
                    ("dskip", D_INNER // P), ("ssmg", D_INNER // P), ("bgate", 3 * KC), ("ln1g", KC),
                    ("ln1b", KC), ("bup", FC), ("bdown", KC), ("ln2g", KC), ("ln2b", KC), ("dtb", 1), ("alog", 1)):
        _V[name] = (at, n)
        at += n
    return at
VW = _vec_layout()


def constants():
    c = np.zeros((P, CW), np.float32)
    def put(name, a):
        at, n = _C[name]
        c[:a.shape[0], at:at + n] = a.reshape(a.shape[0], n)
    r = np.arange(P)
    put("ident", np.eye(P))
    put("tri", (r[:, None] <= r[None, :]) * 1.0)
    last = np.zeros((P, P)); last[P - 1] = 1
    put("last", last)
    put("ones", np.ones((P, P)))
    put("causal", np.where(r[None, :] <= r[:, None], 0.0, NEG))
    put("fold", np.tile(np.eye(ROPE), (2, 2)))
    s = np.arange(NS)
    sb, st = s // DEC_SEQ, s % DEC_SEQ
    same = sb[:, None] == sb[None, :]
    put("tri_s", (same & (s[:, None] <= s[None, :])) * 1.0)
    put("last_s", (same & (st[:, None] == DEC_SEQ - 1)) * 1.0)
    b = np.arange(DEC_BATCH)
    put("lastcol", ((sb[:, None] == b) & (st[:, None] == DEC_SEQ - 1)) * 1.0)
    put("ofbatch", (sb[:, None] == b) * 1.0)
    row = np.arange(P)
    nm = np.zeros((P, 2, NS))
    for half in range(2):
        rb, rt = half * 4 + row // (MLA_HEADS * DEC_SEQ), row % DEC_SEQ
        nm[:, half] = np.where((sb[None] == rb[:, None]) & (st[None] <= rt[:, None]), 0.0, NEG)
    put("newmask", nm)
    sel = np.zeros((HG, HG, P)); pair = np.zeros((HG, HG // 2, P))
    for h in range(HG):
        sel[h, h] = 1
        pair[h, h // 2, HEAD_DIM * (h % 2):HEAD_DIM * (h % 2 + 1)] = 1
    put("sel", sel)
    put("selpair", pair)
    half = ROPE // 2
    pos = np.concatenate([np.arange(SEQ), np.tile(N_PAGES * PAGE + np.arange(DEC_SEQ), DEC_BATCH)])
    inv = (np.float32(THETA) ** (-np.arange(half, dtype=np.float32) / half)).astype(np.float32)
    ang = (inv[:, None] * pos.astype(np.float32)[None, :]).astype(np.float32).astype(np.float64)
    cos, sin = np.cos(ang), np.sin(ang)
    put("rope", np.concatenate([cos, cos, -sin, sin], 0))
    m = np.ones((P, T))
    m[:, 0:SEQ:P] = 0
    m[:, SEQ::DEC_SEQ] = 0
    put("scanmask", m)
    put("bmask", np.broadcast_to((sb[None, None, :] == b[None, :, None]) * 1.0, (P, DEC_BATCH, NS)))
    put("half", np.full((P, 1), 0.5))
    return c


class Count:
    def __init__(self, sem, start=0):
        self.sem, self.base, self.k, self.i, self.per = sem, start, 0, None, 0

    def next(self, n=1):
        self.k += n
        return self.value()

    def value(self):
        return self.base + self.k if self.i is None or self.per == 0 else self.i * self.per + (self.base + self.k)

    def enter(self, i, per):
        self.base, self.k, self.i, self.per = self.base + self.k, 0, i, per

    def leave(self, trips):
        assert self.k == self.per, f"{self.sem} counts {self.k} a turn, not {self.per}"
        self.base, self.k, self.i, self.per = self.base + trips * self.per, 0, None, 0


@contextmanager
def turns(engine, trips, counts, per, name):
    with engine.Fori(0, trips) as i:
        for c in counts:
            c.enter(i, per.get(c.sem.name, 0))
        yield i
        found = {c.sem.name: c.k for c in counts if c.k}
        assert found == per, f"signals a turn of {name}: {found}"
    for c in counts:
        c.k = c.per
        c.leave(trips)


def v2(ap):
    return ap.rearrange("p (a n) -> p a n", a=2)

WORK = 24704
STAGES = ["dt", "ssm", "merge_b", "mla", "merge_a", "mem", "merge_m"]
PHASES = [("dt", 1, 1), ("ssm", GROUPS, QC + GC), ("merge_b", KC, 3), ("latents", 1, 6), ("heads", MLA_HEADS, 2),
          ("values", 1, 2), ("merge_a", KC, 2), ("mem_k", 4, 2), ("mem_v", 1, 8), ("mq", MEM_HEADS, 2),
          ("merge_m", KC, 2), ("out", KC // 4, 4), ("up", FC // 4, 4), ("down", KC // 2, 8)]
START = {}
for _i, (_n, _t, _p) in enumerate(PHASES):
    START[_n] = 0 if _i == 0 else (START[PHASES[_i - 1][0]] + PHASES[_i - 1][2]) % RING
CREDIT = {"acc0_free": 1, "acc1_free": 1, "blocks_begun": 8, "states_stored": 32, "keys_used": 4,
          "rows_used": 4}
SEMAPHORES = ["pe_step", "act_step", "dve_step", "const_loaded", "x_loaded", "vec_loaded", "conv_state_loaded",
              "weights_in_slot0", "weights_in_slot1", "weights_in_slot2", "weights_in_slot3", "blocks_begun",
              "acc0_ready", "acc1_ready", "acc0_free", "acc1_free", "stage_over", "stored",
              "dt_ready", "dt_turned", "cum_ready", "last_ready", "dt_v", "dt_u", "dt_w", "dt_ln", "cum_rows_ready",
              "cum_g_loaded", "wb_ready", "dec_ready",
              "conv_done", "conv_ready", "silu_ready", "x_turned", "turned_read", "b_turned", "b_tm_read", "b_tm_ready",
              "cb_ready", "cb_read", "add_ready", "add_read", "cum_s_ready", "states_loaded", "states_stored",
              "cum_spread", "pair_read", "decay_ready", "y_ready", "sq_ready", "sq_summed", "adds_ready", "adds_read",
              "var_ready", "std_ready", "e_pair_ready", "seg_ready", "seg_exp", "z_ready", "y_gated", "states_done",
              "gate_bias_ready", "gate_ready", "page_ids_loaded", "act_over", "squares_ready", "cq_summed", "ckv_summed",
              "kr_ready", "kr_folded", "krope_ready", "latents_ready", "new_turned", "new_read", "head_read",
              "q_lat_ready", "q_lat_read", "k_ready", "v_ready", "kv_read", "prob_ready", "prob_turned", "scores_ready",
              "exp_ready", "turned_out", "head_out", "max_ready", "lat_ready", "lat_read", "lat_turned", "o_lat_ready",
              "sample_out", "keys_used", "rows_used"]
SEMAPHORES += [f"{n}_in_slot{i}" for n in ("keys", "rows") for i in range(4)]
SEMAPHORES += [f"mem_{n}{i}_loaded" for n in "kv" for i in range(2)]
SEMAPHORES += ["mem_loaded", "mem_kv_ready", "kv_head_ready", "q_b_ready", "norm_in", "sums_ready", "norm_summed",
               "centred", "normed", "hidden_ready"]
PER = {
    "ssm_act": {"act_step": 35, "acc0_ready": 5, "acc1_ready": 5, "acc0_free": 5, "acc1_free": 5, "conv_done":
        6, "conv_ready": 6, "silu_ready": 6, "b_turned": 1, "b_tm_read": 1, "states_stored": 32, "cum_spread":
        4, "sq_ready": 4, "sq_summed": 4, "var_ready": 1, "std_ready": 1, "e_pair_ready": 4, "seg_ready": 8,
        "seg_exp": 8, "z_ready": 4, "y_gated": 4, "states_done": 1},
    "merge_b_act": {"acc0_ready": 1, "acc0_free": 1, "gate_bias_ready": 1, "gate_ready": 1},
    "heads_act": {"acc0_ready": 1, "acc0_free": 1, "k_ready": 1, "v_ready": 1, "kv_read": 2, "prob_turned": 4,
        "exp_ready": 4, "turned_out": 4, "max_ready": 4},
    "sample_a_act": {"act_step": 4, "prob_turned": 4, "exp_ready": 1, "turned_out": 4, "max_ready": 1,
        "lat_ready": 1, "lat_read": 1},
    "merge_a_act": {"acc0_ready": 1, "acc0_free": 1, "gate_bias_ready": 1, "gate_ready": 1},
    "mem_heads_act": {"acc0_ready": 1, "acc1_ready": 1, "acc0_free": 1, "acc1_free": 1, "prob_turned": 4,
        "exp_ready": 4, "turned_out": 4, "max_ready": 4},
    "merge_m_act": {"acc0_ready": 1, "acc0_free": 1, "gate_bias_ready": 1, "gate_ready": 1},
    "ssm_dve": {"dve_step": 131, "acc0_free": 5, "acc1_free": 5, "conv_done": 6, "conv_ready": 6, "silu_ready":
        6, "x_turned": 5, "turned_read": 5, "b_tm_read": 1, "b_tm_ready": 1, "cb_ready": 1, "cb_read": 1,
        "add_ready": 4, "add_read": 4, "cum_s_ready": 1, "states_stored": 32, "cum_spread": 4, "pair_read": 4,
        "decay_ready": 4, "y_ready": 4, "sq_summed": 4, "adds_ready": 8, "adds_read": 8, "var_ready": 1,
        "std_ready": 1, "e_pair_ready": 4, "seg_ready": 8, "seg_exp": 8, "z_ready": 4, "y_gated": 4,
        "states_done": 1},
    "merge_b_dve": {"acc1_ready": 1, "acc1_free": 1, "gate_bias_ready": 1, "gate_ready": 1},
    "heads_dve": {"dve_step": 14, "acc1_ready": 1, "acc1_free": 1, "head_read": 1, "q_lat_ready": 1,
        "q_lat_read": 1, "prob_ready": 4, "scores_ready": 4, "exp_ready": 4, "head_out": 1, "max_ready": 4},
    "sample_a_dve": {"dve_step": 17, "acc0_ready": 1, "acc1_ready": 1, "acc0_free": 1, "acc1_free": 1,
        "q_lat_read": 1, "prob_ready": 1, "exp_ready": 1, "max_ready": 1, "lat_turned": 1, "o_lat_ready": 1},
    "merge_a_dve": {"dve_step": 1, "acc1_ready": 1, "acc1_free": 1, "gate_bias_ready": 1, "gate_ready": 1},
    "mem_k_dve": {"acc0_ready": 1, "acc1_ready": 1, "acc0_free": 1, "acc1_free": 1},
    "mem_heads_dve": {"dve_step": 11, "acc0_free": 1, "acc1_free": 1, "head_read": 1, "prob_ready": 4,
        "scores_ready": 4, "exp_ready": 4, "head_out": 1, "max_ready": 4, "kv_head_ready": 1},
    "sample_m_dve": {"dve_step": 2, "scores_ready": 2, "q_b_ready": 2},
    "sample_mv_dve": {"head_read": 2, "head_out": 2},
    "merge_m_dve": {"dve_step": 1, "acc1_ready": 1, "acc1_free": 1, "gate_bias_ready": 1, "gate_ready": 1},
    "out_dve": {"acc0_ready": 2, "acc1_ready": 2, "acc0_free": 2, "acc1_free": 2},
    "up_dve": {"dve_step": 4, "acc0_ready": 2, "acc1_ready": 2, "acc0_free": 2, "acc1_free": 2},
    "down_dve": {"dve_step": 2, "acc0_ready": 1, "acc1_ready": 1, "acc0_free": 1, "acc1_free": 1},
    "ssm_pe": {"weights_in_slot0": 32, "weights_in_slot1": 48, "weights_in_slot2": 48, "weights_in_slot3": 32,
        "acc0_free": 5, "acc1_free": 5, "conv_ready": 6, "turned_read": 5, "b_tm_ready": 1, "cb_read": 1,
        "add_read": 4, "cum_s_ready": 1, "states_loaded": 16, "pair_read": 4, "decay_ready": 4, "sq_ready": 4,
        "adds_read": 8, "var_ready": 1},
    "merge_b_pe": {"weights_in_slot0": 16, "weights_in_slot1": 16, "weights_in_slot3": 16, "acc0_free": 1,
        "acc1_free": 1},
    "heads_pe": {"weights_in_slot0": 16, "weights_in_slot1": 16, "acc0_free": 1, "acc1_free": 1, "head_read": 1,
        "q_lat_read": 1, "kv_read": 2, "prob_ready": 4, "exp_ready": 4, "turned_out": 4},
    "sample_a_pe": {"acc0_free": 1, "acc1_free": 1, "q_lat_read": 1, "prob_ready": 1, "turned_out": 4,
        "lat_read": 1, "o_lat_ready": 1, "keys_in_slot0": 512, "keys_in_slot1": 512, "keys_in_slot2": 512,
        "keys_in_slot3": 512, "rows_in_slot0": 256, "rows_in_slot1": 256, "rows_in_slot2": 256, "rows_in_slot3":
        256},
    "merge_a_pe": {"weights_in_slot0": 16, "weights_in_slot1": 16, "acc0_free": 1, "acc1_free": 1},
    "mem_k_pe": {"weights_in_slot2": 16, "weights_in_slot3": 16, "acc0_free": 1, "acc1_free": 1},
    "mem_heads_pe": {"weights_in_slot0": 16, "weights_in_slot1": 16, "acc0_free": 1, "acc1_free": 1,
        "head_read": 1, "prob_ready": 4, "exp_ready": 4, "turned_out": 4, "kv_head_ready": 1},
    "sample_m_pe": {"mem_k0_loaded": 16, "mem_k1_loaded": 16, "q_b_ready": 2},
    "sample_mv_pe": {"head_read": 2, "mem_v0_loaded": 16, "mem_v1_loaded": 16},
    "merge_m_pe": {"weights_in_slot2": 16, "weights_in_slot3": 16, "acc0_free": 1, "acc1_free": 1},
    "out_pe": {"weights_in_slot0": 16, "weights_in_slot1": 16, "weights_in_slot2": 16, "weights_in_slot3": 16,
        "acc0_free": 2, "acc1_free": 2},
    "up_pe": {"weights_in_slot0": 16, "weights_in_slot1": 16, "weights_in_slot2": 16, "weights_in_slot3": 16,
        "acc0_free": 2, "acc1_free": 2},
    "down_pe": {"weights_in_slot0": 32, "weights_in_slot1": 32, "weights_in_slot2": 32, "weights_in_slot3": 32,
        "acc0_free": 1, "acc1_free": 1},
}


def program(nc, stream, x_t, mem_t, const, vec, conv_state, ssm_state, pages, ckv_rows, ckv_cols, krope_cols,
            memk_cols, memv_rows, o):
    from concourse import mybir
    import concourse.bass as bass
    F, I32 = mybir.dt.float32, mybir.dt.int32
    ACT, ALU, AX = mybir.ActivationFunctionType, mybir.AluOpType, mybir.AxisListType
    MUL, ADD, SUB, MAX, MIN = ALU.mult, ALU.add, ALU.subtract, ALU.max, ALU.min

    with ExitStack() as ctx:
        def sb(name, cols, dt=F, rows=P):
            return ctx.enter_context(nc.sbuf_tensor(name, [rows, cols], dt))

        ring = sb("ring", RING * BLOCK)
        cst = sb("cst", CW)
        vecs = sb("vecs", VW)
        xt = sb("xt", KC * T)
        branch = sb("branch", D_INNER // P * T)
        merged = sb("merged", KC * T)
        work = sb("work", WORK)
        mark = sb("mark", 2, F, 1)
        act_mark = sb("act_mark", 2, F, 1)
        grant = sb("grant", 4, F, 1)
        page_ids = sb("page_ids", DEC_BATCH * N_PAGES, I32, 1)

        acc = [ctx.enter_context(nc.psum_tensor(f"acc{a}", [P, 2, 512], F)) for a in range(2)]
        bank = [ctx.enter_context(nc.psum_tensor(f"bank{a}", [P, 512], F)) for a in range(4)]

        def C(name):
            at, n = _C[name]
            return cst[:, at:at + n]

        def V(name, j=0):
            at, n = _V[name]
            return vecs[:, at + j:at + j + 1]

        def chunks(tensor, n):
            return tensor[:, 0:n * T].rearrange("p (c t) -> p c t", t=T)

        X, BR, MG = chunks(xt, KC), chunks(branch, D_INNER // P), chunks(merged, KC)

        class Carver:
            def __init__(self, tensor=work, cols=WORK):
                self.tensor, self.at, self.cols = tensor, 0, cols

            def __call__(self, cols, rows=P):
                a = self.tensor[0:rows, self.at:self.at + cols]
                self.at += cols
                assert self.at <= self.cols, self.at
                return a

        sem = {name: ctx.enter_context(nc.semaphore(name)) for name in SEMAPHORES}

        class Counts:
            def __init__(self, engine, given):
                self.engine = engine
                self.of = {n: Count(sem[n], given.get(n, 0)) for n in SEMAPHORES}

            def next(self, name, n=1):
                return self.of[name].next(n)

            def value(self, name):
                return self.of[name].value()

            def skip(self, name, n=1):
                self.of[name].next(n)

            def loop(self, name, trips):
                return turns(self.engine, trips, list(self.of.values()), PER.get(name, {}), name)

        def accv(p, rows=P):
            return acc[p][0:rows, :, 0:HT]

        k = Carver()
        dt_tm, cum_tm, wb_tm = (k((NB + 1) * SSM_HEADS).rearrange("p (c h) -> p c h", h=SSM_HEADS) for _ in range(3))
        dec_p = k(NB * SSM_HEADS).rearrange("p (c h) -> p c h", h=SSM_HEADS)
        dec_s = k(DEC_BATCH * SSM_HEADS).rearrange("p (b h) -> p b h", h=SSM_HEADS)
        cum_g = k(GROUPS * T, HG).rearrange("p (g t) -> p g t", t=T)
        st_conv = k(NC * DEC_BATCH * 3).rearrange("p (c b t) -> p c b t", b=DEC_BATCH, t=3)
        conv_out = k(NC * 27).rearrange("p (c n) -> p c n", n=27)
        after_dt = k.at
        dtw = {n: k(T, SSM_HEADS) for n in ("v", "abs", "u", "w", "d", "e", "ln", "dt", "dta", "cum", "r")}
        na = k(2, SSM_HEADS)
        cum_last = k(DEC_BATCH * SSM_HEADS, NS).rearrange("p (b h) -> p b h", h=SSM_HEADS)
        ident32 = cst[0:SSM_HEADS, _C["ident"][0]:_C["ident"][0] + SSM_HEADS]

        def blocks_of(row):
            return [row[:, c * P:(c + 1) * P] if c < NB else row[:, SEQ:T] for c in range(NB + 1)]

        k = Carver()
        k.at = after_dt
        fm = k(QC * T).rearrange("p (q t) -> p q t", t=T)
        ext = [k(EXT) for _ in range(2)]
        cacc = [k(CL) for _ in range(2)]
        sq = [a[:, 0:T] for a in cacc] + [a[:, 3:3 + T] for a in ext]
        th = [k(CL) for _ in range(2)]
        cum_s = k(T, HG)
        xdt = k((NB + 1) * GW).rearrange("p (c n) -> p c n", n=GW)
        xw = k((NB + 1) * GW).rearrange("p (c n) -> p c n", n=GW)
        b_tm = k(NB * P).rearrange("p (c n) -> p c n", n=P)
        b_s = k(P, NS)
        b_mask = k(DEC_BATCH * P, NS).rearrange("p (b n) -> p b n", n=P)
        cb_p = k(NB * P).rearrange("p (c n) -> p c n", n=P)
        cb_s = k(NS, NS)
        st_p = k(NB * GW).rearrange("p (c n) -> p c n", n=GW)
        st_s = merged[:, 0:DEC_BATCH * GW].rearrange("p (b n) -> p b n", n=GW)
        dec = [k(T) for _ in range(2)]
        e_pair = k(T)
        t1 = k(T)
        rstd = k(T)
        zc = [k(T) for _ in range(2)]
        zth = [a[:, 0:T] for a in th]

        def ext_s(j):
            return ext[j][:, EXT_P:EXT].rearrange("p (b t) -> p b t", t=EXT_S)

        def conv_p(a):
            return a[:, 0:SEQ]

        def heads(a, c, g, rows):
            s = a[0:rows, c, bass.ds(g * HG, HG)]
            return s.rearrange("p (h o) -> p h o", o=1).broadcast_to([rows, HG, HEAD_DIM])

        def by_head(ap):
            return ap.rearrange("p (h d) -> p h d", d=HEAD_DIM)

        def rows_of(c):
            return P if c < NB else NS

        def toks(row, c):
            return row[:, c * P:(c + 1) * P] if c < NB else row[:, SEQ:T]

        k = Carver()
        k.at = WORK - 2 * T - 1
        gate, product, gate_bias = k(T), k(T), k(1)

        k = Carver()
        ckv = k(2 * T).rearrange("p (c t) -> p c t", t=T)
        krope = k(T)
        q_lat = k(2 * DEC_BATCH * NS).rearrange("p (c b h t) -> p c b h t", b=DEC_BATCH, h=MLA_HEADS, t=DEC_SEQ)
        q_rot = k(DEC_BATCH * NS, ROPE).rearrange("p (b h t) -> p b h t", h=MLA_HEADS, t=DEC_SEQ)
        ckv_new = k(KV_LORA, NS)
        o_lat_t = k(2 * MLA_HEADS * NS).rearrange("p (c h t) -> p c h t", h=MLA_HEADS, t=NS)
        keys = [k(4 * KV_LORA) for _ in range(4)]
        key_rope = [k(4 * PAGE, ROPE) for _ in range(4)]
        rows = [k(4 * KV_LORA) for _ in range(4)]
        for_heads = k.at
        cq = k(3 * T).rearrange("p (c t) -> p c t", t=T)
        a_rstd = k(T)
        a_sq = [k(T) for _ in range(5)]
        q_n, q_r = k(T), k(T)
        k_n = k(SEQ)
        v_tm = k(SEQ).rearrange("p (b v) -> p b v", v=P)
        prob = [k(SEQ) for _ in range(2)]
        prob_t = k(NB * SEQ).rearrange("p (b q) -> p b q", q=SEQ)
        stats = [k(4) for _ in range(2)]
        k.at = for_heads
        s_prob = k(N_PAGES * PAGE + NS)
        s_prob_t = k(N_PAGES * P).rearrange("p (g n) -> p g n", n=P)
        s_prob_n = k(P, NS)
        o_lat = k(KV_LORA)
        s_new = k(NS)
        s_stat = k(16)
        q_lat_g = k(2 * 4 * NS).rearrange("p (c b n) -> p c b n", c=2, b=4)
        q_rot_g = k(4 * NS, ROPE).rearrange("p (b n) -> p b n", n=NS)
        A_SCALE = (NOPE + ROPE) ** -0.5

        k = Carver()
        mem = k(KC * N_MEM).rearrange("p (c m) -> p c m", m=N_MEM)
        mk = k(8 * N_MEM).rearrange("p (c m) -> p c m", m=N_MEM)
        mv = k(2 * 1024).rearrange("p (b e) -> p b e", b=2)
        q_h = k(2 * T).rearrange("p (c t) -> p c t", t=T)
        k_h = k(2 * N_MEM).rearrange("p (c m) -> p c m", m=N_MEM)
        v_h = k(2 * MEM_DIM).rearrange("p (b e) -> p b e", b=2)
        m_prob = [k(N_MEM) for _ in range(2)]
        m_prob_t = k(2 * SEQ).rearrange("p (b q) -> p b q", q=SEQ)
        m_stats = [k(4) for _ in range(2)]
        mq_s = k(8 * NS).rearrange("p (c t) -> p c t", t=NS)
        q_b = [k(8 * NS).rearrange("p (c t) -> p c t", t=NS) for _ in range(2)]
        m_scores = k(N_MEM)
        ms_prob_t = k(2 * P).rearrange("p (b n) -> p b n", b=2)
        mem_k = [k(8 * N_MEM).rearrange("p (c m) -> p c m", m=N_MEM) for _ in range(2)]
        mem_v = [k(2 * 1024).rearrange("p (b e) -> p b e", b=2) for _ in range(2)]
        M_SCALE = MEM_DIM ** -0.5

        k = Carver()
        hid = k(FC * T).rearrange("p (c t) -> p c t", t=T)
        mean, inv = k(T), k(T)
        relu = [k(T) for _ in range(2)]
        n_sq = hid[:, 0:KC, :]

        block = ctx.enter_context(nc.Block())

        @block.gpsimd
        def _(pool):
            pool.memset(mark[0:1, 0:1], 0.0).then_inc(sem["acc0_free"], CREDIT["acc0_free"])
            pool.memset(act_mark[0:1, 0:1], 0.0).then_inc(sem["acc1_free"], CREDIT["acc1_free"])
            for i, name in enumerate(("blocks_begun", "states_stored", "keys_used", "rows_used")):
                pool.memset(grant[0:1, i:i + 1], 0.0).then_inc(sem[name], CREDIT[name])

        @block.sync
        def _(sp):
            sp.dma_start(cst[:, :], const).then_inc(sem["const_loaded"], 16)
            n, last = 0, {}
            for name, trips, per in PHASES:
                slots = [(START[name] + b) % RING for b in range(per)]

                def load(i, b):
                    s = slots[b]
                    before = [x for x in range(b) if slots[x] == s]
                    again = [x for x in range(per) if slots[x] == s][-1]
                    gaps = [b - before[-1]] if before else []
                    if not before and trips > 1:
                        gaps.append(per - again + b)
                    if not before and s in last:
                        gaps.append(n + b - last[s])
                    assert all(x >= 2 for x in gaps)
                    at = n + b if trips == 1 else i * per + (n + b)
                    if gaps:
                        sp.wait_ge(sem["blocks_begun"], at + (CREDIT["blocks_begun"] + 2 - min(gaps)))
                    sp.dma_start(ring[:, s * BLOCK:(s + 1) * BLOCK],
                            stream[at]).then_inc(sem[f"weights_in_slot{s}"], 16)

                if trips > 1:
                    with sp.Fori(0, trips) as i:
                        for b in range(per):
                            load(i, b)
                else:
                    for b in range(per):
                        load(0, b)
                for b in range(per):
                    last[slots[b]] = n + (trips - 1) * per + b
                n += trips * per
                if name == "heads":
                    sp.wait_ge(sem["page_ids_loaded"], 16)
                    sp.wait_ge(sem["stage_over"], STAGES.index("merge_b") + 1)
                    with sp.Fori(0, 2) as g:
                        for kind in ("keys", "rows"):
                            with sp.Fori(0, 4) as b:
                                for kq in range(4):
                                    sp.wait_ge(sem[f"{kind}_used"], g * 16 + b * 4 + (kq + 1))
                                    for i in range(4):
                                        p = sp.value_load(page_ids[0:1, bass.ds(g * 64 + b * 16 + (kq * 4 + i), 1)],
                                                          min_val=0, max_val=N_POOL - 1)
                                        if kind == "keys":
                                            sp.dma_start(keys[kq][:, i * KV_LORA:(i + 1) * KV_LORA],
                                                         ckv_cols[p]).then_inc(sem[f"keys_in_slot{kq}"], 16)
                                            sp.dma_start(key_rope[kq][:, i * PAGE:(i + 1) * PAGE],
                                                         krope_cols[p]).then_inc(sem[f"keys_in_slot{kq}"], 16)
                                        else:
                                            sp.dma_start(rows[kq][:, i * KV_LORA:(i + 1) * KV_LORA],
                                                         ckv_rows[p]).then_inc(sem[f"rows_in_slot{kq}"], 16)
                if name == "mq":
                    sp.wait_ge(sem["stage_over"], STAGES.index("merge_a") + 1)
                    for j in range(2):
                        sp.dma_start(mem_k[j], memk_cols[j]).then_inc(sem[f"mem_k{j}_loaded"], 16)
                        sp.dma_start(mem_v[j], memv_rows[j]).then_inc(sem[f"mem_v{j}_loaded"], 16)
                    first = MLA_HEADS * NB + MEM_HEADS * NB
                    with sp.Fori(0, DEC_BATCH // 2 - 1) as i:
                        for j in range(2):
                            sp.wait_ge(sem["scores_ready"], 2 * i + (first + j + 1))
                            sp.dma_start(mem_k[j], memk_cols[2 * i + (2 + j)]).then_inc(sem[f"mem_k{j}_loaded"], 16)
                    first = MLA_HEADS + MEM_HEADS
                    with sp.Fori(0, DEC_BATCH // 2 - 1) as i:
                        for j in range(2):
                            sp.wait_ge(sem["head_out"], 2 * i + (first + j + 1))
                            sp.dma_start(mem_v[j], memv_rows[2 * i + (2 + j)]).then_inc(sem[f"mem_v{j}_loaded"], 16)

        @block.scalar
        def _(act):
            t = Counts(act, {"acc0_free": 1, "acc1_free": 1})
            act.dma_start(X, x_t).then_inc(sem["x_loaded"], 16)
            act.dma_start(vecs[:, :], vec).then_inc(sem["vec_loaded"], 16)
            act.dma_start(st_conv, conv_state).then_inc(sem["conv_state_loaded"], 16)
            act.dma_start(page_ids[:, :], pages).then_inc(sem["page_ids_loaded"], 16)
            act.wait_ge(sem["acc1_free"], 1)
            act.wait_ge(sem["vec_loaded"], 16)
            act.wait_ge(sem["const_loaded"], 16)

            def root(a):
                act.wait_ge(sem["var_ready"], t.next("var_ready"))
                act.activation(a, a, ACT.Sqrt).then_inc(sem["std_ready"], 1)
                act.wait_ge(sem["std_ready"], t.next("std_ready"))

            def norm():
                act.wait_ge(sem["centred"], t.next("centred"))
                act.activation(n_sq, X, ACT.Square).then_inc(sem["norm_in"], 1)
                act.wait_ge(sem["norm_in"], t.next("norm_in"))
                root(inv)

            def merge(name):
                act.wait_ge(sem["stage_over"], t.next("stage_over"))
                with t.loop(f"{name}_act", KC):
                    act.wait_ge(sem["gate_bias_ready"], t.next("gate_bias_ready"))
                    act.wait_ge(sem["acc0_ready"], t.next("acc0_ready"))
                    act.activation(v2(gate), accv(0), ACT.Tanh, scale=0.5, bias=gate_bias).then_inc(sem["acc0_free"], 1)
                    act.wait_ge(sem["acc0_free"], t.next("acc0_free"))
                    act.activation(gate, gate, ACT.Identity, scale=0.5, bias=C("half")).then_inc(sem["gate_ready"], 1)
                    act.wait_ge(sem["gate_ready"], t.next("gate_ready"))
                t.skip("acc1_ready", KC), t.skip("acc1_free", KC)

            t.skip("acc0_ready"), t.skip("acc0_free")
            act.wait_ge(sem["dt_v"], t.next("dt_v"))
            act.activation(dtw["u"], dtw["abs"], ACT.Exp, scale=-1.0).then_inc(sem["dt_u"], 1)
            act.wait_ge(sem["dt_u"], t.next("dt_u"))
            act.activation(na[:, 0:1], V("alog")[0:SSM_HEADS], ACT.Exp).then_inc(sem["dt_u"], 1)
            act.wait_ge(sem["dt_u"], t.next("dt_u"))
            act.wait_ge(sem["dt_w"], t.next("dt_w"))
            act.activation(dtw["ln"], dtw["w"], ACT.Ln).then_inc(sem["dt_ln"], 1)
            act.wait_ge(sem["dt_ln"], t.next("dt_ln"))
            for g in range(GROUPS):
                if g == 0:
                    act.wait_ge(sem["cum_rows_ready"], t.next("cum_rows_ready"))
                act.dma_start(cum_g[:, g, :], dtw["cum"][g * HG:(g + 1) * HG, :]).then_inc(sem["cum_g_loaded"], 16)
            act.wait_ge(sem["wb_ready"], t.next("wb_ready"))
            act.activation(wb_tm[:, 0:NB, :], wb_tm[:, 0:NB, :], ACT.Exp).then_inc(sem["act_step"], 1)
            act.wait_ge(sem["act_step"], t.next("act_step"))
            act.activation(wb_tm[0:NS, NB, :], wb_tm[0:NS, NB, :], ACT.Exp).then_inc(sem["act_step"], 1)
            act.wait_ge(sem["act_step"], t.next("act_step"))
            act.activation(dec_p, bank[2][:, 0:NB * SSM_HEADS].rearrange("p (c h) -> p c h", h=SSM_HEADS),
                    ACT.Exp).then_inc(sem["act_step"], 1)
            act.wait_ge(sem["act_step"], t.next("act_step"))
            act.activation(dec_s, bank[1][:, 0:DEC_BATCH * SSM_HEADS].rearrange("p (b h) -> p b h", h=SSM_HEADS),
                    ACT.Exp).then_inc(sem["dec_ready"], 1)
            act.wait_ge(sem["dec_ready"], t.next("dec_ready"))

            act.wait_ge(sem["stage_over"], t.next("stage_over"))
            with t.loop("ssm_act", GROUPS) as g:
                def evac(q):
                    j = q % 2
                    act.wait_ge(sem[f"acc{j}_ready"], t.next(f"acc{j}_ready"))
                    act.activation(ext[j][:, 3:3 + HT], acc[j][:, 0, 0:HT], ACT.Copy).then_inc(sem["act_step"], 1)
                    act.wait_ge(sem["act_step"], t.next("act_step"))
                    act.activation(ext[j][:, 3 + HT:EXT_P], acc[j][:, 1, 0:SEQ - HT],
                            ACT.Copy).then_inc(sem["act_step"], 1)
                    act.wait_ge(sem["act_step"], t.next("act_step"))
                    act.activation(ext_s(j)[:, :, 3:EXT_S], acc[j][:, 1, SEQ - HT:HT].rearrange("p (b t) -> p b t",
                            t=DEC_SEQ), ACT.Copy).then_inc(sem[f"acc{j}_free"], 1)
                    act.wait_ge(sem[f"acc{j}_free"], t.next(f"acc{j}_free"))

                def silu(q):
                    j = q % 2
                    act.wait_ge(sem["conv_done"], t.next("conv_done"))
                    act.activation(th[j], cacc[j], ACT.Tanh, scale=0.5).then_inc(sem["act_step"], 1)
                    act.wait_ge(sem["act_step"], t.next("act_step"))
                    act.activation(th[j], th[j], ACT.Identity, scale=0.5,
                            bias=C("half")).then_inc(sem["silu_ready"], 1)
                    act.wait_ge(sem["silu_ready"], t.next("silu_ready"))

                for q in range(QC):
                    evac(q)
                    if q == 1:
                        act.wait_ge(sem["states_stored"], t.next("states_stored", 32))
                        act.dma_start(st_s, ssm_state[g]).then_inc(sem["states_loaded"], 16)
                    if q >= 1:
                        silu(q - 1)
                silu(QC - 1)

                def z_read(hp):
                    j = hp % 2
                    if hp == 0:
                        act.wait_ge(sem["conv_ready"], t.next("conv_ready", QC))
                    act.wait_ge(sem[f"acc{j}_ready"], t.next(f"acc{j}_ready"))
                    act.activation(v2(zth[j]), accv(j), ACT.Tanh, scale=0.5).then_inc(sem["act_step"], 1)
                    act.wait_ge(sem["act_step"], t.next("act_step"))
                    act.activation(v2(zc[j]), accv(j), ACT.Copy).then_inc(sem[f"acc{j}_free"], 1)
                    act.wait_ge(sem[f"acc{j}_free"], t.next(f"acc{j}_free"))
                    act.activation(zth[j], zth[j], ACT.Identity, scale=0.5,
                            bias=C("half")).then_inc(sem["z_ready"], 1)
                    act.wait_ge(sem["z_ready"], t.next("z_ready"))

                z_read(0)
                z_read(1)
                act.wait_ge(sem["b_turned"], t.next("b_turned"))
                act.activation(b_tm, bank[2][:, :].rearrange("p (c n) -> p c n", n=P),
                        ACT.Copy).then_inc(sem["act_step"], 1)
                act.wait_ge(sem["act_step"], t.next("act_step"))
                act.activation(b_s, bank[3][0:NS, 0:P], ACT.Copy).then_inc(sem["b_tm_read"], 1)
                act.wait_ge(sem["b_tm_read"], t.next("b_tm_read"))
                for hp in range(GC):
                    act.wait_ge(sem["cum_spread"], t.next("cum_spread"))
                    act.activation(e_pair[:, 0:SEQ], bank[2][:, 0:SEQ], ACT.Exp).then_inc(sem["act_step"], 1)
                    act.wait_ge(sem["act_step"], t.next("act_step"))
                    act.activation(e_pair[:, SEQ:T], bank[3][:, 2 * NS:3 * NS],
                            ACT.Exp).then_inc(sem["e_pair_ready"], 1)
                    act.wait_ge(sem["e_pair_ready"], t.next("e_pair_ready"))
                    for j in range(2):
                        act.wait_ge(sem["seg_ready"], t.next("seg_ready"))
                        act.activation(conv_p(dec[j]), conv_p(dec[j]), ACT.Exp).then_inc(sem["act_step"], 1)
                        act.wait_ge(sem["act_step"], t.next("act_step"))
                        act.activation(dec[j][0:NS, SEQ:T], dec[j][0:NS, SEQ:T], ACT.Exp).then_inc(sem["seg_exp"], 1)
                        act.wait_ge(sem["seg_exp"], t.next("seg_exp"))
                    if hp in (1, 2):
                        z_read(hp + 1)
                    act.wait_ge(sem["y_gated"], t.next("y_gated"))
                    act.activation(sq[hp], fm[:, hp, :], ACT.Square).then_inc(sem["sq_ready"], 1)
                    act.wait_ge(sem["sq_ready"], t.next("sq_ready"))
                act.wait_ge(sem["var_ready"], t.next("var_ready"))
                act.activation(rstd, rstd, ACT.Sqrt).then_inc(sem["std_ready"], 1)
                act.wait_ge(sem["std_ready"], t.next("std_ready"))
                act.wait_ge(sem["states_done"], t.next("states_done"))
                act.dma_start(o["ssm_p"][g], st_p[:, NB - 1, :]).then_inc(sem["states_stored"], 16)
                act.dma_start(o["ssm_s"][g], st_s).then_inc(sem["states_stored"], 16)
                act.wait_ge(sem["sq_summed"], t.next("sq_summed", GC))
            act.wait_ge(sem["states_stored"], t.next("states_stored", 32))
            act.dma_start(o["conv"], conv_out).then_inc(sem["stored"], 16)
            act.wait_ge(sem["stored"], t.next("stored", 16))
            act.activation(act_mark[0:1, 1:2], act_mark[0:1, 0:1], ACT.Copy).then_inc(sem["act_over"], 1)
            act.wait_ge(sem["act_over"], t.next("act_over"))

            merge("merge_b")

            act.wait_ge(sem["stage_over"], t.next("stage_over"))
            for i in range(5):
                p = i % 2
                dst = cq[:, i, :] if i < 3 else ckv[:, i - 3, :]
                act.wait_ge(sem[f"acc{p}_ready"], t.next(f"acc{p}_ready"))
                act.activation(v2(dst), accv(p), ACT.Copy).then_inc(sem[f"acc{p}_free"], 1)
                act.wait_ge(sem[f"acc{p}_free"], t.next(f"acc{p}_free"))
                act.activation(a_sq[i], dst, ACT.Square).then_inc(sem["squares_ready"], 1)
                act.wait_ge(sem["squares_ready"], t.next("squares_ready"))
            t.skip("acc1_ready"), t.skip("acc1_free")
            root(a_rstd)
            act.wait_ge(sem["kr_folded"], t.next("kr_folded"))
            act.activation(krope[:, 0:HT], bank[0][:, 0:HT], ACT.Copy).then_inc(sem["act_step"], 1)
            act.wait_ge(sem["act_step"], t.next("act_step"))
            act.activation(krope[:, HT:T], bank[1][:, 0:HT], ACT.Copy).then_inc(sem["krope_ready"], 1)
            act.wait_ge(sem["krope_ready"], t.next("krope_ready"))
            root(a_rstd)
            act.wait_ge(sem["latents_ready"], t.next("latents_ready"))
            act.dma_start(o["ckv"], ckv).then_inc(sem["stored"], 16)
            act.dma_start(o["krope"], krope[0:ROPE, :]).then_inc(sem["stored"], 16)
            act.wait_ge(sem["new_turned"], t.next("new_turned"))
            act.activation(ckv_new, bank[0][0:NS, 0:KV_LORA], ACT.Copy).then_inc(sem["new_read"], 1)
            act.wait_ge(sem["new_read"], t.next("new_read"))
            with t.loop("heads_act", MLA_HEADS):
                act.wait_ge(sem["acc0_ready"], t.next("acc0_ready"))
                act.activation(v2(q_n), accv(0), ACT.Copy).then_inc(sem["acc0_free"], 1)
                act.wait_ge(sem["acc0_free"], t.next("acc0_free"))
                act.wait_ge(sem["k_ready"], t.next("k_ready"))
                act.activation(k_n, bank[1][:, :], ACT.Copy).then_inc(sem["kv_read"], 1)
                act.wait_ge(sem["kv_read"], t.next("kv_read"))
                act.wait_ge(sem["v_ready"], t.next("v_ready"))
                act.activation(v_tm, bank[2][:, :].rearrange("p (b v) -> p b v", v=P),
                        ACT.Copy).then_inc(sem["kv_read"], 1)
                act.wait_ge(sem["kv_read"], t.next("kv_read"))

                def turned(qb):
                    act.wait_ge(sem["prob_turned"], t.next("prob_turned"))
                    n = (qb + 1) * P
                    act.activation(prob_t[:, 0:qb + 1, qb * P:n], bank[1 + qb % 2][:,
                            0:n].rearrange("p (b q) -> p b q", q=P), ACT.Copy).then_inc(sem["turned_out"], 1)
                    act.wait_ge(sem["turned_out"], t.next("turned_out"))

                for qb in range(NB):
                    n = (qb + 1) * P
                    act.wait_ge(sem["max_ready"], t.next("max_ready"))
                    act.activation(prob[qb % 2][:, 0:n], bank[3 * (qb % 2)][:, 0:n], ACT.Exp, scale=A_SCALE,
                            bias=stats[qb % 2][:, 1:2], accum_out=stats[qb % 2][:, 2:3]).then_inc(sem["exp_ready"], 1)
                    act.wait_ge(sem["exp_ready"], t.next("exp_ready"))
                    if qb >= 1:
                        turned(qb - 1)
                turned(NB - 1)
            t.skip("acc1_ready", MLA_HEADS), t.skip("acc1_free", MLA_HEADS)
            with t.loop("sample_a_act", 2):
                for kq in range(4):
                    if kq == 0:
                        act.wait_ge(sem["max_ready"], t.next("max_ready"))
                    act.activation(s_prob[:, kq * 512:(kq + 1) * 512], bank[kq][:, :], ACT.Exp, scale=A_SCALE,
                            bias=s_stat[:, 1:2], accum_out=s_stat[:, 8 + kq:9 + kq]).then_inc(sem["act_step"], 1)
                    act.wait_ge(sem["act_step"], t.next("act_step"))
                act.activation(s_prob[:, N_PAGES * PAGE:], s_new, ACT.Exp, scale=A_SCALE, bias=s_stat[:, 1:2],
                        accum_out=s_stat[:, 12:13]).then_inc(sem["exp_ready"], 1)
                act.wait_ge(sem["exp_ready"], t.next("exp_ready"))
                for kq in range(4):
                    act.wait_ge(sem["prob_turned"], t.next("prob_turned"))
                    act.activation(s_prob_t[:, kq * 4:(kq + 1) * 4, :], bank[kq][:,
                            :].rearrange("p (g n) -> p g n", n=P), ACT.Copy).then_inc(sem["turned_out"], 1)
                    act.wait_ge(sem["turned_out"], t.next("turned_out"))
                act.wait_ge(sem["lat_ready"], t.next("lat_ready"))
                act.activation(o_lat, bank[0][:, 0:KV_LORA], ACT.Copy).then_inc(sem["lat_read"], 1)
                act.wait_ge(sem["lat_read"], t.next("lat_read"))
            t.skip("acc0_ready", 2), t.skip("acc0_free", 2), t.skip("acc1_ready", 2), t.skip("acc1_free", 2)
            act.wait_ge(sem["stored"], t.next("stored", 32))
            act.activation(act_mark[0:1, 1:2], act_mark[0:1, 0:1], ACT.Copy).then_inc(sem["act_over"], 1)
            act.wait_ge(sem["act_over"], t.next("act_over"))

            merge("merge_a")

            act.wait_ge(sem["stage_over"], t.next("stage_over"))
            act.dma_start(mem, mem_t).then_inc(sem["mem_loaded"], 16)
            for j in range(2):
                t.skip(f"acc{j}_ready", 5), t.skip(f"acc{j}_free", 5)
            act.wait_ge(sem["mem_kv_ready"], t.next("mem_kv_ready"))
            act.dma_start(o["mem_k"], mk).then_inc(sem["stored"], 16)
            act.dma_start(o["mem_v"], mv).then_inc(sem["stored"], 16)
            with t.loop("mem_heads_act", MEM_HEADS):
                for p in range(2):
                    act.wait_ge(sem[f"acc{p}_ready"], t.next(f"acc{p}_ready"))
                    act.activation(v2(q_h[:, p, :]), accv(p), ACT.Copy).then_inc(sem[f"acc{p}_free"], 1)
                    act.wait_ge(sem[f"acc{p}_free"], t.next(f"acc{p}_free"))

                def turned(qb):
                    act.wait_ge(sem["prob_turned"], t.next("prob_turned"))
                    act.activation(m_prob_t[:, :, qb * P:(qb + 1) * P], bank[2 + qb % 2][:,
                            0:2 * P].rearrange("p (b q) -> p b q", q=P), ACT.Copy).then_inc(sem["turned_out"], 1)
                    act.wait_ge(sem["turned_out"], t.next("turned_out"))

                for qb in range(NB):
                    act.wait_ge(sem["max_ready"], t.next("max_ready"))
                    act.activation(m_prob[qb % 2], bank[qb % 2][:, 0:N_MEM], ACT.Exp, scale=M_SCALE,
                            bias=m_stats[qb % 2][:, 1:2], accum_out=m_stats[qb % 2][:,
                                    2:3]).then_inc(sem["exp_ready"], 1)
                    act.wait_ge(sem["exp_ready"], t.next("exp_ready"))
                    if qb >= 1:
                        turned(qb - 1)
                turned(NB - 1)
            act.wait_ge(sem["max_ready"], t.next("max_ready"))
            act.activation(m_scores, m_scores, ACT.Exp, scale=M_SCALE, bias=m_stats[0][:, 1:2],
                    accum_out=m_stats[0][:, 2:3]).then_inc(sem["exp_ready"], 1)
            act.wait_ge(sem["exp_ready"], t.next("exp_ready"))
            act.wait_ge(sem["prob_turned"], t.next("prob_turned"))
            act.activation(ms_prob_t, bank[2][:, 0:2 * P].rearrange("p (b n) -> p b n", b=2),
                    ACT.Copy).then_inc(sem["turned_out"], 1)
            act.wait_ge(sem["turned_out"], t.next("turned_out"))
            act.wait_ge(sem["stored"], t.next("stored", 32))
            act.activation(act_mark[0:1, 1:2], act_mark[0:1, 0:1], ACT.Copy).then_inc(sem["act_over"], 1)
            act.wait_ge(sem["act_over"], t.next("act_over"))

            merge("merge_m")

            act.wait_ge(sem["stage_over"], t.next("stage_over"))
            norm()
            norm()
            act.wait_ge(sem["normed"], t.next("normed", 2))
            act.dma_start(o["y"], X).then_inc(sem["stored"], 16)
            act.wait_ge(sem["stored"], t.next("stored", 16))

        @block.vector
        def _(dve):
            t = Counts(dve, {"acc0_free": 1, "acc1_free": 1})
            dve.wait_ge(sem["vec_loaded"], 16)
            dve.wait_ge(sem["conv_state_loaded"], 16)
            dve.wait_ge(sem["acc0_free"], 1)

            def inv_std(out, summed, n, eps):
                dve.wait_ge(sem[summed], t.next(summed))
                for half in range(2):
                    signal = "var_ready" if half else "dve_step"
                    dve.tensor_scalar(out[:, half * HT:(half + 1) * HT], bank[2 + half][:, 0:HT], 1.0 / n, eps, MUL,
                            ADD).then_inc(sem[signal], 1)
                    dve.wait_ge(sem[signal], t.next(signal))
                dve.wait_ge(sem["std_ready"], t.next("std_ready"))
                dve.reciprocal(out, out).then_inc(sem["dve_step"], 1)
                dve.wait_ge(sem["dve_step"], t.next("dve_step"))

            def softmax(scores, stats, p, scale, scaled):
                dve.reduce_max(stats[:, 0:1], scores, AX.X).then_inc(sem["dve_step"], 1)
                dve.wait_ge(sem["dve_step"], t.next("dve_step"))
                dve.tensor_scalar(stats[:, 1:2], stats[:, 0:1], -scale, None, MUL).then_inc(sem["max_ready"], 1)
                dve.wait_ge(sem["max_ready"], t.next("max_ready"))
                dve.wait_ge(sem["exp_ready"], t.next("exp_ready"))
                dve.reciprocal(stats[:, 3:4], stats[:, 2:3]).then_inc(sem["dve_step"], 1)
                dve.wait_ge(sem["dve_step"], t.next("dve_step"))
                dve.tensor_scalar(p, p, stats[:, 3:4], None, MUL).then_inc(sem[scaled], 1)
                dve.wait_ge(sem[scaled], t.next(scaled))

            def norm(gain, bias):
                dve.tensor_copy(mark[0:1, 1:2], mark[0:1, 0:1]).then_inc(sem["norm_in"], 1)
                dve.wait_ge(sem["norm_in"], t.next("norm_in"))
                dve.wait_ge(sem["sums_ready"], t.next("sums_ready"))
                for half in range(2):
                    dve.tensor_scalar(mean[:, half * HT:(half + 1) * HT], bank[half][:, 0:HT], 1.0 / D_MODEL, None,
                            MUL).then_inc(sem["dve_step"], 1)
                    dve.wait_ge(sem["dve_step"], t.next("dve_step"))
                dve.tensor_tensor(X, X, mean.rearrange("p (o t) -> p o t", o=1).broadcast_to([P, KC, T]),
                        SUB).then_inc(sem["centred"], 1)
                dve.wait_ge(sem["centred"], t.next("centred"))
                t.skip("norm_in")
                inv_std(inv, "norm_summed", D_MODEL, LN_EPS)
                for c in range(KC):
                    dve.scalar_tensor_tensor(out=X[:, c, :], in0=X[:, c, :], scalar=V(gain, c), in1=inv, op0=MUL,
                            op1=MUL).then_inc(sem["dve_step"], 1)
                    dve.wait_ge(sem["dve_step"], t.next("dve_step"))
                    dve.tensor_scalar(X[:, c, :], X[:, c, :], V(bias, c), None, ADD).then_inc(sem["dve_step"], 1)
                    dve.wait_ge(sem["dve_step"], t.next("dve_step"))

            def merge(name, branch_i):
                with t.loop(f"{name}_dve", KC) as j:
                    dve.tensor_scalar(gate_bias, vecs[:, bass.ds(_V["bgate"][0] + branch_i * KC + j, 1)], 0.5, None,
                            MUL).then_inc(sem["gate_bias_ready"], 1)
                    dve.wait_ge(sem["gate_bias_ready"], t.next("gate_bias_ready"))
                    dve.wait_ge(sem["gate_ready"], t.next("gate_ready"))
                    dve.wait_ge(sem["acc1_ready"], t.next("acc1_ready"))
                    m = MG[:, bass.ds(j, 1), :].rearrange("p o t -> p (o t)")
                    if name == "merge_b":
                        dve.tensor_tensor(v2(m), v2(gate), accv(1), MUL).then_inc(sem["acc1_free"], 1)
                        dve.wait_ge(sem["acc1_free"], t.next("acc1_free"))
                    else:
                        dve.tensor_tensor(v2(product), v2(gate), accv(1), MUL).then_inc(sem["acc1_free"], 1)
                        dve.wait_ge(sem["acc1_free"], t.next("acc1_free"))
                        dve.tensor_tensor(m, m, product, ADD).then_inc(sem["dve_step"], 1)
                        dve.wait_ge(sem["dve_step"], t.next("dve_step"))
                t.skip("acc0_ready", KC), t.skip("acc0_free", KC)
                dve.tensor_copy(mark[0:1, 1:2], mark[0:1, 0:1]).then_inc(sem["stage_over"], 1)
                dve.wait_ge(sem["stage_over"], t.next("stage_over"))

            R = SSM_HEADS
            w = dtw
            dve.wait_ge(sem["const_loaded"], 16)
            dve.wait_ge(sem["acc0_ready"], t.next("acc0_ready"))
            dve.tensor_scalar(v2(w["v"]), accv(0, R), V("dtb")[0:R], None, ADD).then_inc(sem["acc0_free"], 1)
            dve.wait_ge(sem["acc0_free"], t.next("acc0_free"))
            dve.scalar_tensor_tensor(out=w["abs"], in0=w["v"], scalar=-1.0, in1=w["v"], op0=MUL,
                    op1=MAX).then_inc(sem["dt_v"], 1)
            dve.wait_ge(sem["dt_v"], t.next("dt_v"))
            dve.wait_ge(sem["dt_u"], t.next("dt_u", 2))
            dve.tensor_scalar(w["w"], w["u"], 1.0, None, ADD).then_inc(sem["dt_w"], 1)
            dve.wait_ge(sem["dt_w"], t.next("dt_w"))
            dve.tensor_scalar(w["d"], w["w"], -1.0, None, ADD).then_inc(sem["dve_step"], 1)
            dve.wait_ge(sem["dve_step"], t.next("dve_step"))
            dve.tensor_scalar(w["e"], w["d"], 0.0, None, ALU.is_equal).then_inc(sem["dve_step"], 1)
            dve.wait_ge(sem["dve_step"], t.next("dve_step"))
            dve.tensor_tensor(w["d"], w["d"], w["e"], ADD).then_inc(sem["dve_step"], 1)
            dve.wait_ge(sem["dve_step"], t.next("dve_step"))
            dve.reciprocal(w["r"], w["d"]).then_inc(sem["dve_step"], 1)
            dve.wait_ge(sem["dve_step"], t.next("dve_step"))
            dve.tensor_tensor(w["r"], w["r"], w["u"], MUL).then_inc(sem["dve_step"], 1)
            dve.wait_ge(sem["dve_step"], t.next("dve_step"))
            dve.wait_ge(sem["dt_ln"], t.next("dt_ln"))
            dve.tensor_tensor(w["ln"], w["ln"], w["e"], ADD).then_inc(sem["dve_step"], 1)
            dve.wait_ge(sem["dve_step"], t.next("dve_step"))
            dve.tensor_tensor(w["r"], w["r"], w["ln"], MUL).then_inc(sem["dve_step"], 1)
            dve.wait_ge(sem["dve_step"], t.next("dve_step"))
            dve.tensor_scalar(w["dt"], w["v"], 0.0, None, MAX).then_inc(sem["dve_step"], 1)
            dve.wait_ge(sem["dve_step"], t.next("dve_step"))
            dve.tensor_tensor(w["dt"], w["dt"], w["r"], ADD).then_inc(sem["dve_step"], 1)
            dve.wait_ge(sem["dve_step"], t.next("dve_step"))
            dve.tensor_scalar(na[:, 1:2], na[:, 0:1], -1.0, None, MUL).then_inc(sem["dve_step"], 1)
            dve.wait_ge(sem["dve_step"], t.next("dve_step"))
            dve.tensor_scalar(w["dta"], w["dt"], na[:, 1:2], None, MUL).then_inc(sem["dve_step"], 1)
            dve.wait_ge(sem["dve_step"], t.next("dve_step"))
            dve.tensor_tensor_scan(w["cum"], C("scanmask")[0:R, :], w["dta"], 0.0, MUL,
                    ADD).then_inc(sem["dt_ready"], 1)
            dve.wait_ge(sem["dt_ready"], t.next("dt_ready"))
            dve.tensor_copy(mark[0:1, 1:2], mark[0:1, 0:1]).then_inc(sem["cum_rows_ready"], 1)
            dve.wait_ge(sem["cum_rows_ready"], t.next("cum_rows_ready"))
            dve.wait_ge(sem["dt_turned"], t.next("dt_turned"))
            for j, out in enumerate((dt_tm, cum_tm)):
                dve.tensor_copy(out[:, 0:NB, :], bank[j][:, 0:NB * R].rearrange("p (c h) -> p c h",
                        h=R)).then_inc(sem["dve_step"], 1)
                dve.wait_ge(sem["dve_step"], t.next("dve_step"))
                dve.tensor_copy(out[0:NS, NB, :], bank[j][0:NS, NB * R:(NB + 1) * R]).then_inc(sem["dve_step"], 1)
                dve.wait_ge(sem["dve_step"], t.next("dve_step"))
            dve.tensor_tensor(cum_last, cum_tm[0:NS, NB:NB + 1, :].broadcast_to([NS, DEC_BATCH, R]),
                    C("lastcol")[0:NS, :].rearrange("p (b o) -> p b o", o=1).broadcast_to([NS, DEC_BATCH, R]), MUL).then_inc(sem["cum_ready"], 1)
            dve.wait_ge(sem["cum_ready"], t.next("cum_ready"))
            dve.wait_ge(sem["last_ready"], t.next("last_ready"))
            dve.tensor_tensor(wb_tm[:, 0:NB, :], bank[2][:, 0:NB * R].rearrange("p (c h) -> p c h", h=R), cum_tm[:,
                    0:NB, :], SUB).then_inc(sem["dve_step"], 1)
            dve.wait_ge(sem["dve_step"], t.next("dve_step"))
            dve.tensor_tensor(wb_tm[0:NS, NB, :], bank[3][0:NS, 0:R], cum_tm[0:NS, NB, :],
                    SUB).then_inc(sem["wb_ready"], 1)
            dve.wait_ge(sem["wb_ready"], t.next("wb_ready"))
            dve.wait_ge(sem["dec_ready"], t.next("dec_ready"))
            dve.tensor_tensor(wb_tm[:, 0:NB, :], wb_tm[:, 0:NB, :], dt_tm[:, 0:NB, :],
                    MUL).then_inc(sem["dve_step"], 1)
            dve.wait_ge(sem["dve_step"], t.next("dve_step"))
            dve.tensor_tensor(wb_tm[0:NS, NB, :], wb_tm[0:NS, NB, :], dt_tm[0:NS, NB, :],
                    MUL).then_inc(sem["dve_step"], 1)
            dve.wait_ge(sem["dve_step"], t.next("dve_step"))
            dve.wait_ge(sem["cum_g_loaded"], 16 * GROUPS)
            dve.tensor_copy(mark[0:1, 1:2], mark[0:1, 0:1]).then_inc(sem["stage_over"], 1)
            dve.wait_ge(sem["stage_over"], t.next("stage_over"))

            dve.wait_ge(sem["conv_state_loaded"], 16)
            for j in range(2):
                dve.memset(ext[j][:, 0:3], 0.0).then_inc(sem["dve_step"], 1)
                dve.wait_ge(sem["dve_step"], t.next("dve_step"))
            with t.loop("ssm_dve", GROUPS) as g:
                def finish(q):
                    j = q % 2
                    dve.wait_ge(sem["silu_ready"], t.next("silu_ready"))
                    dve.tensor_tensor(fm[:, q, 0:SEQ], conv_p(cacc[j]), conv_p(th[j]),
                            MUL).then_inc(sem["dve_step"], 1)
                    dve.wait_ge(sem["dve_step"], t.next("dve_step"))
                    a, b = (x[:, EXT_P:CL] for x in (cacc[j], th[j]))
                    n = (DEC_BATCH - 1) * EXT_S
                    for lo, hi in ((0, DEC_BATCH - 1), (DEC_BATCH - 1, DEC_BATCH)):
                        nb = hi - lo
                        pick = (lambda x: x[:, 0:n].rearrange("p (b t) -> p b t", t=EXT_S)[:, :,
                                0:DEC_SEQ]) if lo == 0 \
                            else (lambda x: x[:, n:n + DEC_SEQ].rearrange("p (b t) -> p b t", t=DEC_SEQ))
                        out = fm[:, q, SEQ + lo * DEC_SEQ:SEQ + hi * DEC_SEQ].rearrange("p (b t) -> p b t", t=DEC_SEQ)
                        signal = "conv_ready" if lo else "dve_step"
                        dve.tensor_tensor(out, pick(a), pick(b), MUL).then_inc(sem[signal], 1)
                        dve.wait_ge(sem[signal], t.next(signal))

                for q in range(QC):
                    j = q % 2
                    ch = g * QC + q
                    dve.tensor_scalar(ext_s(j)[:, :, 0:3], st_conv[:, bass.ds(ch, 1), :,
                            :].rearrange("p o b t -> p (o b) t"), 1.0, None, MUL).then_inc(sem["dve_step"], 1)
                    dve.wait_ge(sem["dve_step"], t.next("dve_step"))
                    dve.wait_ge(sem[f"acc{j}_free"], t.next(f"acc{j}_free"))
                    co = conv_out[:, bass.ds(ch, 1), :]
                    dve.tensor_scalar(co[:, :, 0:3], ext[j][:, SEQ:EXT_P].rearrange("p (o n) -> p o n", o=1), 1.0,
                            None, MUL).then_inc(sem["dve_step"], 1)
                    dve.wait_ge(sem["dve_step"], t.next("dve_step"))
                    dve.tensor_scalar(co[:, :, 3:27].rearrange("p o (b t) -> p (o b) t", t=3), ext_s(j)[:, :,
                            DEC_SEQ:EXT_S], 1.0, None, MUL).then_inc(sem["dve_step"], 1)
                    dve.wait_ge(sem["dve_step"], t.next("dve_step"))
                    w0 = _V["convw"][0]
                    tap = lambda i: vecs[:, bass.ds(w0 + ch * CONV_W + i, 1)]
                    dve.tensor_scalar(cacc[j], ext[j][:, 0:CL], tap(0), vecs[:, bass.ds(_V["convb"][0] + ch, 1)],
                            MUL, ADD).then_inc(sem["dve_step"], 1)
                    dve.wait_ge(sem["dve_step"], t.next("dve_step"))
                    for i in range(1, CONV_W):
                        signal = "conv_done" if i == CONV_W - 1 else "dve_step"
                        dve.scalar_tensor_tensor(out=cacc[j], in0=ext[j][:, i:i + CL], scalar=tap(i), in1=cacc[j],
                                op0=MUL, op1=ADD).then_inc(sem[signal], 1)
                        dve.wait_ge(sem[signal], t.next(signal))
                    if q >= 1:
                        finish(q - 1)
                finish(QC - 1)
                dve.tensor_scalar(cum_s, cum_g[:, bass.ds(g, 1), :].rearrange("p o t -> p (o t)"), 1.0, None,
                        MUL).then_inc(sem["cum_s_ready"], 1)
                dve.wait_ge(sem["cum_s_ready"], t.next("cum_s_ready"))
                for c in range(NB + 1):
                    n = rows_of(c)
                    dve.wait_ge(sem["x_turned"], t.next("x_turned"))
                    ps = by_head(bank[c % 2][0:n, :])
                    dve.tensor_tensor(by_head(xdt[0:n, c, :]), ps, heads(dt_tm, c, g, n),
                            MUL).then_inc(sem["dve_step"], 1)
                    dve.wait_ge(sem["dve_step"], t.next("dve_step"))
                    dve.tensor_tensor(by_head(xw[0:n, c, :]), ps, heads(wb_tm, c, g, n),
                            MUL).then_inc(sem["turned_read"], 1)
                    dve.wait_ge(sem["turned_read"], t.next("turned_read"))
                dve.wait_ge(sem["b_tm_read"], t.next("b_tm_read"))
                dve.tensor_tensor(b_mask, b_s.rearrange("p (o n) -> p o n", o=1).broadcast_to([NS, DEC_BATCH, P]),
                        C("ofbatch")[0:NS, :].rearrange("p (b o) -> p b o", o=1).broadcast_to([NS, DEC_BATCH, P]), MUL).then_inc(sem["b_tm_ready"], 1)
                dve.wait_ge(sem["b_tm_ready"], t.next("b_tm_ready"))
                dve.wait_ge(sem["cb_ready"], t.next("cb_ready"))
                dve.tensor_tensor(cb_p, bank[0][:, :].rearrange("p (c n) -> p c n", n=P),
                        C("tri").rearrange("p (o n) -> p o n", o=1).broadcast_to([P, NB, P]), MUL).then_inc(sem["dve_step"], 1)
                dve.wait_ge(sem["dve_step"], t.next("dve_step"))
                dve.tensor_tensor(cb_s, bank[1][0:NS, 0:NS], C("tri_s")[0:NS, :], MUL).then_inc(sem["cb_read"], 1)
                dve.wait_ge(sem["cb_read"], t.next("cb_read"))
                dve.wait_ge(sem["states_stored"], t.next("states_stored", 32))
                for c in range(NB):
                    dve.wait_ge(sem["add_ready"], t.next("add_ready"))
                    add = by_head(bank[2 + c % 2][:, :])
                    if c == 0:
                        dve.tensor_copy(by_head(st_p[:, 0, :]), add).then_inc(sem["add_read"], 1)
                        dve.wait_ge(sem["add_read"], t.next("add_read"))
                    else:
                        dve.tensor_tensor(by_head(st_p[:, c, :]), by_head(st_p[:, c - 1, :]), heads(dec_p, c, g,
                                P), MUL).then_inc(sem["dve_step"], 1)
                        dve.wait_ge(sem["dve_step"], t.next("dve_step"))
                        dve.tensor_tensor(by_head(st_p[:, c, :]), by_head(st_p[:, c, :]), add,
                                ADD).then_inc(sem["add_read"], 1)
                        dve.wait_ge(sem["add_read"], t.next("add_read"))
                for hp in range(GC):
                    dve.wait_ge(sem["cum_spread"], t.next("cum_spread"))
                    for j in range(2):
                        h = bass.ds(g * HG + 2 * hp + j, 1)
                        cum_p = cum_tm[:, 0:NB, h].broadcast_to([P, NB, P])
                        dve.tensor_tensor(conv_p(dec[j]).rearrange("p (c n) -> p c n", n=P), bank[j][:,
                                :].rearrange("p (c n) -> p c n", n=P), cum_p, SUB).then_inc(sem["dve_step"], 1)
                        dve.wait_ge(sem["dve_step"], t.next("dve_step"))
                        dve.tensor_scalar(conv_p(dec[j]), conv_p(dec[j]), 0.0, None, MIN).then_inc(sem["dve_step"], 1)
                        dve.wait_ge(sem["dve_step"], t.next("dve_step"))
                    dve.wait_ge(sem["e_pair_ready"], t.next("e_pair_ready"))
                    for j in range(2):
                        h = bass.ds(g * HG + 2 * hp + j, 1)
                        dve.tensor_tensor(dec[j][0:NS, SEQ:T], bank[3][0:NS, j * NS:(j + 1) * NS], cum_tm[0:NS, NB,
                                h].broadcast_to([NS, NS]), SUB).then_inc(sem["dve_step"], 1)
                        dve.wait_ge(sem["dve_step"], t.next("dve_step"))
                        dve.tensor_scalar(dec[j][0:NS, SEQ:T], dec[j][0:NS, SEQ:T], 0.0, None,
                                MIN).then_inc(sem["seg_ready"], 1)
                        dve.wait_ge(sem["seg_ready"], t.next("seg_ready"))
                    for j in range(2):
                        dve.wait_ge(sem["seg_exp"], t.next("seg_exp"))
                        dve.tensor_tensor(conv_p(dec[j]), conv_p(dec[j]), cb_p.rearrange("p c n -> p (c n)"),
                                MUL).then_inc(sem["dve_step"], 1)
                        dve.wait_ge(sem["dve_step"], t.next("dve_step"))
                        dve.tensor_tensor(dec[j][0:NS, SEQ:T], dec[j][0:NS, SEQ:T], cb_s,
                                MUL).then_inc(sem["dve_step"], 1)
                        dve.wait_ge(sem["dve_step"], t.next("dve_step"))
                    dve.tensor_copy(mark[0:1, 1:2], mark[0:1, 0:1]).then_inc(sem["decay_ready"], 1)
                    dve.wait_ge(sem["decay_ready"], t.next("decay_ready"))
                    dve.wait_ge(sem["y_ready"], t.next("y_ready"))
                    y = fm[:, hp, :]
                    ds = vecs[:, bass.ds(_V["dskip"][0] + g * GC + hp, 1)]
                    dve.tensor_tensor(t1[:, P:SEQ], bank[1][:, P:SEQ], e_pair[:, P:SEQ],
                            MUL).then_inc(sem["dve_step"], 1)
                    dve.wait_ge(sem["dve_step"], t.next("dve_step"))
                    dve.tensor_tensor(t1[:, SEQ:T], bank[3][:, 0:NS], e_pair[:, SEQ:T],
                            MUL).then_inc(sem["dve_step"], 1)
                    dve.wait_ge(sem["dve_step"], t.next("dve_step"))
                    dve.scalar_tensor_tensor(out=y[:, 0:SEQ], in0=y[:, 0:SEQ], scalar=ds, in1=bank[0][:, :],
                            op0=MUL, op1=ADD).then_inc(sem["dve_step"], 1)
                    dve.wait_ge(sem["dve_step"], t.next("dve_step"))
                    dve.scalar_tensor_tensor(out=y[:, SEQ:T], in0=y[:, SEQ:T], scalar=ds, in1=bank[2][:, 0:NS],
                            op0=MUL, op1=ADD).then_inc(sem["pair_read"], 1)
                    dve.wait_ge(sem["pair_read"], t.next("pair_read"))
                    dve.tensor_tensor(y[:, P:T], y[:, P:T], t1[:, P:T], ADD).then_inc(sem["dve_step"], 1)
                    dve.wait_ge(sem["dve_step"], t.next("dve_step"))
                    dve.wait_ge(sem["z_ready"], t.next("z_ready"))
                    dve.tensor_tensor(zc[hp % 2], zc[hp % 2], zth[hp % 2], MUL).then_inc(sem["dve_step"], 1)
                    dve.wait_ge(sem["dve_step"], t.next("dve_step"))
                    dve.tensor_tensor(y, y, zc[hp % 2], MUL).then_inc(sem["y_gated"], 1)
                    dve.wait_ge(sem["y_gated"], t.next("y_gated"))
                dve.wait_ge(sem["sq_summed"], t.next("sq_summed", GC))
                for half in range(2):
                    signal = "var_ready" if half else "dve_step"
                    dve.tensor_scalar(rstd[:, half * HT:(half + 1) * HT], bank[half][:, 0:HT], 1.0 / GW, RMS_EPS,
                            MUL, ADD).then_inc(sem[signal], 1)
                    dve.wait_ge(sem[signal], t.next(signal))
                for b in range(DEC_BATCH):
                    dve.wait_ge(sem["adds_ready"], t.next("adds_ready"))
                    add = by_head(bank[2 + b % 2][:, :])
                    dve.tensor_tensor(by_head(st_s[:, b, :]), by_head(st_s[:, b, :]), heads(dec_s, b, g, P),
                            MUL).then_inc(sem["dve_step"], 1)
                    dve.wait_ge(sem["dve_step"], t.next("dve_step"))
                    dve.tensor_tensor(by_head(st_s[:, b, :]), by_head(st_s[:, b, :]), add,
                            ADD).then_inc(sem["adds_read"], 1)
                    dve.wait_ge(sem["adds_read"], t.next("adds_read"))
                dve.tensor_copy(mark[0:1, 1:2], mark[0:1, 0:1]).then_inc(sem["states_done"], 1)
                dve.wait_ge(sem["states_done"], t.next("states_done"))
                dve.wait_ge(sem["std_ready"], t.next("std_ready"))
                dve.reciprocal(rstd, rstd).then_inc(sem["dve_step"], 1)
                dve.wait_ge(sem["dve_step"], t.next("dve_step"))
                for hp in range(GC):
                    gcol = vecs[:, bass.ds(_V["ssmg"][0] + g * GC + hp, 1)]
                    dve.scalar_tensor_tensor(out=BR[:, bass.ds(g * GC + hp, 1), :].rearrange("p o t -> p (o t)"),
                            in0=fm[:, hp, :], scalar=gcol, in1=rstd, op0=MUL, op1=MUL).then_inc(sem["dve_step"], 1)
                    dve.wait_ge(sem["dve_step"], t.next("dve_step"))
                for j in range(2):
                    t.skip(f"acc{j}_free", 2)
            dve.wait_ge(sem["states_stored"], t.next("states_stored", 32))
            for j in range(2):
                t.skip(f"acc{j}_ready", 5 * GROUPS)
            dve.wait_ge(sem["act_over"], t.next("act_over"))
            dve.tensor_copy(mark[0:1, 1:2], mark[0:1, 0:1]).then_inc(sem["stage_over"], 1)
            dve.wait_ge(sem["stage_over"], t.next("stage_over"))

            merge("merge_b", 1)

            for i in range(2):
                t.skip("acc0_ready" if i == 0 else "acc1_ready", 3 if i == 0 else 2)
                t.skip("acc0_free" if i == 0 else "acc1_free", 3 if i == 0 else 2)
            dve.wait_ge(sem["acc1_ready"], t.next("acc1_ready"))
            dve.tensor_tensor(v2(q_r), accv(1), v2(C("rope")), MUL).then_inc(sem["acc1_free"], 1)
            dve.wait_ge(sem["acc1_free"], t.next("acc1_free"))
            dve.tensor_copy(mark[0:1, 1:2], mark[0:1, 0:1]).then_inc(sem["kr_ready"], 1)
            dve.wait_ge(sem["kr_ready"], t.next("kr_ready"))
            inv_std(a_rstd, "cq_summed", Q_LORA, RMS_EPS)
            for c in range(3):
                dve.scalar_tensor_tensor(out=cq[:, c, :], in0=cq[:, c, :], scalar=V("qg", c), in1=a_rstd, op0=MUL,
                        op1=MUL).then_inc(sem["dve_step"], 1)
                dve.wait_ge(sem["dve_step"], t.next("dve_step"))
            inv_std(a_rstd, "ckv_summed", KV_LORA, RMS_EPS)
            for c in range(2):
                dve.scalar_tensor_tensor(out=ckv[:, c, :], in0=ckv[:, c, :], scalar=V("kvg", c), in1=a_rstd,
                        op0=MUL, op1=MUL).then_inc(sem["dve_step"], 1)
                dve.wait_ge(sem["dve_step"], t.next("dve_step"))
            dve.wait_ge(sem["krope_ready"], t.next("krope_ready"))
            dve.tensor_copy(mark[0:1, 1:2], mark[0:1, 0:1]).then_inc(sem["latents_ready"], 1)
            dve.wait_ge(sem["latents_ready"], t.next("latents_ready"))
            dve.tensor_copy(mark[0:1, 1:2], mark[0:1, 0:1]).then_inc(sem["head_read"], 1)
            dve.wait_ge(sem["head_read"], t.next("head_read"))
            with t.loop("heads_dve", MLA_HEADS) as h:
                dve.wait_ge(sem["acc1_ready"], t.next("acc1_ready"))
                dve.tensor_tensor(v2(q_r), accv(1), v2(C("rope")), MUL).then_inc(sem["acc1_free"], 1)
                dve.wait_ge(sem["acc1_free"], t.next("acc1_free"))
                dve.wait_ge(sem["q_lat_ready"], t.next("q_lat_ready"))
                hd = bass.ds(h, 1)
                for c in range(2):
                    dve.tensor_scalar(q_lat[:, c, :, hd, :].rearrange("p b o t -> p b (o t)"), bank[0][:,
                            c * NS:(c + 1) * NS].rearrange("p (b t) -> p b t", t=DEC_SEQ), 1.0, None, MUL).then_inc(sem["dve_step"], 1)
                    dve.wait_ge(sem["dve_step"], t.next("dve_step"))
                dve.tensor_scalar(q_rot[:, :, hd, :].rearrange("p b o t -> p b (o t)"), bank[0][0:ROPE,
                        2 * NS:3 * NS].rearrange("p (b t) -> p b t", t=DEC_SEQ), 1.0, None, MUL).then_inc(sem["q_lat_read"], 1)
                dve.wait_ge(sem["q_lat_read"], t.next("q_lat_read"))
                for qb in range(NB):
                    n = (qb + 1) * P
                    s = bank[3 * (qb % 2)]
                    dve.wait_ge(sem["scores_ready"], t.next("scores_ready"))
                    dve.tensor_tensor(s[:, qb * P:n], s[:, qb * P:n], C("causal"), ADD).then_inc(sem["dve_step"], 1)
                    dve.wait_ge(sem["dve_step"], t.next("dve_step"))
                    softmax(s[:, 0:n], stats[qb % 2], prob[qb % 2][:, 0:n], A_SCALE, "prob_ready")
                dve.wait_ge(sem["head_out"], t.next("head_out"))
                dve.tensor_scalar(BR[:, hd, 0:SEQ].rearrange("p o t -> p (o t)"), bank[0][:, :], 1.0, None,
                        MUL).then_inc(sem["head_read"], 1)
                dve.wait_ge(sem["head_read"], t.next("head_read"))
            t.skip("acc0_ready", MLA_HEADS), t.skip("acc0_free", MLA_HEADS)
            with t.loop("sample_a_dve", 2) as g:
                four = bass.ds(g * 4, 4)
                for c in range(2):
                    dve.tensor_scalar(q_lat_g[:, c, :, :], q_lat[:, c, four, :,
                            :].rearrange("p b h t -> p b (h t)"), 1.0, None, MUL).then_inc(sem["dve_step"], 1)
                    dve.wait_ge(sem["dve_step"], t.next("dve_step"))
                dve.tensor_scalar(q_rot_g, q_rot[:, four, :, :].rearrange("p b h t -> p b (h t)"), 1.0, None,
                        MUL).then_inc(sem["q_lat_read"], 1)
                dve.wait_ge(sem["q_lat_read"], t.next("q_lat_read"))
                dve.wait_ge(sem["acc0_ready"], t.next("acc0_ready"))
                dve.tensor_tensor(s_new, acc[0][:, 0, 0:NS], cst[:, bass.ds(g * NS + _C["newmask"][0], NS)],
                        ADD).then_inc(sem["acc0_free"], 1)
                dve.wait_ge(sem["acc0_free"], t.next("acc0_free"))
                dve.reduce_max(s_stat[:, 6:7], s_new, AX.X).then_inc(sem["dve_step"], 1)
                dve.wait_ge(sem["dve_step"], t.next("dve_step"))
                for kq in range(4):
                    dve.reduce_max(s_stat[:, 2 + kq:3 + kq], bank[kq][:, :], AX.X).then_inc(sem["dve_step"], 1)
                    dve.wait_ge(sem["dve_step"], t.next("dve_step"))
                dve.reduce_max(s_stat[:, 0:1], s_stat[:, 2:7], AX.X).then_inc(sem["dve_step"], 1)
                dve.wait_ge(sem["dve_step"], t.next("dve_step"))
                dve.tensor_scalar(s_stat[:, 1:2], s_stat[:, 0:1], -A_SCALE, None, MUL).then_inc(sem["max_ready"], 1)
                dve.wait_ge(sem["max_ready"], t.next("max_ready"))
                dve.wait_ge(sem["exp_ready"], t.next("exp_ready"))
                dve.reduce_sum(s_stat[:, 0:1], s_stat[:, 8:13], AX.X).then_inc(sem["dve_step"], 1)
                dve.wait_ge(sem["dve_step"], t.next("dve_step"))
                dve.reciprocal(s_stat[:, 0:1], s_stat[:, 0:1]).then_inc(sem["dve_step"], 1)
                dve.wait_ge(sem["dve_step"], t.next("dve_step"))
                dve.tensor_scalar(s_prob, s_prob, s_stat[:, 0:1], None, MUL).then_inc(sem["prob_ready"], 1)
                dve.wait_ge(sem["prob_ready"], t.next("prob_ready"))
                dve.wait_ge(sem["acc1_ready"], t.next("acc1_ready"))
                dve.tensor_copy(s_prob_n, acc[1][0:NS, 0, 0:P]).then_inc(sem["acc1_free"], 1)
                dve.wait_ge(sem["acc1_free"], t.next("acc1_free"))
                dve.wait_ge(sem["lat_turned"], t.next("lat_turned"))
                for c in range(2):
                    for b in range(4):
                        at = c * P + b * NS
                        signal = "o_lat_ready" if (c, b) == (1, 3) else "dve_step"
                        dve.tensor_scalar(o_lat_t[:, c, :, bass.ds(g * 16 + b * DEC_SEQ, DEC_SEQ)], bank[1][:,
                                at:at + NS].rearrange("p (h t) -> p h t", t=DEC_SEQ), 1.0, None, MUL).then_inc(sem[signal], 1)
                        dve.wait_ge(sem[signal], t.next(signal))
            dve.wait_ge(sem["sample_out"], t.next("sample_out"))
            dve.tensor_copy(BR[:, 0:MLA_HEADS, SEQ:T], bank[2][:, 0:MLA_HEADS * NS].rearrange("p (h t) -> p h t",
                    t=NS)).then_inc(sem["dve_step"], 1)
            dve.wait_ge(sem["dve_step"], t.next("dve_step"))
            dve.wait_ge(sem["act_over"], t.next("act_over"))
            dve.tensor_copy(mark[0:1, 1:2], mark[0:1, 0:1]).then_inc(sem["stage_over"], 1)
            dve.wait_ge(sem["stage_over"], t.next("stage_over"))

            merge("merge_a", 0)

            with t.loop("mem_k_dve", 4) as i:
                for p in range(2):
                    dve.wait_ge(sem[f"acc{p}_ready"], t.next(f"acc{p}_ready"))
                    dve.tensor_scalar(mk[:, bass.ds(2 * i + p, 1), :].rearrange("p o (a n) -> p (o a) n", a=2),
                            acc[p][:, :, 0:P], 1.0, None, MUL).then_inc(sem[f"acc{p}_free"], 1)
                    dve.wait_ge(sem[f"acc{p}_free"], t.next(f"acc{p}_free"))
            for p in range(2):
                dve.wait_ge(sem[f"acc{p}_ready"], t.next(f"acc{p}_ready"))
                dve.tensor_copy(mv[:, :, p * 512:(p + 1) * 512], acc[p][:, :, :]).then_inc(sem[f"acc{p}_free"], 1)
                dve.wait_ge(sem[f"acc{p}_free"], t.next(f"acc{p}_free"))
            dve.tensor_copy(mark[0:1, 1:2], mark[0:1, 0:1]).then_inc(sem["mem_kv_ready"], 1)
            dve.wait_ge(sem["mem_kv_ready"], t.next("mem_kv_ready"))
            with t.loop("mem_heads_dve", MEM_HEADS) as h:
                dve.tensor_scalar(k_h, mk[:, bass.ds(2 * h, 2), :], 1.0, None, MUL).then_inc(sem["dve_step"], 1)
                dve.wait_ge(sem["dve_step"], t.next("dve_step"))
                dve.tensor_scalar(v_h, mv[:, :, bass.ds(h * MEM_DIM, MEM_DIM)], 1.0, None,
                        MUL).then_inc(sem["kv_head_ready"], 1)
                dve.wait_ge(sem["kv_head_ready"], t.next("kv_head_ready"))
                for p in range(2):
                    dve.wait_ge(sem[f"acc{p}_free"], t.next(f"acc{p}_free"))
                dve.tensor_scalar(mq_s[:, bass.ds(2 * h, 2), :], q_h[:, :, SEQ:T], 1.0, None,
                        MUL).then_inc(sem["dve_step"], 1)
                dve.wait_ge(sem["dve_step"], t.next("dve_step"))
                for qb in range(NB):
                    dve.wait_ge(sem["scores_ready"], t.next("scores_ready"))
                    softmax(bank[qb % 2][:, 0:N_MEM], m_stats[qb % 2], m_prob[qb % 2], M_SCALE, "prob_ready")
                dve.wait_ge(sem["head_out"], t.next("head_out"))
                for c in range(2):
                    signal = "head_read" if c else "dve_step"
                    dve.tensor_scalar(BR[:, bass.ds(2 * h + c, 1), 0:SEQ].rearrange("p o t -> p (o t)"), bank[c][:,
                            :], 1.0, None, MUL).then_inc(sem[signal], 1)
                    dve.wait_ge(sem[signal], t.next(signal))
            for j in range(2):
                t.skip(f"acc{j}_ready", MEM_HEADS)
            dve.memset(m_scores, 0.0).then_inc(sem["dve_step"], 1)
            dve.wait_ge(sem["dve_step"], t.next("dve_step"))
            with t.loop("sample_m_dve", DEC_BATCH // 2) as i:
                for j in range(2):
                    mask = cst[:, bass.ds(i * (2 * NS) + (_C["bmask"][0] + j * NS), NS)]
                    dve.tensor_tensor(q_b[j], mq_s, mask.rearrange("p (o t) -> p o t", o=1).broadcast_to([P, 8,
                            NS]), MUL).then_inc(sem["q_b_ready"], 1)
                    dve.wait_ge(sem["q_b_ready"], t.next("q_b_ready"))
                for j in range(2):
                    dve.wait_ge(sem["scores_ready"], t.next("scores_ready"))
                    dve.tensor_tensor(m_scores, m_scores, bank[j][:, 0:N_MEM], ADD).then_inc(sem["dve_step"], 1)
                    dve.wait_ge(sem["dve_step"], t.next("dve_step"))
            softmax(m_scores, m_stats[0], m_scores, M_SCALE, "prob_ready")
            for j in range(2):
                dve.tensor_copy(mark[0:1, 1:2], mark[0:1, 0:1]).then_inc(sem["head_read"], 1)
                dve.wait_ge(sem["head_read"], t.next("head_read"))
            with t.loop("sample_mv_dve", DEC_BATCH // 2) as i:
                for j in range(2):
                    dve.wait_ge(sem["head_out"], t.next("head_out"))
                    at = i * (2 * DEC_SEQ) + (SEQ + j * DEC_SEQ)
                    dve.tensor_scalar(BR[:, 0:8, bass.ds(at, DEC_SEQ)], bank[j][:,
                            0:8 * DEC_SEQ].rearrange("p (c t) -> p c t", t=DEC_SEQ), 1.0, None, MUL).then_inc(sem["head_read"], 1)
                    dve.wait_ge(sem["head_read"], t.next("head_read"))
            dve.wait_ge(sem["act_over"], t.next("act_over"))
            dve.tensor_copy(mark[0:1, 1:2], mark[0:1, 0:1]).then_inc(sem["stage_over"], 1)
            dve.wait_ge(sem["stage_over"], t.next("stage_over"))

            merge("merge_m", 2)

            with t.loop("out_dve", KC // 4) as i:
                for p in range(4):
                    dve.wait_ge(sem[f"acc{p % 2}_ready"], t.next(f"acc{p % 2}_ready"))
                    x = X[:, bass.ds(4 * i + p, 1), :].rearrange("p o t -> p (o t)")
                    dve.scalar_tensor_tensor(out=v2(x), in0=v2(x), scalar=ALPHA, in1=accv(p % 2), op0=MUL,
                            op1=ADD).then_inc(sem[f"acc{p % 2}_free"], 1)
                    dve.wait_ge(sem[f"acc{p % 2}_free"], t.next(f"acc{p % 2}_free"))
            norm("ln1g", "ln1b")
            dve.tensor_copy(mark[0:1, 1:2], mark[0:1, 0:1]).then_inc(sem["normed"], 1)
            dve.wait_ge(sem["normed"], t.next("normed"))
            with t.loop("up_dve", FC // 4) as i:
                for p in range(4):
                    dve.wait_ge(sem[f"acc{p % 2}_ready"], t.next(f"acc{p % 2}_ready"))
                    b = vecs[:, bass.ds(i * 4 + (_V["bup"][0] + p), 1)]
                    dve.tensor_scalar(v2(relu[p % 2]), accv(p % 2), b, 0.0, ADD,
                            MAX).then_inc(sem[f"acc{p % 2}_free"], 1)
                    dve.wait_ge(sem[f"acc{p % 2}_free"], t.next(f"acc{p % 2}_free"))
                    dve.tensor_tensor(hid[:, bass.ds(4 * i + p, 1), :].rearrange("p o t -> p (o t)"), relu[p % 2],
                            relu[p % 2], MUL).then_inc(sem["dve_step"], 1)
                    dve.wait_ge(sem["dve_step"], t.next("dve_step"))
            dve.tensor_copy(mark[0:1, 1:2], mark[0:1, 0:1]).then_inc(sem["hidden_ready"], 1)
            dve.wait_ge(sem["hidden_ready"], t.next("hidden_ready"))
            with t.loop("down_dve", KC // 2) as i:
                for p in range(2):
                    x = X[:, bass.ds(2 * i + p, 1), :].rearrange("p o t -> p (o t)")
                    b = vecs[:, bass.ds(i * 2 + (_V["bdown"][0] + p), 1)]
                    dve.tensor_scalar(x, x, ALPHA, b, MUL, ADD).then_inc(sem["dve_step"], 1)
                    dve.wait_ge(sem["dve_step"], t.next("dve_step"))
                    dve.wait_ge(sem[f"acc{p}_ready"], t.next(f"acc{p}_ready"))
                    dve.tensor_tensor(v2(x), v2(x), accv(p), ADD).then_inc(sem[f"acc{p}_free"], 1)
                    dve.wait_ge(sem[f"acc{p}_free"], t.next(f"acc{p}_free"))
            norm("ln2g", "ln2b")
            dve.tensor_copy(mark[0:1, 1:2], mark[0:1, 0:1]).then_inc(sem["normed"], 1)
            dve.wait_ge(sem["normed"], t.next("normed"))

        @block.tensor
        def _(pe):
            t = Counts(pe, {})
            at_slot = [0]

            def next_block():
                s = at_slot[0]
                at_slot[0] = (s + 1) % RING
                pe.wait_ge(sem[f"weights_in_slot{s}"], t.next(f"weights_in_slot{s}", 16))
                return ring[:, s * BLOCK:(s + 1) * BLOCK]

            def project(p, x, n_blocks=1, width=HT):
                pe.wait_ge(sem[f"acc{p}_free"], t.next(f"acc{p}_free"))
                for b in range(n_blocks):
                    w = next_block()
                    for half in range(2):
                        for k in range(KC):
                            kk = b * KC + k
                            m = pe.matmul(acc[p][:, half, 0:width], w[:, k * P:(k + 1) * P],
                                          x(kk)[:, half * width:(half + 1) * width],
                                          start=kk == 0, stop=kk == n_blocks * KC - 1)
                            if half == 0 and k == 0:
                                m.then_inc(sem["blocks_begun"], 1)
                m.then_inc(sem[f"acc{p}_ready"], 1)

            def rms(squares, name):
                for i, s in enumerate(squares):
                    for half in range(2):
                        m = pe.matmul(bank[2 + half][:, 0:HT], C("ones"), s[:, half * HT:(half + 1) * HT],
                                       start=i == 0, stop=i == len(squares) - 1)
                m.then_inc(sem[name], 1)

            def norm():
                for i, (name, src) in enumerate((("sums_ready", X), ("norm_summed", n_sq))):
                    pe.wait_ge(sem["norm_in"], t.next("norm_in"))
                    for c in range(KC):
                        for half in range(2):
                            m = pe.matmul(bank[2 * i + half][:, 0:HT], C("ones"), src[:, c, half * HT:(half + 1) * HT],
                                           start=c == 0, stop=c == KC - 1)
                    m.then_inc(sem[name], 1)

            def merge(name, n_blocks):
                pe.wait_ge(sem["stage_over"], t.next("stage_over"))
                with t.loop(f"{name}_pe", KC):
                    at_slot[0] = START[name]
                    project(0, lambda c: X[:, c, :])
                    project(1, lambda c: BR[:, c, :], n_blocks)

            pe.wait_ge(sem["const_loaded"], 16)
            pe.wait_ge(sem["x_loaded"], 16)
            at_slot[0] = START["dt"]
            project(0, lambda c: X[:, c, :])
            pe.wait_ge(sem["dt_ready"], t.next("dt_ready"))
            for j, row in enumerate((dtw["dt"], dtw["cum"])):
                for c, b in enumerate(blocks_of(row)):
                    n = P if c < NB else NS
                    m = pe.transpose(bank[j][0:n, c * SSM_HEADS:(c + 1) * SSM_HEADS], b, ident32)
            m.then_inc(sem["dt_turned"], 1)
            pe.wait_ge(sem["cum_ready"], t.next("cum_ready"))
            pe.matmul(bank[2][:, 0:NB * SSM_HEADS], C("last"), cum_tm[:, 0:NB, :], start=True, stop=True)
            pe.matmul(bank[3][0:NS, 0:SSM_HEADS], C("last_s")[0:NS, :], cum_tm[0:NS, NB, :], start=True, stop=True)
            m = pe.matmul(bank[1][:, 0:DEC_BATCH * SSM_HEADS], C("ones")[0:NS, :], cum_last[:, :, :],
                           start=True, stop=True)
            m.then_inc(sem["last_ready"], 1)

            pe.wait_ge(sem["stage_over"], t.next("stage_over"))
            with t.loop("ssm_pe", GROUPS) as g:
                at_slot[0] = START["ssm"]
                for q in range(QC):
                    project(q % 2, lambda c: X[:, c, :])
                for hp in range(2):
                    project(hp, lambda c: X[:, c, :])
                pe.wait_ge(sem["conv_ready"], t.next("conv_ready", QC))
                for c in range(NB + 1):
                    n = rows_of(c)
                    if c >= 2:
                        pe.wait_ge(sem["turned_read"], t.next("turned_read"))
                    for f in range(GC):
                        m = pe.transpose(bank[c % 2][0:n, f * P:(f + 1) * P], toks(fm[:, f, :], c), C("ident"))
                    m.then_inc(sem["x_turned"], 1)
                for c in range(NB):
                    pe.transpose(bank[2][:, c * P:(c + 1) * P], toks(fm[:, GC, :], c), C("ident"))
                m = pe.transpose(bank[3][0:NS, 0:P], toks(fm[:, GC, :], NB), C("ident"))
                m.then_inc(sem["b_turned"], 1)
                pe.wait_ge(sem["turned_read"], t.next("turned_read", 2))
                for c in range(NB):
                    pe.matmul(bank[0][:, c * P:(c + 1) * P], toks(fm[:, GC, :], c), toks(fm[:, GC + 1, :], c),
                               start=True, stop=True)
                m = pe.matmul(bank[1][0:NS, 0:NS], toks(fm[:, GC, :], NB), toks(fm[:, GC + 1, :], NB),
                               start=True, stop=True)
                m.then_inc(sem["cb_ready"], 1)
                pe.wait_ge(sem["b_tm_ready"], t.next("b_tm_ready"))
                for c in range(NB):
                    if c >= 2:
                        pe.wait_ge(sem["add_read"], t.next("add_read"))
                    m = pe.matmul(bank[2 + c % 2][:, :], b_tm[:, c, :], xw[:, c, :], start=True, stop=True)
                    m.then_inc(sem["add_ready"], 1)
                pe.wait_ge(sem["add_read"], t.next("add_read", 2))
                pe.wait_ge(sem["cb_read"], t.next("cb_read"))
                pe.wait_ge(sem["cum_s_ready"], t.next("cum_s_ready"))
                pe.wait_ge(sem["states_loaded"], t.next("states_loaded", 16))
                for hp in range(GC):
                    if hp:
                        pe.wait_ge(sem["pair_read"], t.next("pair_read"))
                    for j in range(2):
                        h = 2 * hp + j
                        sel = C("sel")[0:HG, h * P:(h + 1) * P]
                        pe.matmul(bank[j][:, 0:SEQ], sel, cum_s[:, 0:SEQ], start=True, stop=True)
                    sp = C("selpair")[0:HG, hp * P:(hp + 1) * P]
                    pe.matmul(bank[2][:, 0:SEQ], sp, cum_s[:, 0:SEQ], start=True, stop=True)
                    for j in range(2):
                        h = 2 * hp + j
                        pe.matmul(bank[3][0:NS, j * NS:(j + 1) * NS], C("sel")[0:HG, h * P:h * P + NS],
                                   cum_s[:, SEQ:T], start=True, stop=True)
                    m = pe.matmul(bank[3][:, 2 * NS:3 * NS], sp, cum_s[:, SEQ:T], start=True, stop=True)
                    m.then_inc(sem["cum_spread"], 1)
                    if hp in (1, 2):
                        project((hp + 1) % 2, lambda c: X[:, c, :])
                    pe.wait_ge(sem["decay_ready"], t.next("decay_ready"))
                    for c in range(NB):
                        for j in range(2):
                            h = 2 * hp + j
                            pe.matmul(bank[0][j * HEAD_DIM:(j + 1) * HEAD_DIM, c * P:(c + 1) * P],
                                       xdt[:, c, h * HEAD_DIM:(h + 1) * HEAD_DIM], toks(dec[j], c),
                                       start=True, stop=True)
                    for c in range(1, NB):
                        pe.matmul(bank[1][:, c * P:(c + 1) * P], st_p[:, c - 1, hp * P:(hp + 1) * P],
                                   toks(fm[:, GC + 1, :], c), start=True, stop=True)
                    for j in range(2):
                        h = 2 * hp + j
                        pe.matmul(bank[2][j * HEAD_DIM:(j + 1) * HEAD_DIM, 0:NS],
                                   xdt[0:NS, NB, h * HEAD_DIM:(h + 1) * HEAD_DIM], dec[j][0:NS, SEQ:T],
                                   start=True, stop=True)
                    for b in range(DEC_BATCH):
                        at = SEQ + b * DEC_SEQ
                        m = pe.matmul(bank[3][:, b * DEC_SEQ:(b + 1) * DEC_SEQ], st_s[:, b, hp * P:(hp + 1) * P],
                                       fm[:, GC + 1, at:at + DEC_SEQ], start=True, stop=True)
                    m.then_inc(sem["y_ready"], 1)
                pe.wait_ge(sem["pair_read"], t.next("pair_read"))
                for hp in range(GC):
                    pe.wait_ge(sem["sq_ready"], t.next("sq_ready"))
                    for half in range(2):
                        m = pe.matmul(bank[half][:, 0:HT], C("ones"), sq[hp][:, half * HT:(half + 1) * HT],
                                       start=hp == 0, stop=hp == GC - 1)
                    m.then_inc(sem["sq_summed"], 1)
                for b in range(DEC_BATCH):
                    if b >= 2:
                        pe.wait_ge(sem["adds_read"], t.next("adds_read"))
                    m = pe.matmul(bank[2 + b % 2][:, :], b_mask[:, b, :], xw[0:NS, NB, :], start=True, stop=True)
                    m.then_inc(sem["adds_ready"], 1)
                pe.wait_ge(sem["adds_read"], t.next("adds_read", 2))
                pe.wait_ge(sem["var_ready"], t.next("var_ready"))

            merge("merge_b", 2)

            pe.wait_ge(sem["stage_over"], t.next("stage_over"))
            at_slot[0] = START["latents"]
            for i in range(6):
                project(i % 2, lambda c: X[:, c, :])
            pe.wait_ge(sem["squares_ready"], t.next("squares_ready", 3))
            rms(a_sq[0:3], "cq_summed")
            pe.wait_ge(sem["kr_ready"], t.next("kr_ready"))
            for half in range(2):
                m = pe.matmul(bank[half][:, 0:HT], C("fold"), q_r[:, half * HT:(half + 1) * HT], start=True,
                        stop=True)
            m.then_inc(sem["kr_folded"], 1)
            pe.wait_ge(sem["squares_ready"], t.next("squares_ready", 2))
            pe.wait_ge(sem["var_ready"], t.next("var_ready"))
            rms(a_sq[3:5], "ckv_summed")
            pe.wait_ge(sem["latents_ready"], t.next("latents_ready"))
            for c in range(2):
                m = pe.transpose(bank[0][0:NS, c * P:(c + 1) * P], ckv[:, c, SEQ:T], C("ident"))
            m.then_inc(sem["new_turned"], 1)
            pe.wait_ge(sem["new_read"], t.next("new_read"))
            t.skip("var_ready")
            with t.loop("heads_pe", MLA_HEADS):
                at_slot[0] = START["heads"]
                w = next_block()
                for p, off in ((0, 0), (1, P)):
                    pe.wait_ge(sem[f"acc{p}_free"], t.next(f"acc{p}_free"))
                    for half in range(2):
                        for c in range(3):
                            m = pe.matmul(acc[p][:, half, 0:HT], w[:, c * 256 + off:c * 256 + off + P],
                                           cq[:, c, half * HT:(half + 1) * HT], start=c == 0, stop=c == 2)
                            if (p, half, c) == (0, 0, 0):
                                m.then_inc(sem["blocks_begun"], 1)
                    m.then_inc(sem[f"acc{p}_ready"], 1)
                pe.wait_ge(sem["acc0_free"], t.value("acc0_free") + 1)
                pe.wait_ge(sem["acc1_free"], t.value("acc1_free") + 1)
                pe.wait_ge(sem["head_read"], t.next("head_read"))
                for c in range(2):
                    pe.matmul(bank[0][:, c * NS:(c + 1) * NS], w[:, 768 + c * P:768 + (c + 1) * P], q_n[:, SEQ:T],
                               start=True, stop=True)
                m = pe.matmul(bank[0][0:ROPE, 2 * NS:3 * NS], C("fold")[:, 0:ROPE], q_r[:, SEQ:T],
                               start=True, stop=True)
                m.then_inc(sem["q_lat_ready"], 1)
                w = next_block()
                for c in range(2):
                    m = pe.matmul(bank[1][:, :], w[:, c * P:(c + 1) * P], ckv[:, c, 0:SEQ], start=c == 0, stop=c == 1)
                    if c == 0:
                        m.then_inc(sem["blocks_begun"], 1)
                m.then_inc(sem["k_ready"], 1)
                for b in range(NB):
                    for c in range(2):
                        m = pe.matmul(bank[2][:, b * P:(b + 1) * P], ckv[:, c, b * P:(b + 1) * P],
                                       w[:, 256 + c * P:256 + (c + 1) * P], start=c == 0, stop=c == 1)
                m.then_inc(sem["v_ready"], 1)
                pe.wait_ge(sem["kv_read"], t.next("kv_read", 2))
                pe.wait_ge(sem["q_lat_read"], t.next("q_lat_read"))

                def turn(qb):
                    pe.wait_ge(sem["prob_ready"], t.next("prob_ready"))
                    for b in range(qb + 1):
                        m = pe.transpose(bank[1 + qb % 2][:, b * P:(b + 1) * P], prob[qb % 2][:, b * P:(b + 1) * P],
                                          C("ident"))
                    m.then_inc(sem["prob_turned"], 1)

                for qb in range(NB):
                    n = (qb + 1) * P
                    s = bank[3 * (qb % 2)]
                    if qb >= 2:
                        pe.wait_ge(sem["exp_ready"], t.next("exp_ready"))
                    pe.matmul(s[:, 0:n], q_n[:, qb * P:n], k_n[:, 0:n], start=True, stop=False)
                    m = pe.matmul(s[:, 0:n], q_r[:, qb * P:n], krope[:, 0:n], start=False, stop=True)
                    m.then_inc(sem["scores_ready"], 1)
                    if qb >= 1:
                        if qb >= 3:
                            pe.wait_ge(sem["turned_out"], t.next("turned_out"))
                        turn(qb - 1)
                pe.wait_ge(sem["turned_out"], t.next("turned_out"))
                turn(NB - 1)
                pe.wait_ge(sem["turned_out"], t.next("turned_out", 2))
                pe.wait_ge(sem["exp_ready"], t.next("exp_ready", 2))
                for b in range(NB):
                    m = pe.matmul(bank[0][:, b * P:SEQ], v_tm[:, b, :], prob_t[:, b, b * P:SEQ],
                                   start=b == 0, stop=b == NB - 1, skip_group_check=True)
                m.then_inc(sem["head_out"], 1)

            pe.wait_ge(sem["head_read"], t.next("head_read"))
            with t.loop("sample_a_pe", 2):
                pe.wait_ge(sem["q_lat_read"], t.next("q_lat_read"))
                def score(out, b, keys_of, rope):
                    for c in range(2):
                        pe.matmul(out, q_lat_g[:, c, b, :], keys_of(c), start=c == 0, stop=False)
                    return pe.matmul(out, q_rot_g[:, b, :], rope, start=False, stop=True)

                for b in range(4):
                    for kq in range(4):
                        pe.wait_ge(sem[f"keys_in_slot{kq}"], t.next(f"keys_in_slot{kq}", 8 * 16))
                        kv = keys[kq].rearrange("p (g c n) -> p c g n", g=4, c=2)
                        m = score(bank[kq][b * NS:(b + 1) * NS, :], b, lambda c: kv[:, c, :, :], key_rope[kq])
                        m.then_inc(sem["keys_used"], 1)
                pe.wait_ge(sem[f"acc{0}_free"], t.next(f"acc{0}_free"))
                for b in range(4):
                    m = score(acc[0][b * NS:(b + 1) * NS, 0, 0:NS], b, lambda c: ckv[:, c, SEQ:T], krope[0:ROPE,
                            SEQ:T])
                m.then_inc(sem["acc0_ready"], 1)
                pe.wait_ge(sem["prob_ready"], t.next("prob_ready"))
                pe.wait_ge(sem[f"acc{1}_free"], t.next(f"acc{1}_free"))
                m = pe.transpose(acc[1][0:NS, 0, 0:P], s_prob[:, N_PAGES * PAGE:], C("ident"))
                m.then_inc(sem["acc1_ready"], 1)
                for kq in range(4):
                    for i in range(4):
                        at = (kq * 4 + i) * PAGE
                        m = pe.transpose(bank[kq][:, i * P:(i + 1) * P], s_prob[:, at:at + PAGE], C("ident"))
                    m.then_inc(sem["prob_turned"], 1)
                pe.wait_ge(sem["acc1_free"], t.value("acc1_free") + 1)
                pe.wait_ge(sem["turned_out"], t.next("turned_out", 4))
                for b in range(4):
                    out = bank[0][b * NS:(b + 1) * NS, 0:KV_LORA]
                    for kq in range(4):
                        pe.wait_ge(sem[f"rows_in_slot{kq}"], t.next(f"rows_in_slot{kq}", 4 * 16))
                        for i in range(4):
                            m = pe.matmul(out, s_prob_t[:, kq * 4 + i, b * NS:(b + 1) * NS],
                                           rows[kq][:, i * KV_LORA:(i + 1) * KV_LORA],
                                           start=kq == 0 and i == 0, stop=False)
                        m.then_inc(sem["rows_used"], 1)
                    m = pe.matmul(out, s_prob_n[:, b * NS:(b + 1) * NS], ckv_new, start=False, stop=True)
                m.then_inc(sem["lat_ready"], 1)
                pe.wait_ge(sem["lat_read"], t.next("lat_read"))
                for c in range(2):
                    m = pe.transpose(bank[1][:, c * P:(c + 1) * P], o_lat[:, c * P:(c + 1) * P], C("ident"))
                m.then_inc(sem["lat_turned"], 1)
                pe.wait_ge(sem["o_lat_ready"], t.next("o_lat_ready"))
            at_slot[0] = START["values"]
            for w4 in range(2):
                w = next_block()
                for hh in range(4):
                    h = w4 * 4 + hh
                    for c in range(2):
                        m = pe.matmul(bank[2][:, h * NS:(h + 1) * NS], w[:, c * 512 + hh * P:c * 512 + (hh + 1) * P],
                                       o_lat_t[:, c, h, :], start=c == 0, stop=c == 1)
                        if hh == 0 and c == 0:
                            m.then_inc(sem["blocks_begun"], 1)
            m.then_inc(sem["sample_out"], 1)

            merge("merge_a", 1)

            pe.wait_ge(sem["stage_over"], t.next("stage_over"))
            pe.wait_ge(sem["mem_loaded"], t.next("mem_loaded", 16))
            with t.loop("mem_k_pe", 4):
                at_slot[0] = START["mem_k"]
                for p in range(2):
                    project(p, lambda c: mem[:, c, :], width=P)
            at_slot[0] = START["mem_v"]
            for nn in range(2):
                pe.wait_ge(sem[f"acc{nn}_free"], t.next(f"acc{nn}_free"))
                for b in range(4):
                    w = next_block()
                    for c in range(2):
                        for mb in range(2):
                            m = pe.matmul(acc[nn][:, mb, :], mem[:, b * 2 + c, mb * P:(mb + 1) * P],
                                           w[:, c * 512:(c + 1) * 512], start=b == 0 and c == 0, stop=b == 3 and c == 1)
                            if c == 0 and mb == 0:
                                m.then_inc(sem["blocks_begun"], 1)
                m.then_inc(sem[f"acc{nn}_ready"], 1)
            with t.loop("mem_heads_pe", MEM_HEADS):
                at_slot[0] = START["mq"]
                for p in range(2):
                    project(p, lambda c: X[:, c, :])
                pe.wait_ge(sem["acc0_free"], t.value("acc0_free") + 1)
                pe.wait_ge(sem["acc1_free"], t.value("acc1_free") + 1)
                pe.wait_ge(sem["kv_head_ready"], t.next("kv_head_ready"))
                for qb in range(NB):
                    if qb >= 2:
                        pe.wait_ge(sem["exp_ready"], t.next("exp_ready"))
                    for c in range(2):
                        m = pe.matmul(bank[qb % 2][:, 0:N_MEM], q_h[:, c, qb * P:(qb + 1) * P], k_h[:, c, :],
                                       start=c == 0, stop=c == 1)
                    m.then_inc(sem["scores_ready"], 1)
                    for q in ([qb - 1] if 1 <= qb < NB - 1 else [NB - 2, NB - 1] if qb == NB - 1 else []):
                        if q >= 2:
                            pe.wait_ge(sem["turned_out"], t.next("turned_out"))
                        pe.wait_ge(sem["prob_ready"], t.next("prob_ready"))
                        for b in range(2):
                            m = pe.transpose(bank[2 + q % 2][:, b * P:(b + 1) * P], m_prob[q % 2][:,
                                    b * P:(b + 1) * P],
                                              C("ident"))
                        m.then_inc(sem["prob_turned"], 1)
                pe.wait_ge(sem["turned_out"], t.next("turned_out", 2))
                pe.wait_ge(sem["exp_ready"], t.next("exp_ready", 2))
                for c in range(2):
                    for b in range(2):
                        m = pe.matmul(bank[c][:, :], v_h[:, b, c * P:(c + 1) * P], m_prob_t[:, b, :],
                                       start=b == 0, stop=b == 1)
                m.then_inc(sem["head_out"], 1)
                pe.wait_ge(sem["head_read"], t.next("head_read"))
            with t.loop("sample_m_pe", DEC_BATCH // 2):
                for j in range(2):
                    pe.wait_ge(sem[f"mem_k{j}_loaded"], t.next(f"mem_k{j}_loaded", 16))
                    pe.wait_ge(sem["q_b_ready"], t.next("q_b_ready"))
                    for h in range(MEM_HEADS):
                        for c in range(2):
                            m = pe.matmul(bank[j][h * NS:(h + 1) * NS, 0:N_MEM], q_b[j][:, 2 * h + c, :],
                                           mem_k[j][:, 2 * h + c, :], start=c == 0, stop=c == 1)
                    m.then_inc(sem["scores_ready"], 1)
            pe.wait_ge(sem["prob_ready"], t.next("prob_ready"))
            for b in range(2):
                m = pe.transpose(bank[2][:, b * P:(b + 1) * P], m_scores[:, b * P:(b + 1) * P], C("ident"))
            m.then_inc(sem["prob_turned"], 1)
            pe.wait_ge(sem["turned_out"], t.next("turned_out"))
            with t.loop("sample_mv_pe", DEC_BATCH // 2) as i:
                for j in range(2):
                    pe.wait_ge(sem["head_read"], t.next("head_read"))
                    pe.wait_ge(sem[f"mem_v{j}_loaded"], t.next(f"mem_v{j}_loaded", 16))
                    for c in range(8):
                        for b in range(2):
                            m = pe.matmul(bank[j][:, c * DEC_SEQ:(c + 1) * DEC_SEQ], mem_v[j][:, b,
                                    c * P:(c + 1) * P],
                                           ms_prob_t[:, b, bass.ds(i * (2 * DEC_SEQ) + (j * DEC_SEQ + c // 2 * NS),
                                                   DEC_SEQ)],
                                           start=b == 0, stop=b == 1)
                    m.then_inc(sem["head_out"], 1)

            merge("merge_m", 1)

            pe.wait_ge(sem["stage_over"], t.next("stage_over"))
            with t.loop("out_pe", KC // 4):
                at_slot[0] = START["out"]
                for p in range(4):
                    project(p % 2, lambda c: MG[:, c, :])
            norm()
            pe.wait_ge(sem["normed"], t.next("normed"))
            with t.loop("up_pe", FC // 4):
                at_slot[0] = START["up"]
                for p in range(4):
                    project(p % 2, lambda c: X[:, c, :])
            pe.wait_ge(sem["hidden_ready"], t.next("hidden_ready"))
            with t.loop("down_pe", KC // 2):
                at_slot[0] = START["down"]
                for p in range(2):
                    project(p, lambda c: hid[:, c, :], D_FF // BLOCK)
            norm()


def lay_out(a):
    def tiles(w):
        k, n = w.shape
        return w.reshape(k // BLOCK, KC, P, n // P, P).transpose(3, 0, 2, 1, 4).reshape(n // P, k // BLOCK, P, BLOCK)
    w_in = a["w_in"]
    sizes = (Q_LORA, KV_LORA, ROPE, D_INNER, CONV_DIM, SSM_HEADS, MEM_HEADS * MEM_DIM, 3 * D_MODEL)
    cq, ckv, kr, z, xbc, dt, mq, gates = np.split(w_in, np.cumsum(sizes)[:-1], axis=1)
    order = [c for g in range(GROUPS) for c in [*range(g * GC, g * GC + GC), D_INNER // P + g, D_INNER // P + GROUPS + g]]
    blocks = []
    add = lambda x: blocks.extend(x.reshape(-1, P, BLOCK))
    dtp = np.zeros((D_MODEL, P), np.float32); dtp[:, :SSM_HEADS] = dt
    add(tiles(dtp))
    tx, tz = tiles(xbc), tiles(z)
    for g in range(GROUPS):
        add(tx[order[g * QC:(g + 1) * QC]])
        add(tz[g * GC:(g + 1) * GC])
    tg = tiles(gates)
    branches = {"b": (1, tiles(a["w_o_ssm"])), "a": (0, tiles(a["w_o_mla"])), "m": (2, tiles(a["w_o_mem"]))}
    def merge(name):
        i, w = branches[name]
        for j in range(KC):
            add(tg[i * KC + j])
            add(w[j])
    merge("b")
    add(tiles(cq)); add(tiles(ckv))
    swap = np.r_[ROPE // 2:ROPE, 0:ROPE // 2]
    add(tiles(np.concatenate([kr, kr[:, swap]], 1)))
    uq, uk, uv = a["w_uq"], a["w_uk"], a["w_uv"]
    for h in range(MLA_HEADS):
        q = np.concatenate([uq[:, h, :NOPE], uq[:, h, NOPE:], uq[:, h, NOPE:][:, swap]], 1).reshape(3, P, 256)
        add(np.concatenate([q.transpose(1, 0, 2).reshape(P, 768), uk[:, h, :].T], 1))
        kh = uk[:, h, :].reshape(2, P, P).transpose(1, 0, 2).reshape(P, 256)
        vh = uv[:, h, :].reshape(2, P, P).transpose(1, 0, 2).reshape(P, 256)
        add(np.concatenate([kh, vh, np.zeros((P, 512), np.float32)], 1))
    for w4 in range(2):
        add(uv[:, w4 * 4:w4 * 4 + 4].reshape(2, P, 4 * P).transpose(1, 0, 2).reshape(P, BLOCK))
    merge("a")
    add(tiles(a["w_mem_k"].reshape(D_MODEL, -1)))
    mv = a["w_mem_v"].reshape(4, 2, P, 2, 512)
    add(mv.transpose(3, 0, 2, 1, 4).reshape(8, P, BLOCK))
    add(tiles(mq))
    merge("m")
    add(tiles(a["w_out"])); add(tiles(a["w_up"])); add(tiles(a["w_down"]))
    assert len(blocks) == sum(n * b for _, n, b in PHASES)
    x = np.concatenate([a["x_prompt"][0], a["x_sample"].reshape(NS, D_MODEL)])
    x_t = x.T.reshape(KC, P, T).transpose(1, 0, 2)
    vec = np.zeros((P, VW), np.float32)
    def put(name, v):
        at, n = _V[name]
        vec[:v.shape[0], at:at + n] = v.reshape(v.shape[0], n)
    cols = lambda v: v.reshape(-1, P).T
    put("qg", cols(a["q_norm_g"])); put("kvg", cols(a["kv_norm_g"]))
    cw = a["conv_w"].reshape(CONV_W, NC, P)[:, order]
    put("convw", cw.transpose(2, 1, 0)); put("convb", a["conv_b"].reshape(NC, P)[order].T)
    put("dskip", cols(np.repeat(a["d_skip"], HEAD_DIM))); put("ssmg", cols(a["ssm_norm_g"]))
    for n, m in (("bgate", "b_gate"), ("ln1g", "ln1_g"), ("ln1b", "ln1_b"), ("bup", "b_up"), ("bdown", "b_down"),
                 ("ln2g", "ln2_g"), ("ln2b", "ln2_b")):
        put(n, cols(a[m]))
    put("dtb", a["dt_bias"][:, None]); put("alog", a["a_log"][:, None])
    cs = a["state_conv"].reshape(DEC_BATCH, 3, NC, P)[:, :, order].transpose(3, 2, 0, 1)
    ss = a["state_ssm"].reshape(DEC_BATCH, GROUPS, GW, D_STATE).transpose(1, 3, 0, 2)
    ckv_rows = a["cache_ckv"]
    ckv_cols = ckv_rows.reshape(N_POOL, PAGE, 2, P).transpose(0, 3, 2, 1).reshape(N_POOL, P, KV_LORA)
    mem_t = a["mem_prompt"][0].T.reshape(KC, P, N_MEM).transpose(1, 0, 2)
    memk = a["cache_mem_k"].reshape(DEC_BATCH, N_MEM, 8, P).transpose(0, 3, 2, 1)
    memv = a["cache_mem_v"].reshape(DEC_BATCH, 2, P, 1024).transpose(0, 2, 1, 3)
    return dict(stream=np.stack(blocks), x_t=x_t, mem_t=mem_t, const=constants(), vec=vec, conv_state=cs, ssm_state=ss,
                pages=a["page_table"].reshape(1, -1).astype(np.int32), ckv_rows=ckv_rows, ckv_cols=ckv_cols,
                krope_cols=a["cache_krope"].transpose(0, 2, 1), memk_cols=memk, memv_rows=memv), order


def kernel(**inputs):
    import concourse.bacc as bacc
    from concourse import mybir
    from concourse.bass_utils import run_bass_kernel_spmd
    a = {k: np.asarray(v) for k, v in inputs.items()}
    ins, order = lay_out(a)
    nc = bacc.Bacc("TRN2", target_bir_lowering=False, num_devices=1)
    arrays, d = {}, {}
    for name, v in ins.items():
        v = np.ascontiguousarray(v)
        arrays["in_" + name] = v
        d[name] = nc.dram_tensor("in_" + name, v.shape, mybir.dt.from_np(v.dtype), kind="ExternalInput").ap()
    outs = {"y": (P, KC, T), "ckv": (P, 2, T), "krope": (ROPE, T), "mem_k": (P, 8, N_MEM), "mem_v": (P, 2, 1024),
            "ssm_p": (GROUPS, P, GW), "ssm_s": (GROUPS, P, DEC_BATCH, GW), "conv": (P, NC, 27)}
    o = {n: nc.dram_tensor("out_" + n, s, mybir.dt.float32, kind="ExternalOutput").ap() for n, s in outs.items()}
    program(nc, o=o, **d)
    r = run_bass_kernel_spmd(nc, [arrays], core_ids=[0]).results[0]
    back = np.argsort(order)
    def tokens(x):
        x = x.transpose(2, 1, 0).reshape(T, -1)
        return x[None, :SEQ], x[SEQ:].reshape(DEC_BATCH, DEC_SEQ, -1)
    y_p, y_s = tokens(r["out_y"])
    ckv_p, ckv_s = tokens(r["out_ckv"])
    kr_p, kr_s = tokens(r["out_krope"][:, None, :])
    mem_k = r["out_mem_k"].transpose(2, 1, 0).reshape(1, N_MEM, MEM_HEADS, MEM_DIM)
    mem_v = r["out_mem_v"].transpose(1, 0, 2).reshape(1, N_MEM, MEM_HEADS, MEM_DIM)
    ssm_p = r["out_ssm_p"].transpose(0, 2, 1).reshape(1, SSM_HEADS, HEAD_DIM, D_STATE)
    ssm_s = r["out_ssm_s"].transpose(2, 0, 3, 1).reshape(DEC_BATCH, SSM_HEADS, HEAD_DIM, D_STATE)
    conv = r["out_conv"][:, back]
    conv_p = conv[:, :, 0:3].transpose(2, 1, 0).reshape(1, 3, CONV_DIM)
    conv_s = conv[:, :, 3:].reshape(P, NC, DEC_BATCH, 3).transpose(2, 3, 1, 0).reshape(DEC_BATCH, 3, CONV_DIM)
    return (y_p, y_s, ckv_p, kr_p, mem_k, mem_v, ssm_p, conv_p, ckv_s, kr_s, ssm_s, conv_s)
```

```python
import numpy as np
from contextlib import ExitStack, contextmanager

P = 128
D_MODEL, SEQ, DEC_BATCH, DEC_SEQ = 1024, 512, 8, 4
PAGE, N_PAGES, N_POOL = 128, 16, 160
MLA_HEADS, Q_LORA, KV_LORA, NOPE, ROPE, V_DIM = 8, 384, 256, 128, 64, 128
SSM_HEADS, HEAD_DIM, GROUPS, D_STATE, CONV_W = 32, 64, 4, 128, 4
D_INNER = SSM_HEADS * HEAD_DIM
CONV_DIM = D_INNER + 2 * GROUPS * D_STATE
N_MEM, MEM_HEADS, MEM_DIM = 256, 4, 256
D_FF = 4 * D_MODEL
ALPHA = 2 ** 0.25
LN_EPS, RMS_EPS = 1e-5, 1e-6
THETA = 10000.0

NS = DEC_BATCH * DEC_SEQ
T = SEQ + NS
HT = T // 2
KC = D_MODEL // P
NB = SEQ // P
HG = SSM_HEADS // GROUPS
GW = HG * HEAD_DIM
GC = GW // P
QC = GC + 2
NC = CONV_DIM // P
EXT_P = CONV_W - 1 + SEQ
EXT_S = CONV_W - 1 + DEC_SEQ
EXT = EXT_P + DEC_BATCH * EXT_S
CL = EXT - (CONV_W - 1)
FC = D_FF // P
RING = 4
BLOCK = 1024
NEG = -1e30

_C = {}
def _const_layout():
    at = 0
    for name, n in (("ident", P), ("tri", P), ("last", P), ("ones", P), ("causal", P), ("fold", P),
                    ("tri_s", NS), ("last_s", NS), ("lastcol", DEC_BATCH), ("ofbatch", DEC_BATCH),
                    ("newmask", 2 * NS - DEC_SEQ), ("sel", HG * P), ("selpair", HG // 2 * P),
                    ("rope", T), ("scanmask", T), ("half", 1), ("bmask", DEC_BATCH * NS)):
        _C[name] = (at, n)
        at += n
    return at
CW = _const_layout()

_V = {}
def _vec_layout():
    at = 0
    for name, n in (("qg", Q_LORA // P), ("kvg", KV_LORA // P), ("convw", NC * CONV_W), ("convb", NC),
                    ("dskip", D_INNER // P), ("ssmg", D_INNER // P), ("bgate", 3 * KC), ("ln1g", KC),
                    ("ln1b", KC), ("bup", FC), ("bdown", KC), ("ln2g", KC), ("ln2b", KC), ("dtb", 1), ("alog", 1)):
        _V[name] = (at, n)
        at += n
    return at
VW = _vec_layout()


def constants():
    c = np.zeros((P, CW), np.float32)
    def put(name, a):
        at, n = _C[name]
        c[:a.shape[0], at:at + n] = a.reshape(a.shape[0], n)
    r = np.arange(P)
    put("ident", np.eye(P))
    put("tri", (r[:, None] <= r[None, :]) * 1.0)
    last = np.zeros((P, P)); last[P - 1] = 1
    put("last", last)
    put("ones", np.ones((P, P)))
    put("causal", np.where(r[None, :] <= r[:, None], 0.0, NEG))
    put("fold", np.tile(np.eye(ROPE), (2, 2)))
    s = np.arange(NS)
    sb, st = s // DEC_SEQ, s % DEC_SEQ
    same = sb[:, None] == sb[None, :]
    put("tri_s", (same & (s[:, None] <= s[None, :])) * 1.0)
    put("last_s", (same & (st[:, None] == DEC_SEQ - 1)) * 1.0)
    b = np.arange(DEC_BATCH)
    put("lastcol", ((sb[:, None] == b) & (st[:, None] == DEC_SEQ - 1)) * 1.0)
    put("ofbatch", (sb[:, None] == b) * 1.0)
    rt, col = np.arange(NS) % DEC_SEQ, np.arange(2 * NS - DEC_SEQ) - (NS - DEC_SEQ)
    nm = np.where((col[None] >= 0) & (col[None] <= rt[:, None]), 0.0, NEG)
    put("newmask", nm)
    sel = np.zeros((HG, HG, P)); pair = np.zeros((HG, HG // 2, P))
    for h in range(HG):
        sel[h, h] = 1
        pair[h, h // 2, HEAD_DIM * (h % 2):HEAD_DIM * (h % 2 + 1)] = 1
    put("sel", sel)
    put("selpair", pair)
    half = ROPE // 2
    pos = np.concatenate([np.arange(SEQ), np.tile(N_PAGES * PAGE + np.arange(DEC_SEQ), DEC_BATCH)])
    inv = (np.float32(THETA) ** (-np.arange(half, dtype=np.float32) / half)).astype(np.float32)
    ang = (inv[:, None] * pos.astype(np.float32)[None, :]).astype(np.float32).astype(np.float64)
    cos, sin = np.cos(ang), np.sin(ang)
    put("rope", np.concatenate([cos, cos, -sin, sin], 0))
    m = np.ones((P, T))
    m[:, 0:SEQ:P] = 0
    m[:, SEQ::DEC_SEQ] = 0
    put("scanmask", m)
    put("bmask", np.broadcast_to((sb[None, None, :] == b[None, :, None]) * 1.0, (P, DEC_BATCH, NS)))
    put("half", np.full((P, 1), 0.5))
    return c


class Count:
    def __init__(self, sem, start=0):
        self.sem, self.base, self.k, self.i, self.per = sem, start, 0, None, 0

    def next(self, n=1):
        self.k += n
        return self.value()

    def value(self):
        return self.base + self.k if self.i is None or self.per == 0 else self.i * self.per + (self.base + self.k)

    def enter(self, i, per):
        self.base, self.k, self.i, self.per = self.base + self.k, 0, i, per

    def leave(self, trips):
        assert self.k == self.per, f"{self.sem} counts {self.k} a turn, not {self.per}"
        self.base, self.k, self.i, self.per = self.base + trips * self.per, 0, None, 0


@contextmanager
def turns(engine, trips, counts, per, name):
    with engine.Fori(0, trips) as i:
        for c in counts:
            c.enter(i, per.get(c.sem.name, 0))
        yield i
        found = {c.sem.name: c.k for c in counts if c.k}
        assert found == per, f"signals a turn of {name}: {found}"
    for c in counts:
        c.k = c.per
        c.leave(trips)


def v2(ap):
    return ap.rearrange("p (a n) -> p a n", a=2)

WORK = 24704
KEYS_W = KV_LORA + PAGE * ROPE // P
STAGES = ["dt", "ssm", "mla", "merge_b", "merge_a", "mem", "merge_m"]
PHASES = [("dt", 1, 1), ("ssm", GROUPS, QC + GC), ("latents", 1, 6), ("heads", MLA_HEADS, 2), ("merge_b", KC, 3),
          ("values", 1, 2), ("merge_a", KC, 2), ("mem_k", 4, 2), ("mem_v", 1, 8), ("mq", MEM_HEADS, 2),
          ("merge_m", KC, 2), ("out", KC // 4, 4), ("up0", FC // 8, 4), ("down0", KC // 2, 4), ("up1", FC // 8, 4),
          ("down1", KC // 2, 4)]
START = {}
for _i, (_n, _t, _p) in enumerate(PHASES):
    START[_n] = 0 if _i == 0 else (START[PHASES[_i - 1][0]] + PHASES[_i - 1][2]) % RING

def loaded_before(name, slot):
    n = 0
    for part, trips, per in PHASES:
        if part == name:
            return n
        n += trips * sum((START[part] + b) % RING == slot for b in range(per))

CREDIT = {"acc0_free": 1, "acc1_free": 1, "blocks_begun": 8, "states_stored": 32, "keys_used": 4,
          "rows_used": 4, "split_begun": 1}
SEMAPHORES = ["pool_step", "pe_step", "act_step", "dve_step", "const_loaded", "x_loaded", "vec_loaded", "conv_state_loaded",
              "weights_in_slot0", "weights_in_slot1", "weights_in_slot2", "weights_in_slot3", "blocks_begun",
              "acc0_ready", "acc1_ready", "acc0_free", "acc1_free", "stage_over", "stored",
              "dt_ready", "dt_turned", "cum_ready", "last_ready", "dt_v", "dt_u", "dt_w", "dt_ln", "cum_rows_ready",
              "cum_g_loaded", "wb_ready", "dec_ready",
              "conv_done", "conv_ready", "silu_ready", "x_turned", "turned_read", "b_turned", "b_tm_read", "b_tm_ready",
              "cb_ready", "cb_read", "add_ready", "add_read", "cum_s_ready", "states_loaded", "states_stored",
              "cum_spread", "pair_read", "decay_ready", "y_ready", "sq_ready", "sq_summed", "adds_ready", "adds_read",
              "var_ready", "std_ready", "e_pair_ready", "seg_ready", "seg_exp", "z_ready", "y_gated", "states_done",
              "gate_bias_ready", "gate_ready", "page_ids_loaded", "act_over", "squares_ready", "cq_summed", "ckv_summed",
              "kr_ready", "kr_folded", "krope_ready", "latents_ready", "new_turned", "new_read", "head_read",
              "q_lat_ready", "q_lat_read", "k_ready", "v_ready", "kv_read", "prob_ready", "prob_turned", "scores_ready",
              "exp_ready", "turned_out", "head_out", "max_ready", "lat_ready", "lat_read", "lat_turned", "o_lat_ready",
              "sample_out", "batch_q_ready", "keys_used", "rows_used"]
SEMAPHORES += [f"{n}_in_slot{i}" for n in ("keys", "rows") for i in range(4)]
SEMAPHORES += [f"mem_{n}{i}_loaded" for n in "kv" for i in range(2)]
SEMAPHORES += ["mem_loaded", "mem_kv_ready", "kv_head_ready", "q_b_ready", "norm_in", "sums_ready", "norm_summed",
               "centred", "normed", "hidden_ready", "hi_ready", "split_ready", "split_begun", "scaled", "biased", "z_gated", "o_m_ready"]
PER = {
    "split_out_pool": {"blocks_begun": 4, "hi_ready": 4, "split_ready": 4},
    "split_rest_pool": {"blocks_begun": 4, "hi_ready": 4, "split_ready": 4},
    "ssm_act": {"act_step": 35, "acc0_ready": 5, "acc1_ready": 5, "acc0_free": 5, "acc1_free": 5, "conv_done":
        6, "conv_ready": 6, "silu_ready": 6, "b_turned": 1, "b_tm_read": 1, "states_stored": 32, "cum_spread":
        4, "pair_read": 4, "sq_ready": 4, "sq_summed": 4, "var_ready": 1, "std_ready": 1, "e_pair_ready": 4,
        "seg_ready": 8, "seg_exp": 8, "z_ready": 4, "y_gated": 4, "states_done": 1, "z_gated": 4},
    "heads_act": {"acc0_ready": 1, "acc0_free": 1, "k_ready": 1, "v_ready": 1, "kv_read": 2, "prob_turned": 4,
        "exp_ready": 4, "turned_out": 4, "max_ready": 4},
    "merge_b_act": {"act_step": 4, "acc0_ready": 2, "acc0_free": 2, "gate_bias_ready": 1, "gate_ready": 1,
        "prob_turned": 1, "exp_ready": 1, "turned_out": 2, "max_ready": 1},
    "merge_a_act": {"acc0_ready": 1, "acc0_free": 1, "gate_bias_ready": 1, "gate_ready": 1},
    "mem_heads_act": {"acc0_ready": 1, "acc1_ready": 1, "acc0_free": 1, "acc1_free": 1, "prob_turned": 4,
        "exp_ready": 4, "turned_out": 4, "max_ready": 4},
    "merge_m_act": {"acc0_ready": 1, "acc0_free": 1, "gate_bias_ready": 1, "gate_ready": 1},
    "split_out_act": {"weights_in_slot0": 16, "weights_in_slot1": 16, "weights_in_slot2": 16,
        "weights_in_slot3": 16, "hi_ready": 4, "split_begun": 4},
    "split_rest_act": {"weights_in_slot0": 16, "weights_in_slot1": 16, "weights_in_slot2": 16,
        "weights_in_slot3": 16, "hi_ready": 4, "split_begun": 4},
    "ssm_dve": {"dve_step": 127, "acc0_free": 5, "acc1_free": 5, "conv_done": 6, "conv_ready": 6, "silu_ready":
        6, "x_turned": 5, "turned_read": 5, "b_tm_read": 1, "b_tm_ready": 1, "cb_ready": 1, "cb_read": 1,
        "add_ready": 4, "add_read": 4, "cum_s_ready": 1, "states_stored": 32, "cum_spread": 4, "pair_read": 4,
        "decay_ready": 4, "y_ready": 4, "sq_summed": 4, "adds_ready": 8, "adds_read": 8, "var_ready": 1,
        "std_ready": 1, "e_pair_ready": 4, "seg_ready": 8, "seg_exp": 8, "z_ready": 4, "y_gated": 4,
        "states_done": 1, "z_gated": 4},
    "heads_dve": {"dve_step": 14, "acc1_ready": 1, "acc1_free": 1, "head_read": 1, "q_lat_ready": 1,
        "q_lat_read": 1, "prob_ready": 4, "scores_ready": 4, "exp_ready": 4, "head_out": 1, "max_ready": 4},
    "merge_b_dve": {"dve_step": 12, "acc0_ready": 2, "acc1_ready": 1, "acc0_free": 2, "acc1_free": 1,
        "gate_bias_ready": 1, "gate_ready": 1, "exp_ready": 1, "max_ready": 1, "lat_ready": 1, "lat_read": 1,
        "lat_turned": 1, "o_lat_ready": 1, "batch_q_ready": 1},
    "merge_a_dve": {"dve_step": 1, "acc1_ready": 1, "acc1_free": 1, "gate_bias_ready": 1, "gate_ready": 1},
    "mem_k_dve": {"acc0_ready": 1, "acc1_ready": 1, "acc0_free": 1, "acc1_free": 1},
    "mem_heads_dve": {"dve_step": 11, "acc0_free": 1, "acc1_free": 1, "head_read": 1, "prob_ready": 4,
        "scores_ready": 4, "exp_ready": 4, "head_out": 1, "max_ready": 4, "kv_head_ready": 1},
    "sample_m_dve": {"dve_step": 2, "scores_ready": 2, "q_b_ready": 2},
    "sample_mv_dve": {"dve_step": 2, "head_out": 2, "q_b_ready": 2},
    "merge_m_dve": {"dve_step": 3, "acc1_ready": 1, "acc1_free": 1, "gate_bias_ready": 1, "gate_ready": 1},
    "out_dve": {"acc0_ready": 2, "acc1_ready": 2, "acc0_free": 2, "acc1_free": 2},
    "up_dve": {"dve_step": 12, "acc0_ready": 2, "acc1_ready": 2, "acc0_free": 2, "acc1_free": 2},
    "down0_dve": {"dve_step": 2, "acc0_ready": 1, "acc1_ready": 1, "acc0_free": 1, "acc1_free": 1},
    "down1_dve": {"acc0_ready": 1, "acc1_ready": 1, "acc0_free": 1, "acc1_free": 1},
    "ssm_pe": {"weights_in_slot0": 32, "weights_in_slot1": 48, "weights_in_slot2": 48, "weights_in_slot3": 32,
        "acc0_free": 5, "acc1_free": 5, "conv_ready": 6, "turned_read": 5, "b_tm_ready": 1, "cb_read": 1,
        "add_read": 4, "cum_s_ready": 1, "states_loaded": 16, "pair_read": 4, "decay_ready": 4, "sq_ready": 4,
        "adds_read": 8, "var_ready": 1, "seg_ready": 8},
    "heads_pe": {"weights_in_slot1": 16, "weights_in_slot2": 16, "acc0_free": 1, "acc1_free": 1, "head_read": 1,
        "q_lat_read": 1, "kv_read": 2, "prob_ready": 4, "exp_ready": 4, "turned_out": 4},
    "merge_b_pe": {"weights_in_slot0": 16, "weights_in_slot1": 16, "weights_in_slot3": 16, "acc0_free": 2,
        "acc1_free": 1, "exp_ready": 1, "turned_out": 2, "lat_read": 1, "o_lat_ready": 1, "batch_q_ready": 1,
        "keys_in_slot0": 64, "keys_in_slot1": 64, "keys_in_slot2": 64, "keys_in_slot3": 64, "rows_in_slot0": 64,
        "rows_in_slot1": 64, "rows_in_slot2": 64, "rows_in_slot3": 64},
    "merge_a_pe": {"weights_in_slot0": 16, "weights_in_slot1": 16, "acc0_free": 1, "acc1_free": 1},
    "mem_k_pe": {"weights_in_slot2": 16, "weights_in_slot3": 16, "acc0_free": 1, "acc1_free": 1},
    "mem_heads_pe": {"weights_in_slot0": 16, "weights_in_slot1": 16, "acc0_free": 1, "acc1_free": 1,
        "head_read": 1, "prob_ready": 4, "exp_ready": 4, "turned_out": 4, "kv_head_ready": 1},
    "sample_m_pe": {"mem_k0_loaded": 16, "mem_k1_loaded": 16, "q_b_ready": 2},
    "sample_mv_pe": {"mem_v0_loaded": 16, "mem_v1_loaded": 16, "q_b_ready": 2},
    "merge_m_pe": {"weights_in_slot2": 16, "weights_in_slot3": 16, "acc0_free": 1, "acc1_free": 1},
    "out_pe": {"acc0_free": 2, "acc1_free": 2, "split_ready": 4},
    "up_pe": {"acc0_free": 2, "acc1_free": 2, "split_ready": 4},
    "down_pe": {"acc0_free": 1, "acc1_free": 1, "split_ready": 4},
}


def program(nc, stream, x_t, mem_t, const, vec, conv_state, ssm_state, pages, ckv_rows, page_cols,
            memk_cols, memv_rows, o):
    from concourse import mybir
    import concourse.bass as bass
    F, R, I32 = mybir.dt.float32, mybir.dt.float32r, mybir.dt.int32
    ACT, ALU, AX = mybir.ActivationFunctionType, mybir.AluOpType, mybir.AxisListType
    MUL, ADD, SUB, MAX, MIN = ALU.mult, ALU.add, ALU.subtract, ALU.max, ALU.min

    with ExitStack() as ctx:
        def sb(name, cols, dt=F, rows=P):
            return ctx.enter_context(nc.sbuf_tensor(name, [rows, cols], dt))

        ring = sb("ring", RING * BLOCK)
        cst = sb("cst", CW)
        vecs = sb("vecs", VW)
        xt = sb("xt", KC * T)
        mark = sb("mark", 2, F, 1)
        act_mark = sb("act_mark", 2, F, 1)
        grant = sb("grant", 8, F, 1)
        page_ids = sb("page_ids", DEC_BATCH * N_PAGES, I32, 1)
        with ExitStack() as until_merged:
            def early(name, cols):
                return until_merged.enter_context(nc.sbuf_tensor(name, [P, cols], F))
            branch = early("branch", D_INNER // P * T)
            attended = early("attended", KC * T)
            work = early("work", WORK)
        x_parts = sb("x_parts", 2 * KC * T, R)
        mg_parts = sb("mg_parts", KC * T, R)
        f_parts = sb("f_parts", 2 * FC // 2 * T + 4 * BLOCK, R)

        acc = [ctx.enter_context(nc.psum_tensor(f"acc{a}", [P, 2, 512], F)) for a in range(2)]
        bank = [ctx.enter_context(nc.psum_tensor(f"bank{a}", [P, 512], F)) for a in range(4)]

        def C(name):
            at, n = _C[name]
            return cst[:, at:at + n]

        def V(name, j=0):
            at, n = _V[name]
            return vecs[:, at + j:at + j + 1]

        def chunks(tensor, n):
            return tensor[:, 0:n * T].rearrange("p (c t) -> p c t", t=T)

        X, BR, AT = chunks(xt, KC), chunks(branch, D_INNER // P), chunks(attended, KC)

        class Carver:
            def __init__(self, tensor=work, cols=WORK):
                self.tensor, self.at, self.cols = tensor, 0, cols

            def __call__(self, cols, rows=P):
                a = self.tensor[0:rows, self.at:self.at + cols]
                self.at += cols
                assert self.at <= self.cols, self.at
                return a

        sem = {name: ctx.enter_context(nc.semaphore(name)) for name in SEMAPHORES}

        class Counts:
            def __init__(self, engine, given):
                self.engine = engine
                self.of = {n: Count(sem[n], given.get(n, 0)) for n in SEMAPHORES}

            def next(self, name, n=1):
                return self.of[name].next(n)

            def value(self, name):
                return self.of[name].value()

            def skip(self, name, n=1):
                self.of[name].next(n)

            def loop(self, name, trips):
                return turns(self.engine, trips, list(self.of.values()), PER.get(name, {}), name)

        def accv(p, rows=P):
            return acc[p][0:rows, :, 0:HT]

        k = Carver()
        dt_tm, cum_tm, wb_tm = (k((NB + 1) * SSM_HEADS).rearrange("p (c h) -> p c h", h=SSM_HEADS) for _ in range(3))
        dec_p = k(NB * SSM_HEADS).rearrange("p (c h) -> p c h", h=SSM_HEADS)
        dec_s = k(DEC_BATCH * SSM_HEADS).rearrange("p (b h) -> p b h", h=SSM_HEADS)
        cum_g = k(GROUPS * T, HG).rearrange("p (g t) -> p g t", t=T)
        st_conv = k(NC * DEC_BATCH * 3).rearrange("p (c b t) -> p c b t", b=DEC_BATCH, t=3)
        conv_out = k(NC * 27).rearrange("p (c n) -> p c n", n=27)
        after_dt = k.at
        dtw = {n: k(T, SSM_HEADS) for n in ("v", "abs", "u", "w", "d", "e", "ln", "dt", "dta", "cum", "r")}
        na = k(2, SSM_HEADS)
        cum_last = k(DEC_BATCH * SSM_HEADS, NS).rearrange("p (b h) -> p b h", h=SSM_HEADS)
        ident32 = cst[0:SSM_HEADS, _C["ident"][0]:_C["ident"][0] + SSM_HEADS]

        def blocks_of(row):
            return [row[:, c * P:(c + 1) * P] if c < NB else row[:, SEQ:T] for c in range(NB + 1)]

        k = Carver()
        k.at = after_dt
        fm = k(QC * T).rearrange("p (q t) -> p q t", t=T)
        ext = [k(EXT) for _ in range(2)]
        cacc = [k(CL) for _ in range(2)]
        sq = [a[:, 0:T] for a in cacc] + [a[:, 3:3 + T] for a in ext]
        th = [k(CL) for _ in range(2)]
        cum_s = k(T, HG)
        xdt = k((NB + 1) * GW).rearrange("p (c n) -> p c n", n=GW)
        xw = k((NB + 1) * GW).rearrange("p (c n) -> p c n", n=GW)
        b_tm = k(NB * P).rearrange("p (c n) -> p c n", n=P)
        b_s = k(P, NS)
        b_mask = k(DEC_BATCH * P, NS).rearrange("p (b n) -> p b n", n=P)
        cb_p = k(NB * P).rearrange("p (c n) -> p c n", n=P)
        cb_s = k(NS, NS)
        st_p = k(NB * GW).rearrange("p (c n) -> p c n", n=GW)
        st_s = attended[:, 0:DEC_BATCH * GW].rearrange("p (b n) -> p b n", n=GW)
        dec = [k(T) for _ in range(2)]
        e_pair = [k(T), cacc[0][:, 0:T]]
        t1 = k(T)
        rstd = k(T)
        zc = [k(T) for _ in range(2)] + [a[:, 3:3 + T] for a in ext]
        zth = [a[:, 0:T] for a in th]
        decays = [dec, zth]

        def ext_s(j):
            return ext[j][:, EXT_P:EXT].rearrange("p (b t) -> p b t", t=EXT_S)

        def conv_p(a):
            return a[:, 0:SEQ]

        def heads(a, c, g, rows):
            s = a[0:rows, c, bass.ds(g * HG, HG)]
            return s.rearrange("p (h o) -> p h o", o=1).broadcast_to([rows, HG, HEAD_DIM])

        def by_head(ap):
            return ap.rearrange("p (h d) -> p h d", d=HEAD_DIM)

        def rows_of(c):
            return P if c < NB else NS

        def toks(row, c):
            return row[:, c * P:(c + 1) * P] if c < NB else row[:, SEQ:T]

        k = Carver()
        k.at = WORK - (KC + 2) * T - 1
        gate_bias, gate, product = k(1), k(T), k(T)
        MG = k(KC * T).rearrange("p (c t) -> p c t", t=T)
        MG_H, MG_L = chunks(mg_parts, KC), chunks(x_parts, 2 * KC)[:, KC:2 * KC, :]

        k = Carver()
        ckv = k(2 * T).rearrange("p (c t) -> p c t", t=T)
        krope = k(T)
        q_lat = k(2 * (DEC_BATCH + 1) * NS).rearrange("p (c b h t) -> p c b h t", b=DEC_BATCH + 1, h=MLA_HEADS, t=DEC_SEQ)
        q_rot = k((DEC_BATCH + 1) * NS).rearrange("p (b h t) -> p b h t", h=MLA_HEADS, t=DEC_SEQ)
        ckv_new = k(KV_LORA, NS)
        o_lat_t = k(2 * MLA_HEADS * NS).rearrange("p (c h t) -> p c h t", h=MLA_HEADS, t=NS)
        keys = [k(4 * KEYS_W) for _ in range(4)]
        rows = [k(4 * KV_LORA) for _ in range(4)]
        for_heads = k.at
        cq = k(3 * T).rearrange("p (c t) -> p c t", t=T)
        a_rstd = k(T)
        a_sq = [k(T) for _ in range(5)]
        q_n, q_r = k(T), k(T)
        k_n = k(SEQ)
        v_tm = k(SEQ).rearrange("p (b v) -> p b v", v=P)
        prob = [k(SEQ) for _ in range(2)]
        prob_t = k(NB * SEQ).rearrange("p (b q) -> p b q", q=SEQ)
        stats = [k(4) for _ in range(2)]
        k.at = for_heads
        s_prob = k(N_PAGES * PAGE + NS, NS)
        s_prob_t = k(N_PAGES * NS).rearrange("p (g n) -> p g n", n=NS)
        s_prob_n = k(NS, NS)
        s_new = k(NS, NS)
        s_stat = k(16, NS)
        o_lat = k(KV_LORA, NS)
        q_lat_b = k(2 * NS).rearrange("p (c n) -> p c n", c=2)
        q_rot_b = k(2 * NS).rearrange("p (h n) -> p h n", h=2)
        A_SCALE = (NOPE + ROPE) ** -0.5

        k = Carver()
        mem = k(KC * N_MEM).rearrange("p (c m) -> p c m", m=N_MEM)
        mk = k(8 * N_MEM).rearrange("p (c m) -> p c m", m=N_MEM)
        mv = k(2 * 1024).rearrange("p (b e) -> p b e", b=2)
        q_h = k(2 * T).rearrange("p (c t) -> p c t", t=T)
        k_h = k(2 * N_MEM).rearrange("p (c m) -> p c m", m=N_MEM)
        v_h = k(2 * MEM_DIM).rearrange("p (b e) -> p b e", b=2)
        m_prob = [k(N_MEM) for _ in range(2)]
        m_prob_t = k(2 * SEQ).rearrange("p (b q) -> p b q", q=SEQ)
        m_stats = [k(4) for _ in range(2)]
        mq_s = k(8 * NS).rearrange("p (c t) -> p c t", t=NS)
        q_b = [k(8 * NS).rearrange("p (c t) -> p c t", t=NS) for _ in range(2)]
        m_scores = k(N_MEM)
        o_m = m_prob[0]
        ms_prob_t = k(2 * P).rearrange("p (b n) -> p b n", b=2)
        mem_k = [k(8 * N_MEM).rearrange("p (c m) -> p c m", m=N_MEM) for _ in range(2)]
        mem_v = [k(2 * 1024).rearrange("p (b e) -> p b e", b=2) for _ in range(2)]
        M_SCALE = MEM_DIM ** -0.5

        k = Carver(f_parts, 2 * FC // 2 * T + 4 * BLOCK)
        HALF_F = FC // 2
        hid_h, hid_l = (k(HALF_F * T).rearrange("p (c t) -> p c t", t=T) for _ in range(2))
        split = [[k(BLOCK) for _ in range(2)] for _ in range(2)]
        X_H, X_L = chunks(x_parts, 2 * KC)[:, 0:KC, :], chunks(x_parts, 2 * KC)[:, KC:2 * KC, :]
        k = Carver(attended, KC * T)
        mean, inv = k(T), k(T)
        relu, square = [k(T) for _ in range(2)], [k(T) for _ in range(2)]
        n_sq = chunks(work, KC)
        N_SPLIT = [t * per for name, t, per in PHASES if name in ("out", "up0", "down0", "up1", "down1")]

        block = ctx.enter_context(nc.Block())

        @block.gpsimd
        def _(pool):
            pool.memset(mark[0:1, 0:1], 0.0).then_inc(sem["acc0_free"], CREDIT["acc0_free"])
            pool.memset(act_mark[0:1, 0:1], 0.0).then_inc(sem["acc1_free"], CREDIT["acc1_free"])
            for i, name in enumerate(("blocks_begun", "states_stored", "keys_used", "rows_used",
                                     "split_begun")):
                pool.memset(grant[0:1, i:i + 1], 0.0).then_inc(sem[name], CREDIT[name])

            """The samples' pages, feature-major, a batch a turn, in 4 slots of 4 pages each."""
            pool.wait_ge(sem["page_ids_loaded"], 16)
            pool.wait_ge(sem["stage_over"], STAGES.index("ssm") + 1)
            with pool.Fori(0, DEC_BATCH) as b:
                for kq in range(4):
                    for i in range(4):
                        p = pool.value_load(page_ids[0:1, bass.ds(b * N_PAGES + (kq * 4 + i), 1)],
                                            min_val=0, max_val=N_POOL - 1)
                        if i == 0:
                            pool.wait_ge(sem["keys_used"], b * 4 + (kq + 1))
                        pool.dma_start(keys[kq][:, i * KEYS_W:(i + 1) * KEYS_W],
                                       page_cols[p]).then_inc(sem[f"keys_in_slot{kq}"], 16)

            t = Counts(pool, {})

            def split_block(i):
                s, j = (START["out"] + i) % RING, i % 2
                pool.wait_ge(sem["hi_ready"], t.next("hi_ready"))
                pool.tensor_tensor(split[j][1], ring[:, s * BLOCK:(s + 1) * BLOCK], split[j][0].bitcast(F),
                        SUB).then_inc(sem["split_ready"], 1)
                pool.wait_ge(sem["split_ready"], t.next("split_ready"))
                pool.tensor_tensor(grant[0:1, 7:8], grant[0:1, 0:1], grant[0:1, 0:1],
                        ADD).then_inc(sem["blocks_begun"], 1)
                pool.wait_ge(sem["blocks_begun"], t.next("blocks_begun"))
            pool.wait_ge(sem["stage_over"], t.next("stage_over", len(STAGES)))
            t.skip("blocks_begun", CREDIT["blocks_begun"] + sum(n * b for _, n, b in PHASES) - sum(N_SPLIT))
            pool.wait_ge(sem["blocks_begun"], CREDIT["blocks_begun"])
            for name, n in (("out", N_SPLIT[0]), ("rest", sum(N_SPLIT[1:]))):
                with t.loop(f"split_{name}_pool", n // 4):
                    for i in range(4):
                        split_block(i)

        @block.sync
        def _(sp):
            sp.dma_start(cst[:, :], const).then_inc(sem["const_loaded"], 16)
            sp.wait_ge(sem["page_ids_loaded"], 16)
            n, last = 0, {}
            for name, trips, per in PHASES:
                slots = [(START[name] + b) % RING for b in range(per)]

                def load(i, b):
                    s = slots[b]
                    before = [x for x in range(b) if slots[x] == s]
                    again = [x for x in range(per) if slots[x] == s][-1]
                    gaps = [b - before[-1]] if before else []
                    if not before and trips > 1:
                        gaps.append(per - again + b)
                    if not before and s in last:
                        gaps.append(n + b - last[s])
                    assert all(x >= 2 for x in gaps)
                    at = n + b if trips == 1 else i * per + (n + b)
                    if gaps:
                        sp.wait_ge(sem["blocks_begun"], at + (CREDIT["blocks_begun"] + 2 - min(gaps)))
                    sp.dma_start(ring[:, s * BLOCK:(s + 1) * BLOCK],
                            stream[at]).then_inc(sem[f"weights_in_slot{s}"], 16)

                if trips > 1:
                    with sp.Fori(0, trips) as i:
                        for b in range(per):
                            load(i, b)
                        if name == "merge_b":
                            for kq in range(4):
                                sp.wait_ge(sem["rows_used"], i * 4 + (kq + 1))
                                for g in range(4):
                                    page = sp.value_load(page_ids[0:1, bass.ds(i * N_PAGES + (kq * 4 + g), 1)],
                                                         min_val=0, max_val=N_POOL - 1)
                                    sp.dma_start(rows[kq][:, g * KV_LORA:(g + 1) * KV_LORA],
                                                 ckv_rows[page]).then_inc(sem[f"rows_in_slot{kq}"], 16)
                else:
                    for b in range(per):
                        load(0, b)
                for b in range(per):
                    last[slots[b]] = n + (trips - 1) * per + b
                n += trips * per
                if name == "mq":
                    sp.wait_ge(sem["stage_over"], STAGES.index("merge_a") + 1)
                    for j in range(2):
                        sp.dma_start(mem_k[j], memk_cols[j]).then_inc(sem[f"mem_k{j}_loaded"], 16)
                        sp.dma_start(mem_v[j], memv_rows[j]).then_inc(sem[f"mem_v{j}_loaded"], 16)
                    first = MLA_HEADS * NB + MEM_HEADS * NB
                    with sp.Fori(0, DEC_BATCH // 2 - 1) as i:
                        for j in range(2):
                            sp.wait_ge(sem["scores_ready"], 2 * i + (first + j + 1))
                            sp.dma_start(mem_k[j], memk_cols[2 * i + (2 + j)]).then_inc(sem[f"mem_k{j}_loaded"], 16)
                    first = MLA_HEADS + MEM_HEADS
                    with sp.Fori(0, DEC_BATCH // 2 - 1) as i:
                        for j in range(2):
                            sp.wait_ge(sem["head_out"], 2 * i + (first + j + 1))
                            sp.dma_start(mem_v[j], memv_rows[2 * i + (2 + j)]).then_inc(sem[f"mem_v{j}_loaded"], 16)

        @block.scalar
        def _(act):
            t = Counts(act, {"acc0_free": 1, "acc1_free": 1})
            act.dma_start(X, x_t).then_inc(sem["x_loaded"], 16)
            act.dma_start(vecs[:, :], vec).then_inc(sem["vec_loaded"], 16)
            act.dma_start(st_conv, conv_state).then_inc(sem["conv_state_loaded"], 16)
            act.dma_start(page_ids[:, :], pages).then_inc(sem["page_ids_loaded"], 16)
            act.wait_ge(sem["acc1_free"], 1)
            act.wait_ge(sem["vec_loaded"], 16)
            act.wait_ge(sem["const_loaded"], 16)

            def root(a):
                act.wait_ge(sem["var_ready"], t.next("var_ready"))
                act.activation(a, a, ACT.Sqrt).then_inc(sem["std_ready"], 1)
                act.wait_ge(sem["std_ready"], t.next("std_ready"))

            def norm(bias, out):
                act.wait_ge(sem["centred"], t.next("centred"))
                act.activation(n_sq, X, ACT.Square).then_inc(sem["norm_in"], 1)
                act.wait_ge(sem["norm_in"], t.next("norm_in"))
                root(inv)
                for c in range(KC):
                    act.wait_ge(sem["scaled"], t.next("scaled"))
                    act.activation(X[:, c, :], X[:, c, :], ACT.Identity, bias=V(bias, c)).then_inc(sem["biased"], 1)
                    act.wait_ge(sem["biased"], t.next("biased"))
                    if out:
                        act.dma_start(o["y"][:, c, :], X[:, c, :]).then_inc(sem["stored"], 16)
                    else:
                        act.activation(X_H[:, c, :], X[:, c, :], ACT.Copy).then_inc(sem["biased"], 1)
                        act.wait_ge(sem["biased"], t.next("biased"))

            def merge(name):
                act.wait_ge(sem["stage_over"], t.next("stage_over"))
                with t.loop(f"{name}_act", KC):
                    act.wait_ge(sem["gate_bias_ready"], t.next("gate_bias_ready"))
                    act.wait_ge(sem["acc0_ready"], t.next("acc0_ready"))
                    act.activation(v2(gate), accv(0), ACT.Tanh, scale=0.5, bias=gate_bias).then_inc(sem["acc0_free"], 1)
                    act.wait_ge(sem["acc0_free"], t.next("acc0_free"))
                    act.activation(gate, gate, ACT.Identity, scale=0.5, bias=C("half")).then_inc(sem["gate_ready"], 1)
                    act.wait_ge(sem["gate_ready"], t.next("gate_ready"))
                t.skip("acc1_ready", KC), t.skip("acc1_free", KC)

            def split_block(i):
                s, j = (START["out"] + i) % RING, i % 2
                act.wait_ge(sem["split_begun"], t.next("split_begun"))
                act.wait_ge(sem[f"weights_in_slot{s}"], t.next(f"weights_in_slot{s}", 16))
                act.activation(split[j][0], ring[:, s * BLOCK:(s + 1) * BLOCK], ACT.Copy).then_inc(sem["hi_ready"], 1)
                act.wait_ge(sem["hi_ready"], t.next("hi_ready"))

            t.skip("acc0_ready"), t.skip("acc0_free")
            act.wait_ge(sem["dt_v"], t.next("dt_v"))
            act.activation(dtw["u"], dtw["abs"], ACT.Exp, scale=-1.0).then_inc(sem["dt_u"], 1)
            act.wait_ge(sem["dt_u"], t.next("dt_u"))
            act.activation(na[:, 0:1], V("alog")[0:SSM_HEADS], ACT.Exp).then_inc(sem["dt_u"], 1)
            act.wait_ge(sem["dt_u"], t.next("dt_u"))
            act.wait_ge(sem["dt_w"], t.next("dt_w"))
            act.activation(dtw["ln"], dtw["w"], ACT.Ln).then_inc(sem["dt_ln"], 1)
            act.wait_ge(sem["dt_ln"], t.next("dt_ln"))
            for g in range(GROUPS):
                if g == 0:
                    act.wait_ge(sem["cum_rows_ready"], t.next("cum_rows_ready"))
                act.dma_start(cum_g[:, g, :], dtw["cum"][g * HG:(g + 1) * HG, :]).then_inc(sem["cum_g_loaded"], 16)
            act.wait_ge(sem["wb_ready"], t.next("wb_ready"))
            act.activation(wb_tm[:, 0:NB, :], wb_tm[:, 0:NB, :], ACT.Exp).then_inc(sem["act_step"], 1)
            act.wait_ge(sem["act_step"], t.next("act_step"))
            act.activation(wb_tm[0:NS, NB, :], wb_tm[0:NS, NB, :], ACT.Exp).then_inc(sem["act_step"], 1)
            act.wait_ge(sem["act_step"], t.next("act_step"))
            act.activation(dec_p, bank[2][:, 0:NB * SSM_HEADS].rearrange("p (c h) -> p c h", h=SSM_HEADS),
                    ACT.Exp).then_inc(sem["act_step"], 1)
            act.wait_ge(sem["act_step"], t.next("act_step"))
            act.activation(dec_s, bank[1][:, 0:DEC_BATCH * SSM_HEADS].rearrange("p (b h) -> p b h", h=SSM_HEADS),
                    ACT.Exp).then_inc(sem["dec_ready"], 1)
            act.wait_ge(sem["dec_ready"], t.next("dec_ready"))

            act.wait_ge(sem["stage_over"], t.next("stage_over"))
            with t.loop("ssm_act", GROUPS) as g:
                def evac(q):
                    j = q % 2
                    act.wait_ge(sem[f"acc{j}_ready"], t.next(f"acc{j}_ready"))
                    act.activation(ext[j][:, 3:3 + HT], acc[j][:, 0, 0:HT], ACT.Copy).then_inc(sem["act_step"], 1)
                    act.wait_ge(sem["act_step"], t.next("act_step"))
                    act.activation(ext[j][:, 3 + HT:EXT_P], acc[j][:, 1, 0:SEQ - HT],
                            ACT.Copy).then_inc(sem["act_step"], 1)
                    act.wait_ge(sem["act_step"], t.next("act_step"))
                    act.activation(ext_s(j)[:, :, 3:EXT_S], acc[j][:, 1, SEQ - HT:HT].rearrange("p (b t) -> p b t",
                            t=DEC_SEQ), ACT.Copy).then_inc(sem[f"acc{j}_free"], 1)
                    act.wait_ge(sem[f"acc{j}_free"], t.next(f"acc{j}_free"))

                def silu(q):
                    j = q % 2
                    act.wait_ge(sem["conv_done"], t.next("conv_done"))
                    act.activation(th[j], cacc[j], ACT.Tanh, scale=0.5).then_inc(sem["act_step"], 1)
                    act.wait_ge(sem["act_step"], t.next("act_step"))
                    act.activation(th[j], th[j], ACT.Identity, scale=0.5,
                            bias=C("half")).then_inc(sem["silu_ready"], 1)
                    act.wait_ge(sem["silu_ready"], t.next("silu_ready"))

                for q in range(QC):
                    evac(q)
                    if q == 1:
                        act.wait_ge(sem["states_stored"], t.next("states_stored", 32))
                        act.dma_start(st_s, ssm_state[g]).then_inc(sem["states_loaded"], 16)
                    if q >= 1:
                        silu(q - 1)
                silu(QC - 1)

                def z_read(hp):
                    j = hp % 2
                    if hp == 0:
                        act.wait_ge(sem["conv_ready"], t.next("conv_ready", QC))
                    if hp >= 2:
                        act.wait_ge(sem["z_gated"], t.next("z_gated"))
                    act.wait_ge(sem[f"acc{j}_ready"], t.next(f"acc{j}_ready"))
                    act.activation(v2(zth[j]), accv(j), ACT.Tanh, scale=0.5).then_inc(sem["act_step"], 1)
                    act.wait_ge(sem["act_step"], t.next("act_step"))
                    act.activation(v2(zc[hp]), accv(j), ACT.Copy).then_inc(sem[f"acc{j}_free"], 1)
                    act.wait_ge(sem[f"acc{j}_free"], t.next(f"acc{j}_free"))
                    act.activation(zth[j], zth[j], ACT.Identity, scale=0.5,
                            bias=C("half")).then_inc(sem["z_ready"], 1)
                    act.wait_ge(sem["z_ready"], t.next("z_ready"))

                z_read(0)
                act.wait_ge(sem["b_turned"], t.next("b_turned"))
                act.activation(b_tm, bank[2][:, :].rearrange("p (c n) -> p c n", n=P),
                        ACT.Copy).then_inc(sem["act_step"], 1)
                act.wait_ge(sem["act_step"], t.next("act_step"))
                act.activation(b_s, bank[3][0:NS, 0:P], ACT.Copy).then_inc(sem["b_tm_read"], 1)
                act.wait_ge(sem["b_tm_read"], t.next("b_tm_read"))
                for hp in range(1, GC):
                    z_read(hp)
                act.wait_ge(sem["z_gated"], t.next("z_gated", 2))
                for hp in range(GC):
                    if hp >= 2:
                        act.wait_ge(sem["pair_read"], t.next("pair_read"))
                    act.wait_ge(sem["cum_spread"], t.next("cum_spread"))
                    e, d = e_pair[hp % 2], decays[hp % 2]
                    act.activation(e[:, 0:SEQ], acc[0][:, 0, 0:SEQ], ACT.Exp).then_inc(sem["act_step"], 1)
                    act.wait_ge(sem["act_step"], t.next("act_step"))
                    act.activation(e[:, SEQ:T], acc[0][:, 1, 2 * NS:3 * NS], ACT.Exp).then_inc(sem["e_pair_ready"], 1)
                    act.wait_ge(sem["e_pair_ready"], t.next("e_pair_ready"))
                    for j in range(2):
                        act.wait_ge(sem["seg_ready"], t.next("seg_ready"))
                        act.activation(conv_p(d[j]), conv_p(d[j]), ACT.Exp).then_inc(sem["act_step"], 1)
                        act.wait_ge(sem["act_step"], t.next("act_step"))
                        act.activation(d[j][0:NS, SEQ:T], d[j][0:NS, SEQ:T], ACT.Exp).then_inc(sem["seg_exp"], 1)
                        act.wait_ge(sem["seg_exp"], t.next("seg_exp"))
                act.wait_ge(sem["pair_read"], t.next("pair_read", 2))
                act.wait_ge(sem["y_gated"], t.next("y_gated", GC))
                for hp in range(GC):
                    act.activation(sq[hp], fm[:, hp, :], ACT.Square).then_inc(sem["sq_ready"], 1)
                    act.wait_ge(sem["sq_ready"], t.next("sq_ready"))
                act.wait_ge(sem["var_ready"], t.next("var_ready"))
                act.activation(rstd, rstd, ACT.Sqrt).then_inc(sem["std_ready"], 1)
                act.wait_ge(sem["std_ready"], t.next("std_ready"))
                act.wait_ge(sem["states_done"], t.next("states_done"))
                act.dma_start(o["ssm_p"][g], st_p[:, NB - 1, :]).then_inc(sem["states_stored"], 16)
                act.dma_start(o["ssm_s"][g], st_s).then_inc(sem["states_stored"], 16)
                act.wait_ge(sem["sq_summed"], t.next("sq_summed", GC))
            act.wait_ge(sem["states_stored"], t.next("states_stored", 32))
            act.dma_start(o["conv"], conv_out).then_inc(sem["stored"], 16)
            act.wait_ge(sem["stored"], t.next("stored", 16))
            act.activation(act_mark[0:1, 1:2], act_mark[0:1, 0:1], ACT.Copy).then_inc(sem["act_over"], 1)
            act.wait_ge(sem["act_over"], t.next("act_over"))

            act.wait_ge(sem["stage_over"], t.next("stage_over"))
            for i in range(5):
                p = i % 2
                dst = cq[:, i, :] if i < 3 else ckv[:, i - 3, :]
                act.wait_ge(sem[f"acc{p}_ready"], t.next(f"acc{p}_ready"))
                act.activation(v2(dst), accv(p), ACT.Copy).then_inc(sem[f"acc{p}_free"], 1)
                act.wait_ge(sem[f"acc{p}_free"], t.next(f"acc{p}_free"))
                act.activation(a_sq[i], dst, ACT.Square).then_inc(sem["squares_ready"], 1)
                act.wait_ge(sem["squares_ready"], t.next("squares_ready"))
            t.skip("acc1_ready"), t.skip("acc1_free")
            root(a_rstd)
            act.wait_ge(sem["kr_folded"], t.next("kr_folded"))
            act.activation(krope[:, 0:HT], bank[0][:, 0:HT], ACT.Copy).then_inc(sem["act_step"], 1)
            act.wait_ge(sem["act_step"], t.next("act_step"))
            act.activation(krope[:, HT:T], bank[1][:, 0:HT], ACT.Copy).then_inc(sem["krope_ready"], 1)
            act.wait_ge(sem["krope_ready"], t.next("krope_ready"))
            root(a_rstd)
            act.wait_ge(sem["latents_ready"], t.next("latents_ready"))
            act.dma_start(o["ckv"], ckv).then_inc(sem["stored"], 16)
            act.dma_start(o["krope"], krope[0:ROPE, :]).then_inc(sem["stored"], 16)
            act.wait_ge(sem["new_turned"], t.next("new_turned"))
            act.activation(ckv_new, bank[0][0:NS, 0:KV_LORA], ACT.Copy).then_inc(sem["new_read"], 1)
            act.wait_ge(sem["new_read"], t.next("new_read"))
            with t.loop("heads_act", MLA_HEADS):
                act.wait_ge(sem["acc0_ready"], t.next("acc0_ready"))
                act.activation(v2(q_n), accv(0), ACT.Copy).then_inc(sem["acc0_free"], 1)
                act.wait_ge(sem["acc0_free"], t.next("acc0_free"))
                act.wait_ge(sem["k_ready"], t.next("k_ready"))
                act.activation(k_n, bank[1][:, :], ACT.Copy).then_inc(sem["kv_read"], 1)
                act.wait_ge(sem["kv_read"], t.next("kv_read"))
                act.wait_ge(sem["v_ready"], t.next("v_ready"))
                act.activation(v_tm, bank[2][:, :].rearrange("p (b v) -> p b v", v=P),
                        ACT.Copy).then_inc(sem["kv_read"], 1)
                act.wait_ge(sem["kv_read"], t.next("kv_read"))

                def turned(qb):
                    act.wait_ge(sem["prob_turned"], t.next("prob_turned"))
                    n = (qb + 1) * P
                    act.activation(prob_t[:, 0:qb + 1, qb * P:n], bank[1 + qb % 2][:,
                            0:n].rearrange("p (b q) -> p b q", q=P), ACT.Copy).then_inc(sem["turned_out"], 1)
                    act.wait_ge(sem["turned_out"], t.next("turned_out"))

                for qb in range(NB):
                    n = (qb + 1) * P
                    act.wait_ge(sem["max_ready"], t.next("max_ready"))
                    act.activation(prob[qb % 2][:, 0:n], bank[3 * (qb % 2)][:, 0:n], ACT.Exp, scale=A_SCALE,
                            bias=stats[qb % 2][:, 1:2], accum_out=stats[qb % 2][:, 2:3]).then_inc(sem["exp_ready"], 1)
                    act.wait_ge(sem["exp_ready"], t.next("exp_ready"))
                    if qb >= 1:
                        turned(qb - 1)
                turned(NB - 1)
            t.skip("acc1_ready", MLA_HEADS), t.skip("acc1_free", MLA_HEADS)

            act.wait_ge(sem["stage_over"], t.next("stage_over"))
            with t.loop("merge_b_act", KC):
                t.skip("acc0_ready"), t.skip("acc0_free")
                for kq in range(4):
                    if kq == 0:
                        act.wait_ge(sem["max_ready"], t.next("max_ready"))
                    act.activation(s_prob[:, kq * 512:(kq + 1) * 512], bank[kq][0:NS, :], ACT.Exp, scale=A_SCALE,
                            bias=s_stat[:, 1:2], accum_out=s_stat[:, 8 + kq:9 + kq]).then_inc(sem["act_step"], 1)
                    act.wait_ge(sem["act_step"], t.next("act_step"))
                act.activation(s_prob[:, N_PAGES * PAGE:], s_new, ACT.Exp, scale=A_SCALE, bias=s_stat[:, 1:2],
                        accum_out=s_stat[:, 12:13]).then_inc(sem["exp_ready"], 1)
                act.wait_ge(sem["exp_ready"], t.next("exp_ready"))
                act.wait_ge(sem["prob_turned"], t.next("prob_turned"))
                act.activation(s_prob_t, bank[1][:, :].rearrange("p (g n) -> p g n", n=NS),
                        ACT.Copy).then_inc(sem["turned_out"], 1)
                act.wait_ge(sem["turned_out"], t.next("turned_out"))
                act.activation(s_prob_n, bank[2][0:NS, 0:NS], ACT.Copy).then_inc(sem["turned_out"], 1)
                act.wait_ge(sem["turned_out"], t.next("turned_out"))
                act.wait_ge(sem["gate_bias_ready"], t.next("gate_bias_ready"))
                act.wait_ge(sem["acc0_ready"], t.next("acc0_ready"))
                act.activation(v2(gate), accv(0), ACT.Tanh, scale=0.5, bias=gate_bias).then_inc(sem["acc0_free"], 1)
                act.wait_ge(sem["acc0_free"], t.next("acc0_free"))
                act.activation(gate, gate, ACT.Identity, scale=0.5, bias=C("half")).then_inc(sem["gate_ready"], 1)
                act.wait_ge(sem["gate_ready"], t.next("gate_ready"))
            t.skip("acc1_ready", KC), t.skip("acc1_free", KC)
            act.wait_ge(sem["stored"], t.next("stored", 32))
            act.activation(act_mark[0:1, 1:2], act_mark[0:1, 0:1], ACT.Copy).then_inc(sem["act_over"], 1)
            act.wait_ge(sem["act_over"], t.next("act_over"))

            merge("merge_a")

            act.wait_ge(sem["stage_over"], t.next("stage_over"))
            act.dma_start(mem, mem_t).then_inc(sem["mem_loaded"], 16)
            for j in range(2):
                t.skip(f"acc{j}_ready", 5), t.skip(f"acc{j}_free", 5)
            act.wait_ge(sem["mem_kv_ready"], t.next("mem_kv_ready"))
            act.dma_start(o["mem_k"], mk).then_inc(sem["stored"], 16)
            act.dma_start(o["mem_v"], mv).then_inc(sem["stored"], 16)
            with t.loop("mem_heads_act", MEM_HEADS):
                for p in range(2):
                    act.wait_ge(sem[f"acc{p}_ready"], t.next(f"acc{p}_ready"))
                    act.activation(v2(q_h[:, p, :]), accv(p), ACT.Copy).then_inc(sem[f"acc{p}_free"], 1)
                    act.wait_ge(sem[f"acc{p}_free"], t.next(f"acc{p}_free"))

                def turned(qb):
                    act.wait_ge(sem["prob_turned"], t.next("prob_turned"))
                    act.activation(m_prob_t[:, :, qb * P:(qb + 1) * P], bank[2 + qb % 2][:,
                            0:2 * P].rearrange("p (b q) -> p b q", q=P), ACT.Copy).then_inc(sem["turned_out"], 1)
                    act.wait_ge(sem["turned_out"], t.next("turned_out"))

                for qb in range(NB):
                    act.wait_ge(sem["max_ready"], t.next("max_ready"))
                    act.activation(m_prob[qb % 2], bank[qb % 2][:, 0:N_MEM], ACT.Exp, scale=M_SCALE,
                            bias=m_stats[qb % 2][:, 1:2], accum_out=m_stats[qb % 2][:,
                                    2:3]).then_inc(sem["exp_ready"], 1)
                    act.wait_ge(sem["exp_ready"], t.next("exp_ready"))
                    if qb >= 1:
                        turned(qb - 1)
                turned(NB - 1)
            act.wait_ge(sem["max_ready"], t.next("max_ready"))
            act.activation(m_scores, m_scores, ACT.Exp, scale=M_SCALE, bias=m_stats[0][:, 1:2],
                    accum_out=m_stats[0][:, 2:3]).then_inc(sem["exp_ready"], 1)
            act.wait_ge(sem["exp_ready"], t.next("exp_ready"))
            act.wait_ge(sem["prob_turned"], t.next("prob_turned"))
            act.activation(ms_prob_t, bank[2][:, 0:2 * P].rearrange("p (b n) -> p b n", b=2),
                    ACT.Copy).then_inc(sem["turned_out"], 1)
            act.wait_ge(sem["turned_out"], t.next("turned_out"))
            act.wait_ge(sem["stored"], t.next("stored", 32))
            act.activation(act_mark[0:1, 1:2], act_mark[0:1, 0:1], ACT.Copy).then_inc(sem["act_over"], 1)
            act.wait_ge(sem["act_over"], t.next("act_over"))

            merge("merge_m")

            act.wait_ge(sem["stage_over"], t.next("stage_over"))
            for s in range(RING):
                t.skip(f"weights_in_slot{s}", 16 * loaded_before("out", s))
            with t.loop("split_out_act", N_SPLIT[0] // 4):
                for i in range(4):
                    split_block(i)
            norm("ln1b", False)
            with t.loop("split_rest_act", sum(N_SPLIT[1:]) // 4):
                for i in range(4):
                    split_block(i)
            norm("ln2b", True)
            act.wait_ge(sem["stored"], t.next("stored", KC * 16))

        @block.vector
        def _(dve):
            t = Counts(dve, {"acc0_free": 1, "acc1_free": 1})
            dve.wait_ge(sem["vec_loaded"], 16)
            dve.wait_ge(sem["conv_state_loaded"], 16)
            dve.wait_ge(sem["acc0_free"], 1)

            def inv_std(out, summed, n, eps):
                dve.wait_ge(sem[summed], t.next(summed))
                for half in range(2):
                    signal = "var_ready" if half else "dve_step"
                    dve.tensor_scalar(out[:, half * HT:(half + 1) * HT], bank[2 + half][:, 0:HT], 1.0 / n, eps, MUL,
                            ADD).then_inc(sem[signal], 1)
                    dve.wait_ge(sem[signal], t.next(signal))
                dve.wait_ge(sem["std_ready"], t.next("std_ready"))
                dve.reciprocal(out, out).then_inc(sem["dve_step"], 1)
                dve.wait_ge(sem["dve_step"], t.next("dve_step"))

            def softmax(scores, stats, p, scale, scaled):
                dve.reduce_max(stats[:, 0:1], scores, AX.X).then_inc(sem["dve_step"], 1)
                dve.wait_ge(sem["dve_step"], t.next("dve_step"))
                dve.tensor_scalar(stats[:, 1:2], stats[:, 0:1], -scale, None, MUL).then_inc(sem["max_ready"], 1)
                dve.wait_ge(sem["max_ready"], t.next("max_ready"))
                dve.wait_ge(sem["exp_ready"], t.next("exp_ready"))
                dve.reciprocal(stats[:, 3:4], stats[:, 2:3]).then_inc(sem["dve_step"], 1)
                dve.wait_ge(sem["dve_step"], t.next("dve_step"))
                dve.tensor_scalar(p, p, stats[:, 3:4], None, MUL).then_inc(sem[scaled], 1)
                dve.wait_ge(sem[scaled], t.next(scaled))

            def norm(gain, out):
                dve.tensor_copy(mark[0:1, 1:2], mark[0:1, 0:1]).then_inc(sem["norm_in"], 1)
                dve.wait_ge(sem["norm_in"], t.next("norm_in"))
                dve.wait_ge(sem["sums_ready"], t.next("sums_ready"))
                for half in range(2):
                    dve.tensor_scalar(mean[:, half * HT:(half + 1) * HT], bank[half][:, 0:HT], 1.0 / D_MODEL, None,
                            MUL).then_inc(sem["dve_step"], 1)
                    dve.wait_ge(sem["dve_step"], t.next("dve_step"))
                dve.tensor_tensor(X, X, mean.rearrange("p (o t) -> p o t", o=1).broadcast_to([P, KC, T]),
                        SUB).then_inc(sem["centred"], 1)
                dve.wait_ge(sem["centred"], t.next("centred"))
                t.skip("norm_in")
                inv_std(inv, "norm_summed", D_MODEL, LN_EPS)
                for c in range(KC + 1):
                    if c < KC:
                        dve.scalar_tensor_tensor(out=X[:, c, :], in0=X[:, c, :], scalar=V(gain, c), in1=inv, op0=MUL,
                                op1=MUL).then_inc(sem["scaled"], 1)
                        dve.wait_ge(sem["scaled"], t.next("scaled"))
                    if c and not out:
                        dve.wait_ge(sem["biased"], t.next("biased", 2))
                        dve.tensor_tensor(X_L[:, c - 1, :], X[:, c - 1, :], X_H[:, c - 1, :].bitcast(F),
                                SUB).then_inc(sem["normed"], 1)
                        dve.wait_ge(sem["normed"], t.next("normed"))

            def merge(name, branch_i):
                with t.loop(f"{name}_dve", KC) as j:
                    dve.tensor_scalar(gate_bias, vecs[:, bass.ds(_V["bgate"][0] + branch_i * KC + j, 1)], 0.5, None,
                            MUL).then_inc(sem["gate_bias_ready"], 1)
                    dve.wait_ge(sem["gate_bias_ready"], t.next("gate_bias_ready"))
                    dve.wait_ge(sem["gate_ready"], t.next("gate_ready"))
                    dve.wait_ge(sem["acc1_ready"], t.next("acc1_ready"))
                    m = MG[:, bass.ds(j, 1), :].rearrange("p o t -> p (o t)")
                    dve.tensor_tensor(v2(product), v2(gate), accv(1), MUL).then_inc(sem["acc1_free"], 1)
                    dve.wait_ge(sem["acc1_free"], t.next("acc1_free"))
                    dve.tensor_tensor(m, m, product, ADD).then_inc(sem["dve_step"], 1)
                    dve.wait_ge(sem["dve_step"], t.next("dve_step"))
                    if name == "merge_m":
                        hi, lo = (a[:, bass.ds(j, 1), :].rearrange("p o t -> p (o t)") for a in (MG_H, MG_L))
                        dve.tensor_scalar(hi, m, 1.0, None, MUL).then_inc(sem["dve_step"], 1)
                        dve.wait_ge(sem["dve_step"], t.next("dve_step"))
                        dve.tensor_tensor(lo, m, hi.bitcast(F), SUB).then_inc(sem["dve_step"], 1)
                        dve.wait_ge(sem["dve_step"], t.next("dve_step"))
                t.skip("acc0_ready", KC), t.skip("acc0_free", KC)
                dve.tensor_copy(mark[0:1, 1:2], mark[0:1, 0:1]).then_inc(sem["stage_over"], 1)
                dve.wait_ge(sem["stage_over"], t.next("stage_over"))

            w = dtw
            dve.wait_ge(sem["const_loaded"], 16)
            dve.wait_ge(sem["acc0_ready"], t.next("acc0_ready"))
            dve.tensor_scalar(v2(w["v"]), accv(0, SSM_HEADS), V("dtb")[0:SSM_HEADS], None,
                    ADD).then_inc(sem["acc0_free"], 1)
            dve.wait_ge(sem["acc0_free"], t.next("acc0_free"))
            dve.scalar_tensor_tensor(out=w["abs"], in0=w["v"], scalar=-1.0, in1=w["v"], op0=MUL,
                    op1=MAX).then_inc(sem["dt_v"], 1)
            dve.wait_ge(sem["dt_v"], t.next("dt_v"))
            dve.wait_ge(sem["dt_u"], t.next("dt_u", 2))
            dve.tensor_scalar(w["w"], w["u"], 1.0, None, ADD).then_inc(sem["dt_w"], 1)
            dve.wait_ge(sem["dt_w"], t.next("dt_w"))
            dve.tensor_scalar(w["d"], w["w"], -1.0, None, ADD).then_inc(sem["dve_step"], 1)
            dve.wait_ge(sem["dve_step"], t.next("dve_step"))
            dve.tensor_scalar(w["e"], w["d"], 0.0, None, ALU.is_equal).then_inc(sem["dve_step"], 1)
            dve.wait_ge(sem["dve_step"], t.next("dve_step"))
            dve.tensor_tensor(w["d"], w["d"], w["e"], ADD).then_inc(sem["dve_step"], 1)
            dve.wait_ge(sem["dve_step"], t.next("dve_step"))
            dve.reciprocal(w["r"], w["d"]).then_inc(sem["dve_step"], 1)
            dve.wait_ge(sem["dve_step"], t.next("dve_step"))
            dve.tensor_tensor(w["r"], w["r"], w["u"], MUL).then_inc(sem["dve_step"], 1)
            dve.wait_ge(sem["dve_step"], t.next("dve_step"))
            dve.wait_ge(sem["dt_ln"], t.next("dt_ln"))
            dve.tensor_tensor(w["ln"], w["ln"], w["e"], ADD).then_inc(sem["dve_step"], 1)
            dve.wait_ge(sem["dve_step"], t.next("dve_step"))
            dve.tensor_tensor(w["r"], w["r"], w["ln"], MUL).then_inc(sem["dve_step"], 1)
            dve.wait_ge(sem["dve_step"], t.next("dve_step"))
            dve.tensor_scalar(w["dt"], w["v"], 0.0, None, MAX).then_inc(sem["dve_step"], 1)
            dve.wait_ge(sem["dve_step"], t.next("dve_step"))
            dve.tensor_tensor(w["dt"], w["dt"], w["r"], ADD).then_inc(sem["dve_step"], 1)
            dve.wait_ge(sem["dve_step"], t.next("dve_step"))
            dve.tensor_scalar(na[:, 1:2], na[:, 0:1], -1.0, None, MUL).then_inc(sem["dve_step"], 1)
            dve.wait_ge(sem["dve_step"], t.next("dve_step"))
            dve.tensor_scalar(w["dta"], w["dt"], na[:, 1:2], None, MUL).then_inc(sem["dve_step"], 1)
            dve.wait_ge(sem["dve_step"], t.next("dve_step"))
            dve.tensor_tensor_scan(w["cum"], C("scanmask")[0:SSM_HEADS, :], w["dta"], 0.0, MUL,
                    ADD).then_inc(sem["dt_ready"], 1)
            dve.wait_ge(sem["dt_ready"], t.next("dt_ready"))
            dve.tensor_copy(mark[0:1, 1:2], mark[0:1, 0:1]).then_inc(sem["cum_rows_ready"], 1)
            dve.wait_ge(sem["cum_rows_ready"], t.next("cum_rows_ready"))
            dve.wait_ge(sem["dt_turned"], t.next("dt_turned"))
            for j, out in enumerate((dt_tm, cum_tm)):
                dve.tensor_copy(out[:, 0:NB, :], bank[j][:, 0:NB * SSM_HEADS].rearrange("p (c h) -> p c h",
                        h=SSM_HEADS)).then_inc(sem["dve_step"], 1)
                dve.wait_ge(sem["dve_step"], t.next("dve_step"))
                dve.tensor_copy(out[0:NS, NB, :], bank[j][0:NS,
                        NB * SSM_HEADS:(NB + 1) * SSM_HEADS]).then_inc(sem["dve_step"], 1)
                dve.wait_ge(sem["dve_step"], t.next("dve_step"))
            dve.tensor_tensor(cum_last, cum_tm[0:NS, NB:NB + 1, :].broadcast_to([NS, DEC_BATCH, SSM_HEADS]),
                    C("lastcol")[0:NS, :].rearrange("p (b o) -> p b o", o=1).broadcast_to([NS, DEC_BATCH,
                            SSM_HEADS]), MUL).then_inc(sem["cum_ready"], 1)
            dve.wait_ge(sem["cum_ready"], t.next("cum_ready"))
            dve.wait_ge(sem["last_ready"], t.next("last_ready"))
            dve.tensor_tensor(wb_tm[:, 0:NB, :], bank[2][:, 0:NB * SSM_HEADS].rearrange("p (c h) -> p c h",
                    h=SSM_HEADS), cum_tm[:, 0:NB, :], SUB).then_inc(sem["dve_step"], 1)
            dve.wait_ge(sem["dve_step"], t.next("dve_step"))
            dve.tensor_tensor(wb_tm[0:NS, NB, :], bank[3][0:NS, 0:SSM_HEADS], cum_tm[0:NS, NB, :],
                    SUB).then_inc(sem["wb_ready"], 1)
            dve.wait_ge(sem["wb_ready"], t.next("wb_ready"))
            dve.wait_ge(sem["dec_ready"], t.next("dec_ready"))
            dve.tensor_tensor(wb_tm[:, 0:NB, :], wb_tm[:, 0:NB, :], dt_tm[:, 0:NB, :],
                    MUL).then_inc(sem["dve_step"], 1)
            dve.wait_ge(sem["dve_step"], t.next("dve_step"))
            dve.tensor_tensor(wb_tm[0:NS, NB, :], wb_tm[0:NS, NB, :], dt_tm[0:NS, NB, :],
                    MUL).then_inc(sem["dve_step"], 1)
            dve.wait_ge(sem["dve_step"], t.next("dve_step"))
            dve.wait_ge(sem["cum_g_loaded"], 16 * GROUPS)
            dve.tensor_copy(mark[0:1, 1:2], mark[0:1, 0:1]).then_inc(sem["stage_over"], 1)
            dve.wait_ge(sem["stage_over"], t.next("stage_over"))

            dve.wait_ge(sem["conv_state_loaded"], 16)
            for j in range(2):
                dve.memset(ext[j][:, 0:3], 0.0).then_inc(sem["dve_step"], 1)
                dve.wait_ge(sem["dve_step"], t.next("dve_step"))
            with t.loop("ssm_dve", GROUPS) as g:
                def finish(q):
                    j = q % 2
                    dve.wait_ge(sem["silu_ready"], t.next("silu_ready"))
                    dve.tensor_tensor(fm[:, q, 0:SEQ], conv_p(cacc[j]), conv_p(th[j]),
                            MUL).then_inc(sem["dve_step"], 1)
                    dve.wait_ge(sem["dve_step"], t.next("dve_step"))
                    a, b = (x[:, EXT_P:CL] for x in (cacc[j], th[j]))
                    n = (DEC_BATCH - 1) * EXT_S
                    for lo, hi in ((0, DEC_BATCH - 1), (DEC_BATCH - 1, DEC_BATCH)):
                        nb = hi - lo
                        pick = (lambda x: x[:, 0:n].rearrange("p (b t) -> p b t", t=EXT_S)[:, :,
                                0:DEC_SEQ]) if lo == 0 \
                            else (lambda x: x[:, n:n + DEC_SEQ].rearrange("p (b t) -> p b t", t=DEC_SEQ))
                        out = fm[:, q, SEQ + lo * DEC_SEQ:SEQ + hi * DEC_SEQ].rearrange("p (b t) -> p b t", t=DEC_SEQ)
                        signal = "conv_ready" if lo else "dve_step"
                        dve.tensor_tensor(out, pick(a), pick(b), MUL).then_inc(sem[signal], 1)
                        dve.wait_ge(sem[signal], t.next(signal))

                for q in range(QC):
                    j = q % 2
                    ch = g * QC + q
                    dve.tensor_scalar(ext_s(j)[:, :, 0:3], st_conv[:, bass.ds(ch, 1), :,
                            :].rearrange("p o b t -> p (o b) t"), 1.0, None, MUL).then_inc(sem["dve_step"], 1)
                    dve.wait_ge(sem["dve_step"], t.next("dve_step"))
                    dve.wait_ge(sem[f"acc{j}_free"], t.next(f"acc{j}_free"))
                    co = conv_out[:, bass.ds(ch, 1), :]
                    dve.tensor_scalar(co[:, :, 0:3], ext[j][:, SEQ:EXT_P].rearrange("p (o n) -> p o n", o=1), 1.0,
                            None, MUL).then_inc(sem["dve_step"], 1)
                    dve.wait_ge(sem["dve_step"], t.next("dve_step"))
                    dve.tensor_scalar(co[:, :, 3:27].rearrange("p o (b t) -> p (o b) t", t=3), ext_s(j)[:, :,
                            DEC_SEQ:EXT_S], 1.0, None, MUL).then_inc(sem["dve_step"], 1)
                    dve.wait_ge(sem["dve_step"], t.next("dve_step"))
                    w0 = _V["convw"][0]
                    tap = lambda i: vecs[:, bass.ds(w0 + ch * CONV_W + i, 1)]
                    dve.tensor_scalar(cacc[j], ext[j][:, 0:CL], tap(0), vecs[:, bass.ds(_V["convb"][0] + ch, 1)],
                            MUL, ADD).then_inc(sem["dve_step"], 1)
                    dve.wait_ge(sem["dve_step"], t.next("dve_step"))
                    for i in range(1, CONV_W):
                        signal = "conv_done" if i == CONV_W - 1 else "dve_step"
                        dve.scalar_tensor_tensor(out=cacc[j], in0=ext[j][:, i:i + CL], scalar=tap(i), in1=cacc[j],
                                op0=MUL, op1=ADD).then_inc(sem[signal], 1)
                        dve.wait_ge(sem[signal], t.next(signal))
                    if q >= 1:
                        finish(q - 1)
                finish(QC - 1)
                dve.tensor_scalar(cum_s, cum_g[:, bass.ds(g, 1), :].rearrange("p o t -> p (o t)"), 1.0, None,
                        MUL).then_inc(sem["cum_s_ready"], 1)
                dve.wait_ge(sem["cum_s_ready"], t.next("cum_s_ready"))
                for c in range(NB + 1):
                    n = rows_of(c)
                    dve.wait_ge(sem["x_turned"], t.next("x_turned"))
                    ps = by_head(bank[c % 2][0:n, :])
                    dve.tensor_tensor(by_head(xdt[0:n, c, :]), ps, heads(dt_tm, c, g, n),
                            MUL).then_inc(sem["dve_step"], 1)
                    dve.wait_ge(sem["dve_step"], t.next("dve_step"))
                    dve.tensor_tensor(by_head(xw[0:n, c, :]), ps, heads(wb_tm, c, g, n),
                            MUL).then_inc(sem["turned_read"], 1)
                    dve.wait_ge(sem["turned_read"], t.next("turned_read"))
                def z_gate(hp):
                    dve.wait_ge(sem["z_ready"], t.next("z_ready"))
                    dve.tensor_tensor(zc[hp], zc[hp], zth[hp % 2], MUL).then_inc(sem["z_gated"], 1)
                    dve.wait_ge(sem["z_gated"], t.next("z_gated"))

                z_gate(0)
                dve.wait_ge(sem["b_tm_read"], t.next("b_tm_read"))
                dve.tensor_tensor(b_mask, b_s.rearrange("p (o n) -> p o n", o=1).broadcast_to([NS, DEC_BATCH, P]),
                        C("ofbatch")[0:NS, :].rearrange("p (b o) -> p b o", o=1).broadcast_to([NS, DEC_BATCH, P]), MUL).then_inc(sem["b_tm_ready"], 1)
                dve.wait_ge(sem["b_tm_ready"], t.next("b_tm_ready"))
                dve.wait_ge(sem["cb_ready"], t.next("cb_ready"))
                dve.tensor_tensor(cb_p, bank[0][:, :].rearrange("p (c n) -> p c n", n=P),
                        C("tri").rearrange("p (o n) -> p o n", o=1).broadcast_to([P, NB, P]), MUL).then_inc(sem["dve_step"], 1)
                dve.wait_ge(sem["dve_step"], t.next("dve_step"))
                dve.tensor_tensor(cb_s, bank[1][0:NS, 0:NS], C("tri_s")[0:NS, :], MUL).then_inc(sem["cb_read"], 1)
                dve.wait_ge(sem["cb_read"], t.next("cb_read"))
                z_gate(1)
                dve.wait_ge(sem["states_stored"], t.next("states_stored", 32))
                for c in range(NB):
                    dve.wait_ge(sem["add_ready"], t.next("add_ready"))
                    add = by_head(bank[2 + c % 2][:, :])
                    if c == 0:
                        dve.tensor_copy(by_head(st_p[:, 0, :]), add).then_inc(sem["add_read"], 1)
                        dve.wait_ge(sem["add_read"], t.next("add_read"))
                    else:
                        dve.tensor_tensor(by_head(st_p[:, c, :]), by_head(st_p[:, c - 1, :]), heads(dec_p, c, g,
                                P), MUL).then_inc(sem["dve_step"], 1)
                        dve.wait_ge(sem["dve_step"], t.next("dve_step"))
                        dve.tensor_tensor(by_head(st_p[:, c, :]), by_head(st_p[:, c, :]), add,
                                ADD).then_inc(sem["add_read"], 1)
                        dve.wait_ge(sem["add_read"], t.next("add_read"))
                z_gate(2)

                def segments(hp):
                    dve.wait_ge(sem["cum_spread"], t.next("cum_spread"))
                    d = decays[hp % 2]
                    for j in range(2):
                        h = bass.ds(g * HG + 2 * hp + j, 1)
                        cum_p = cum_tm[:, 0:NB, h].broadcast_to([P, NB, P])
                        dve.tensor_tensor(conv_p(d[j]).rearrange("p (c n) -> p c n", n=P), acc[1][:, j,
                                0:SEQ].rearrange("p (c n) -> p c n", n=P), cum_p, SUB).then_inc(sem["dve_step"], 1)
                        dve.wait_ge(sem["dve_step"], t.next("dve_step"))
                        dve.tensor_scalar(conv_p(d[j]), conv_p(d[j]), 0.0, None, MIN).then_inc(sem["dve_step"], 1)
                        dve.wait_ge(sem["dve_step"], t.next("dve_step"))
                        if j == 0:
                            dve.wait_ge(sem["e_pair_ready"], t.next("e_pair_ready"))
                        dve.tensor_tensor(d[j][0:NS, SEQ:T], acc[0][0:NS, 1, j * NS:(j + 1) * NS], cum_tm[0:NS, NB,
                                h].broadcast_to([NS, NS]), SUB).then_inc(sem["dve_step"], 1)
                        dve.wait_ge(sem["dve_step"], t.next("dve_step"))
                        dve.tensor_scalar(d[j][0:NS, SEQ:T], d[j][0:NS, SEQ:T], 0.0, None,
                                MIN).then_inc(sem["seg_ready"], 1)
                        dve.wait_ge(sem["seg_ready"], t.next("seg_ready"))

                def weigh(hp):
                    d = decays[hp % 2]
                    for j in range(2):
                        dve.wait_ge(sem["seg_exp"], t.next("seg_exp"))
                        dve.tensor_tensor(conv_p(d[j]), conv_p(d[j]), cb_p.rearrange("p c n -> p (c n)"),
                                MUL).then_inc(sem["dve_step"], 1)
                        dve.wait_ge(sem["dve_step"], t.next("dve_step"))
                        dve.tensor_tensor(d[j][0:NS, SEQ:T], d[j][0:NS, SEQ:T], cb_s,
                                MUL).then_inc(sem["dve_step"], 1)
                        dve.wait_ge(sem["dve_step"], t.next("dve_step"))
                    dve.tensor_copy(mark[0:1, 1:2], mark[0:1, 0:1]).then_inc(sem["decay_ready"], 1)
                    dve.wait_ge(sem["decay_ready"], t.next("decay_ready"))

                z_gate(3)
                segments(0)
                weigh(0)
                for hp in range(GC):
                    if hp < GC - 1:
                        segments(hp + 1)
                    dve.wait_ge(sem["y_ready"], t.next("y_ready"))
                    y, e = fm[:, hp, :], e_pair[hp % 2]
                    ds = vecs[:, bass.ds(_V["dskip"][0] + g * GC + hp, 1)]
                    dve.tensor_tensor(t1[:, P:SEQ], bank[1][:, P:SEQ], e[:, P:SEQ], MUL).then_inc(sem["dve_step"], 1)
                    dve.wait_ge(sem["dve_step"], t.next("dve_step"))
                    dve.tensor_tensor(t1[:, SEQ:T], bank[3][:, 0:NS], e[:, SEQ:T], MUL).then_inc(sem["dve_step"], 1)
                    dve.wait_ge(sem["dve_step"], t.next("dve_step"))
                    dve.scalar_tensor_tensor(out=y[:, 0:SEQ], in0=y[:, 0:SEQ], scalar=ds, in1=bank[0][:, :],
                            op0=MUL, op1=ADD).then_inc(sem["dve_step"], 1)
                    dve.wait_ge(sem["dve_step"], t.next("dve_step"))
                    dve.scalar_tensor_tensor(out=y[:, SEQ:T], in0=y[:, SEQ:T], scalar=ds, in1=bank[2][:, 0:NS],
                            op0=MUL, op1=ADD).then_inc(sem["pair_read"], 1)
                    dve.wait_ge(sem["pair_read"], t.next("pair_read"))
                    if hp < GC - 1:
                        weigh(hp + 1)
                    dve.tensor_tensor(y[:, P:T], y[:, P:T], t1[:, P:T], ADD).then_inc(sem["dve_step"], 1)
                    dve.wait_ge(sem["dve_step"], t.next("dve_step"))
                    dve.tensor_tensor(y, y, zc[hp], MUL).then_inc(sem["y_gated"], 1)
                    dve.wait_ge(sem["y_gated"], t.next("y_gated"))
                dve.wait_ge(sem["sq_summed"], t.next("sq_summed", GC))
                for half in range(2):
                    signal = "var_ready" if half else "dve_step"
                    dve.tensor_scalar(rstd[:, half * HT:(half + 1) * HT], bank[half][:, 0:HT], 1.0 / GW, RMS_EPS,
                            MUL, ADD).then_inc(sem[signal], 1)
                    dve.wait_ge(sem[signal], t.next(signal))
                for b in range(DEC_BATCH):
                    dve.wait_ge(sem["adds_ready"], t.next("adds_ready"))
                    add = by_head(bank[2 + b % 2][:, :])
                    dve.tensor_tensor(by_head(st_s[:, b, :]), by_head(st_s[:, b, :]), heads(dec_s, b, g, P),
                            MUL).then_inc(sem["dve_step"], 1)
                    dve.wait_ge(sem["dve_step"], t.next("dve_step"))
                    dve.tensor_tensor(by_head(st_s[:, b, :]), by_head(st_s[:, b, :]), add,
                            ADD).then_inc(sem["adds_read"], 1)
                    dve.wait_ge(sem["adds_read"], t.next("adds_read"))
                dve.tensor_copy(mark[0:1, 1:2], mark[0:1, 0:1]).then_inc(sem["states_done"], 1)
                dve.wait_ge(sem["states_done"], t.next("states_done"))
                dve.wait_ge(sem["std_ready"], t.next("std_ready"))
                dve.reciprocal(rstd, rstd).then_inc(sem["dve_step"], 1)
                dve.wait_ge(sem["dve_step"], t.next("dve_step"))
                for hp in range(GC):
                    gcol = vecs[:, bass.ds(_V["ssmg"][0] + g * GC + hp, 1)]
                    dve.scalar_tensor_tensor(out=BR[:, bass.ds(g * GC + hp, 1), :].rearrange("p o t -> p (o t)"),
                            in0=fm[:, hp, :], scalar=gcol, in1=rstd, op0=MUL, op1=MUL).then_inc(sem["dve_step"], 1)
                    dve.wait_ge(sem["dve_step"], t.next("dve_step"))
                for j in range(2):
                    t.skip(f"acc{j}_free", 2)
            dve.wait_ge(sem["states_stored"], t.next("states_stored", 32))
            for j in range(2):
                t.skip(f"acc{j}_ready", 5 * GROUPS)
            dve.wait_ge(sem["act_over"], t.next("act_over"))
            dve.tensor_copy(mark[0:1, 1:2], mark[0:1, 0:1]).then_inc(sem["stage_over"], 1)
            dve.wait_ge(sem["stage_over"], t.next("stage_over"))

            for i in range(2):
                t.skip("acc0_ready" if i == 0 else "acc1_ready", 3 if i == 0 else 2)
                t.skip("acc0_free" if i == 0 else "acc1_free", 3 if i == 0 else 2)
            dve.wait_ge(sem["acc1_ready"], t.next("acc1_ready"))
            dve.tensor_tensor(v2(q_r), accv(1), v2(C("rope")), MUL).then_inc(sem["acc1_free"], 1)
            dve.wait_ge(sem["acc1_free"], t.next("acc1_free"))
            dve.tensor_copy(mark[0:1, 1:2], mark[0:1, 0:1]).then_inc(sem["kr_ready"], 1)
            dve.wait_ge(sem["kr_ready"], t.next("kr_ready"))
            inv_std(a_rstd, "cq_summed", Q_LORA, RMS_EPS)
            for c in range(3):
                dve.scalar_tensor_tensor(out=cq[:, c, :], in0=cq[:, c, :], scalar=V("qg", c), in1=a_rstd, op0=MUL,
                        op1=MUL).then_inc(sem["dve_step"], 1)
                dve.wait_ge(sem["dve_step"], t.next("dve_step"))
            inv_std(a_rstd, "ckv_summed", KV_LORA, RMS_EPS)
            for c in range(2):
                dve.scalar_tensor_tensor(out=ckv[:, c, :], in0=ckv[:, c, :], scalar=V("kvg", c), in1=a_rstd,
                        op0=MUL, op1=MUL).then_inc(sem["dve_step"], 1)
                dve.wait_ge(sem["dve_step"], t.next("dve_step"))
            dve.wait_ge(sem["krope_ready"], t.next("krope_ready"))
            dve.tensor_copy(mark[0:1, 1:2], mark[0:1, 0:1]).then_inc(sem["latents_ready"], 1)
            dve.wait_ge(sem["latents_ready"], t.next("latents_ready"))
            dve.tensor_copy(mark[0:1, 1:2], mark[0:1, 0:1]).then_inc(sem["head_read"], 1)
            dve.wait_ge(sem["head_read"], t.next("head_read"))
            with t.loop("heads_dve", MLA_HEADS) as h:
                dve.wait_ge(sem["acc1_ready"], t.next("acc1_ready"))
                dve.tensor_tensor(v2(q_r), accv(1), v2(C("rope")), MUL).then_inc(sem["acc1_free"], 1)
                dve.wait_ge(sem["acc1_free"], t.next("acc1_free"))
                dve.wait_ge(sem["q_lat_ready"], t.next("q_lat_ready"))
                hd = bass.ds(h, 1)
                for c in range(2):
                    dve.tensor_scalar(q_lat[:, c, 0:DEC_BATCH, hd, :].rearrange("p b o t -> p b (o t)"), bank[0][:,
                            c * NS:(c + 1) * NS].rearrange("p (b t) -> p b t", t=DEC_SEQ), 1.0, None, MUL).then_inc(sem["dve_step"], 1)
                    dve.wait_ge(sem["dve_step"], t.next("dve_step"))
                dve.tensor_scalar(q_rot[:, 0:DEC_BATCH, hd, :].rearrange("p b o t -> p b (o t)"), bank[0][:,
                        2 * NS:3 * NS].rearrange("p (b t) -> p b t", t=DEC_SEQ), 1.0, None, MUL).then_inc(sem["q_lat_read"], 1)
                dve.wait_ge(sem["q_lat_read"], t.next("q_lat_read"))
                for qb in range(NB):
                    n = (qb + 1) * P
                    s = bank[3 * (qb % 2)]
                    dve.wait_ge(sem["scores_ready"], t.next("scores_ready"))
                    dve.tensor_tensor(s[:, qb * P:n], s[:, qb * P:n], C("causal"), ADD).then_inc(sem["dve_step"], 1)
                    dve.wait_ge(sem["dve_step"], t.next("dve_step"))
                    softmax(s[:, 0:n], stats[qb % 2], prob[qb % 2][:, 0:n], A_SCALE, "prob_ready")
                dve.wait_ge(sem["head_out"], t.next("head_out"))
                dve.tensor_scalar(AT[:, hd, 0:SEQ].rearrange("p o t -> p (o t)"), bank[0][:, :], 1.0, None,
                        MUL).then_inc(sem["head_read"], 1)
                dve.wait_ge(sem["head_read"], t.next("head_read"))
            t.skip("acc0_ready", MLA_HEADS), t.skip("acc0_free", MLA_HEADS)
            dve.tensor_copy(mark[0:1, 1:2], mark[0:1, 0:1]).then_inc(sem["stage_over"], 1)
            dve.wait_ge(sem["stage_over"], t.next("stage_over"))

            def queries(b):
                one = bass.ds(b, 1)
                for c in range(2):
                    dve.tensor_scalar(q_lat_b[:, c, :], q_lat[:, c, one, :, :].rearrange("p b h t -> p (b h t)"),
                            1.0, None, MUL).then_inc(sem["dve_step"], 1)
                    dve.wait_ge(sem["dve_step"], t.next("dve_step"))
                for h in range(2):
                    of = slice(h * ROPE, (h + 1) * ROPE)
                    signal = "batch_q_ready" if h else "dve_step"
                    dve.tensor_scalar(q_rot_b[of, h, :], q_rot[of, one, :, :].rearrange("p b h t -> p (b h t)"),
                            1.0, None, MUL).then_inc(sem[signal], 1)
                    dve.wait_ge(sem[signal], t.next(signal))

            dve.memset(q_lat[:, :, DEC_BATCH, :, :], 0.0).then_inc(sem["dve_step"], 1)
            dve.wait_ge(sem["dve_step"], t.next("dve_step"))
            dve.memset(q_rot[:, DEC_BATCH, :, :], 0.0).then_inc(sem["dve_step"], 1)
            dve.wait_ge(sem["dve_step"], t.next("dve_step"))
            dve.memset(q_rot_b, 0.0).then_inc(sem["dve_step"], 1)
            dve.wait_ge(sem["dve_step"], t.next("dve_step"))
            queries(0)
            dve.tensor_copy(mark[0:1, 1:2], mark[0:1, 0:1]).then_inc(sem["o_lat_ready"], 1)
            dve.wait_ge(sem["o_lat_ready"], t.next("o_lat_ready"))
            with t.loop("merge_b_dve", KC) as j:
                dve.tensor_scalar(gate_bias, vecs[:, bass.ds(_V["bgate"][0] + KC + j, 1)], 0.5, None,
                        MUL).then_inc(sem["gate_bias_ready"], 1)
                dve.wait_ge(sem["gate_bias_ready"], t.next("gate_bias_ready"))
                dve.wait_ge(sem["acc0_ready"], t.next("acc0_ready"))
                dve.tensor_tensor(s_new, acc[0][0:NS, 0, 0:NS], cst[0:NS,
                        bass.ds((_C["newmask"][0] + NS - DEC_SEQ) - j * DEC_SEQ, NS)], ADD).then_inc(sem["acc0_free"], 1)
                dve.wait_ge(sem["acc0_free"], t.next("acc0_free"))
                dve.reduce_max(s_stat[:, 6:7], s_new, AX.X).then_inc(sem["dve_step"], 1)
                dve.wait_ge(sem["dve_step"], t.next("dve_step"))
                for kq in range(4):
                    dve.reduce_max(s_stat[:, 2 + kq:3 + kq], bank[kq][0:NS, :], AX.X).then_inc(sem["dve_step"], 1)
                    dve.wait_ge(sem["dve_step"], t.next("dve_step"))
                dve.reduce_max(s_stat[:, 0:1], s_stat[:, 2:7], AX.X).then_inc(sem["dve_step"], 1)
                dve.wait_ge(sem["dve_step"], t.next("dve_step"))
                dve.tensor_scalar(s_stat[:, 1:2], s_stat[:, 0:1], -A_SCALE, None, MUL).then_inc(sem["max_ready"], 1)
                dve.wait_ge(sem["max_ready"], t.next("max_ready"))
                queries(j + 1)
                dve.wait_ge(sem["exp_ready"], t.next("exp_ready"))
                dve.reduce_sum(s_stat[:, 0:1], s_stat[:, 8:13], AX.X).then_inc(sem["dve_step"], 1)
                dve.wait_ge(sem["dve_step"], t.next("dve_step"))
                dve.reciprocal(s_stat[:, 0:1], s_stat[:, 0:1]).then_inc(sem["dve_step"], 1)
                dve.wait_ge(sem["dve_step"], t.next("dve_step"))
                dve.wait_ge(sem["lat_ready"], t.next("lat_ready"))
                dve.tensor_scalar(o_lat, bank[3][0:NS, 0:KV_LORA], s_stat[:, 0:1], None,
                        MUL).then_inc(sem["lat_read"], 1)
                dve.wait_ge(sem["lat_read"], t.next("lat_read"))
                dve.wait_ge(sem["lat_turned"], t.next("lat_turned"))
                for c in range(2):
                    signal = "o_lat_ready" if c == 1 else "dve_step"
                    dve.tensor_scalar(o_lat_t[:, c, :, bass.ds(j * DEC_SEQ, DEC_SEQ)], bank[3][:,
                            KV_LORA + c * NS:KV_LORA + (c + 1) * NS].rearrange("p (h t) -> p h t",
                                                                                       t=DEC_SEQ), 1.0, None, MUL).then_inc(sem[signal], 1)
                    dve.wait_ge(sem[signal], t.next(signal))
                dve.wait_ge(sem["gate_ready"], t.next("gate_ready"))
                dve.wait_ge(sem["acc1_ready"], t.next("acc1_ready"))
                dve.tensor_tensor(v2(MG[:, bass.ds(j, 1), :].rearrange("p o t -> p (o t)")), v2(gate), accv(1),
                        MUL).then_inc(sem["acc1_free"], 1)
                dve.wait_ge(sem["acc1_free"], t.next("acc1_free"))
                t.skip("acc0_ready"), t.skip("acc0_free")
            dve.wait_ge(sem["sample_out"], t.next("sample_out"))
            dve.tensor_copy(AT[:, 0:MLA_HEADS, SEQ:T], bank[2][:, 0:MLA_HEADS * NS].rearrange("p (h t) -> p h t",
                    t=NS)).then_inc(sem["dve_step"], 1)
            dve.wait_ge(sem["dve_step"], t.next("dve_step"))
            dve.wait_ge(sem["act_over"], t.next("act_over"))
            dve.tensor_copy(mark[0:1, 1:2], mark[0:1, 0:1]).then_inc(sem["stage_over"], 1)
            dve.wait_ge(sem["stage_over"], t.next("stage_over"))

            merge("merge_a", 0)

            with t.loop("mem_k_dve", 4) as i:
                for p in range(2):
                    dve.wait_ge(sem[f"acc{p}_ready"], t.next(f"acc{p}_ready"))
                    dve.tensor_scalar(mk[:, bass.ds(2 * i + p, 1), :].rearrange("p o (a n) -> p (o a) n", a=2),
                            acc[p][:, :, 0:P], 1.0, None, MUL).then_inc(sem[f"acc{p}_free"], 1)
                    dve.wait_ge(sem[f"acc{p}_free"], t.next(f"acc{p}_free"))
            for p in range(2):
                dve.wait_ge(sem[f"acc{p}_ready"], t.next(f"acc{p}_ready"))
                dve.tensor_copy(mv[:, :, p * 512:(p + 1) * 512], acc[p][:, :, :]).then_inc(sem[f"acc{p}_free"], 1)
                dve.wait_ge(sem[f"acc{p}_free"], t.next(f"acc{p}_free"))
            dve.tensor_copy(mark[0:1, 1:2], mark[0:1, 0:1]).then_inc(sem["mem_kv_ready"], 1)
            dve.wait_ge(sem["mem_kv_ready"], t.next("mem_kv_ready"))
            with t.loop("mem_heads_dve", MEM_HEADS) as h:
                dve.tensor_scalar(k_h, mk[:, bass.ds(2 * h, 2), :], 1.0, None, MUL).then_inc(sem["dve_step"], 1)
                dve.wait_ge(sem["dve_step"], t.next("dve_step"))
                dve.tensor_scalar(v_h, mv[:, :, bass.ds(h * MEM_DIM, MEM_DIM)], 1.0, None,
                        MUL).then_inc(sem["kv_head_ready"], 1)
                dve.wait_ge(sem["kv_head_ready"], t.next("kv_head_ready"))
                for p in range(2):
                    dve.wait_ge(sem[f"acc{p}_free"], t.next(f"acc{p}_free"))
                dve.tensor_scalar(mq_s[:, bass.ds(2 * h, 2), :], q_h[:, :, SEQ:T], 1.0, None,
                        MUL).then_inc(sem["dve_step"], 1)
                dve.wait_ge(sem["dve_step"], t.next("dve_step"))
                for qb in range(NB):
                    dve.wait_ge(sem["scores_ready"], t.next("scores_ready"))
                    softmax(bank[qb % 2][:, 0:N_MEM], m_stats[qb % 2], m_prob[qb % 2], M_SCALE, "prob_ready")
                dve.wait_ge(sem["head_out"], t.next("head_out"))
                for c in range(2):
                    signal = "head_read" if c else "dve_step"
                    dve.tensor_scalar(BR[:, bass.ds(2 * h + c, 1), 0:SEQ].rearrange("p o t -> p (o t)"), bank[c][:,
                            :], 1.0, None, MUL).then_inc(sem[signal], 1)
                    dve.wait_ge(sem[signal], t.next(signal))
            for j in range(2):
                t.skip(f"acc{j}_ready", MEM_HEADS)
            dve.memset(m_scores, 0.0).then_inc(sem["dve_step"], 1)
            dve.wait_ge(sem["dve_step"], t.next("dve_step"))
            with t.loop("sample_m_dve", DEC_BATCH // 2) as i:
                for j in range(2):
                    mask = cst[:, bass.ds(i * (2 * NS) + (_C["bmask"][0] + j * NS), NS)]
                    dve.tensor_tensor(q_b[j], mq_s, mask.rearrange("p (o t) -> p o t", o=1).broadcast_to([P, 8,
                            NS]), MUL).then_inc(sem["q_b_ready"], 1)
                    dve.wait_ge(sem["q_b_ready"], t.next("q_b_ready"))
                for j in range(2):
                    dve.wait_ge(sem["scores_ready"], t.next("scores_ready"))
                    dve.tensor_tensor(m_scores, m_scores, bank[j][:, 0:N_MEM], ADD).then_inc(sem["dve_step"], 1)
                    dve.wait_ge(sem["dve_step"], t.next("dve_step"))
            softmax(m_scores, m_stats[0], m_scores, M_SCALE, "prob_ready")
            dve.memset(o_m, 0.0).then_inc(sem["dve_step"], 1)
            dve.wait_ge(sem["dve_step"], t.next("dve_step"))
            t.skip("turned_out", (MLA_HEADS + MEM_HEADS) * NB + 2 * KC)
            dve.wait_ge(sem["turned_out"], t.next("turned_out"))
            with t.loop("sample_mv_dve", DEC_BATCH // 2) as i:
                for j in range(2):
                    mask = cst[:, bass.ds(i * (2 * NS) + (_C["bmask"][0] + j * NS), NS)]
                    dve.tensor_tensor(q_b[j], ms_prob_t.rearrange("p b (h n) -> p (b h) n", n=NS),
                            mask.rearrange("p (o t) -> p o t", o=1).broadcast_to([P, 8, NS]), MUL).then_inc(sem["q_b_ready"], 1)
                    dve.wait_ge(sem["q_b_ready"], t.next("q_b_ready"))
                for j in range(2):
                    dve.wait_ge(sem["head_out"], t.next("head_out"))
                    dve.tensor_tensor(o_m, o_m, bank[j][:, 0:MEM_DIM], ADD).then_inc(sem["dve_step"], 1)
                    dve.wait_ge(sem["dve_step"], t.next("dve_step"))
            dve.tensor_copy(mark[0:1, 1:2], mark[0:1, 0:1]).then_inc(sem["o_m_ready"], 1)
            dve.wait_ge(sem["o_m_ready"], t.next("o_m_ready"))
            dve.wait_ge(sem["sample_out"], t.next("sample_out"))
            for c in range(2):
                dve.tensor_copy(BR[:, c:2 * MEM_HEADS:2, SEQ:T], bank[2][:,
                        c * P:(c + 1) * P].rearrange("p (h t) -> p h t", t=NS)).then_inc(sem["dve_step"], 1)
                dve.wait_ge(sem["dve_step"], t.next("dve_step"))
            dve.wait_ge(sem["act_over"], t.next("act_over"))
            dve.tensor_copy(mark[0:1, 1:2], mark[0:1, 0:1]).then_inc(sem["stage_over"], 1)
            dve.wait_ge(sem["stage_over"], t.next("stage_over"))

            merge("merge_m", 2)

            with t.loop("out_dve", KC // 4) as i:
                for p in range(4):
                    dve.wait_ge(sem[f"acc{p % 2}_ready"], t.next(f"acc{p % 2}_ready"))
                    x = X[:, bass.ds(4 * i + p, 1), :].rearrange("p o t -> p (o t)")
                    dve.scalar_tensor_tensor(out=v2(x), in0=v2(x), scalar=ALPHA, in1=accv(p % 2), op0=MUL,
                            op1=ADD).then_inc(sem[f"acc{p % 2}_free"], 1)
                    dve.wait_ge(sem[f"acc{p % 2}_free"], t.next(f"acc{p % 2}_free"))
            norm("ln1g", False)
            for half in range(2):
                with t.loop("up_dve", HALF_F // 4) as i:
                    for p in range(4):
                        dve.wait_ge(sem[f"acc{p % 2}_ready"], t.next(f"acc{p % 2}_ready"))
                        b = vecs[:, bass.ds(i * 4 + (_V["bup"][0] + half * HALF_F + p), 1)]
                        r, q = relu[p % 2], square[p % 2]
                        dve.tensor_scalar(v2(r), accv(p % 2), b, 0.0, ADD, MAX).then_inc(sem[f"acc{p % 2}_free"], 1)
                        dve.wait_ge(sem[f"acc{p % 2}_free"], t.next(f"acc{p % 2}_free"))
                        dve.tensor_tensor(q, r, r, MUL).then_inc(sem["dve_step"], 1)
                        dve.wait_ge(sem["dve_step"], t.next("dve_step"))
                        hi, lo = (a[:, bass.ds(4 * i + p, 1), :].rearrange("p o t -> p (o t)") for a in (hid_h,
                                hid_l))
                        dve.tensor_scalar(hi, q, 1.0, None, MUL).then_inc(sem["dve_step"], 1)
                        dve.wait_ge(sem["dve_step"], t.next("dve_step"))
                        dve.tensor_tensor(lo, q, hi.bitcast(F), SUB).then_inc(sem["dve_step"], 1)
                        dve.wait_ge(sem["dve_step"], t.next("dve_step"))
                dve.tensor_copy(mark[0:1, 1:2], mark[0:1, 0:1]).then_inc(sem["hidden_ready"], 1)
                dve.wait_ge(sem["hidden_ready"], t.next("hidden_ready"))
                with t.loop(f"down{half}_dve", KC // 2) as i:
                    for p in range(2):
                        x = X[:, bass.ds(2 * i + p, 1), :].rearrange("p o t -> p (o t)")
                        if half == 0:
                            b = vecs[:, bass.ds(i * 2 + (_V["bdown"][0] + p), 1)]
                            dve.tensor_scalar(x, x, ALPHA, b, MUL, ADD).then_inc(sem["dve_step"], 1)
                            dve.wait_ge(sem["dve_step"], t.next("dve_step"))
                        dve.wait_ge(sem[f"acc{p}_ready"], t.next(f"acc{p}_ready"))
                        dve.tensor_tensor(v2(x), v2(x), accv(p), ADD).then_inc(sem[f"acc{p}_free"], 1)
                        dve.wait_ge(sem[f"acc{p}_free"], t.next(f"acc{p}_free"))
            norm("ln2g", True)

        @block.tensor
        def _(pe):
            t = Counts(pe, {})
            at_slot = [0]

            def next_block():
                s = at_slot[0]
                at_slot[0] = (s + 1) % RING
                pe.wait_ge(sem[f"weights_in_slot{s}"], t.next(f"weights_in_slot{s}", 16))
                return ring[:, s * BLOCK:(s + 1) * BLOCK]

            def project(p, x, n_blocks=1, width=HT):
                pe.wait_ge(sem[f"acc{p}_free"], t.next(f"acc{p}_free"))
                for b in range(n_blocks):
                    w = next_block()
                    for half in range(2):
                        for k in range(KC):
                            kk = b * KC + k
                            m = pe.matmul(acc[p][:, half, 0:width], w[:, k * P:(k + 1) * P],
                                          x(kk)[:, half * width:(half + 1) * width],
                                          start=kk == 0, stop=kk == n_blocks * KC - 1)
                            if half == 0 and k == 0:
                                m.then_inc(sem["blocks_begun"], 1)
                m.then_inc(sem[f"acc{p}_ready"], 1)

            def rms(squares, name):
                for i, s in enumerate(squares):
                    for half in range(2):
                        m = pe.matmul(bank[2 + half][:, 0:HT], C("ones"), s[:, half * HT:(half + 1) * HT],
                                       start=i == 0, stop=i == len(squares) - 1)
                m.then_inc(sem[name], 1)

            def norm():
                for i, (name, src) in enumerate((("sums_ready", X), ("norm_summed", n_sq))):
                    pe.wait_ge(sem["norm_in"], t.next("norm_in"))
                    for c in range(KC):
                        for half in range(2):
                            m = pe.matmul(bank[2 * i + half][:, 0:HT], C("ones"), src[:, c, half * HT:(half + 1) * HT],
                                           start=c == 0, stop=c == KC - 1)
                    m.then_inc(sem[name], 1)

            def merge(name, source):
                pe.wait_ge(sem["stage_over"], t.next("stage_over"))
                with t.loop(f"{name}_pe", KC):
                    at_slot[0] = START[name]
                    project(0, lambda c: X[:, c, :])
                    project(1, lambda c: source[:, c, :])

            def project_parts(p, xh, xl, n_blocks=1):
                pe.wait_ge(sem[f"acc{p}_free"], t.next(f"acc{p}_free"))
                for b in range(n_blocks):
                    j = (p * n_blocks + b) % 2
                    pe.wait_ge(sem["split_ready"], t.next("split_ready"))
                    wh, wl = split[j]
                    for half in range(2):
                        of = slice(half * HT, (half + 1) * HT)
                        for k in range(KC):
                            kk = b * KC + k
                            for n, (w, x) in enumerate(((wh, xh), (wh, xl), (wl, xh))):
                                m = pe.matmul(acc[p][:, half, 0:HT], w[:, k * P:(k + 1) * P], x[:, kk, of],
                                               start=kk == 0 and n == 0, stop=kk == n_blocks * KC - 1 and n == 2)
                                if half == 0 and k == 0 and n == 0:
                                    m.then_inc(sem["split_begun"], 1)
                m.then_inc(sem[f"acc{p}_ready"], 1)

            pe.wait_ge(sem["const_loaded"], 16)
            pe.wait_ge(sem["x_loaded"], 16)
            at_slot[0] = START["dt"]
            project(0, lambda c: X[:, c, :])
            pe.wait_ge(sem["dt_ready"], t.next("dt_ready"))
            for j, row in enumerate((dtw["dt"], dtw["cum"])):
                for c, b in enumerate(blocks_of(row)):
                    n = P if c < NB else NS
                    m = pe.transpose(bank[j][0:n, c * SSM_HEADS:(c + 1) * SSM_HEADS], b, ident32)
            m.then_inc(sem["dt_turned"], 1)
            pe.wait_ge(sem["cum_ready"], t.next("cum_ready"))
            pe.matmul(bank[2][:, 0:NB * SSM_HEADS], C("last"), cum_tm[:, 0:NB, :], start=True, stop=True)
            pe.matmul(bank[3][0:NS, 0:SSM_HEADS], C("last_s")[0:NS, :], cum_tm[0:NS, NB, :], start=True, stop=True)
            m = pe.matmul(bank[1][:, 0:DEC_BATCH * SSM_HEADS], C("ones")[0:NS, :], cum_last[:, :, :],
                           start=True, stop=True)
            m.then_inc(sem["last_ready"], 1)

            pe.wait_ge(sem["stage_over"], t.next("stage_over"))
            with t.loop("ssm_pe", GROUPS) as g:
                at_slot[0] = START["ssm"]
                for q in range(QC):
                    project(q % 2, lambda c: X[:, c, :])
                project(0, lambda c: X[:, c, :])
                pe.wait_ge(sem["conv_ready"], t.next("conv_ready", QC))
                for c in range(NB + 1):
                    n = rows_of(c)
                    if c >= 2:
                        pe.wait_ge(sem["turned_read"], t.next("turned_read"))
                    for f in range(GC):
                        m = pe.transpose(bank[c % 2][0:n, f * P:(f + 1) * P], toks(fm[:, f, :], c), C("ident"))
                    m.then_inc(sem["x_turned"], 1)
                for c in range(NB):
                    pe.transpose(bank[2][:, c * P:(c + 1) * P], toks(fm[:, GC, :], c), C("ident"))
                m = pe.transpose(bank[3][0:NS, 0:P], toks(fm[:, GC, :], NB), C("ident"))
                m.then_inc(sem["b_turned"], 1)
                project(1, lambda c: X[:, c, :])
                pe.wait_ge(sem["turned_read"], t.next("turned_read", 2))
                for c in range(NB):
                    pe.matmul(bank[0][:, c * P:(c + 1) * P], toks(fm[:, GC, :], c), toks(fm[:, GC + 1, :], c),
                               start=True, stop=True)
                m = pe.matmul(bank[1][0:NS, 0:NS], toks(fm[:, GC, :], NB), toks(fm[:, GC + 1, :], NB),
                               start=True, stop=True)
                m.then_inc(sem["cb_ready"], 1)
                project(0, lambda c: X[:, c, :])
                pe.wait_ge(sem["b_tm_ready"], t.next("b_tm_ready"))
                for c in range(NB):
                    if c >= 2:
                        pe.wait_ge(sem["add_read"], t.next("add_read"))
                    m = pe.matmul(bank[2 + c % 2][:, :], b_tm[:, c, :], xw[:, c, :], start=True, stop=True)
                    m.then_inc(sem["add_ready"], 1)
                project(1, lambda c: X[:, c, :])
                pe.wait_ge(sem["add_read"], t.next("add_read", 2))
                pe.wait_ge(sem["cb_read"], t.next("cb_read"))
                pe.wait_ge(sem["cum_s_ready"], t.next("cum_s_ready"))
                pe.wait_ge(sem["states_loaded"], t.next("states_loaded", 16))
                pe.wait_ge(sem["acc0_free"], t.value("acc0_free") + 1)
                pe.wait_ge(sem["acc1_free"], t.value("acc1_free") + 1)

                def spread(hp):
                    for j in range(2):
                        h = 2 * hp + j
                        sel = C("sel")[0:HG, h * P:(h + 1) * P]
                        pe.matmul(acc[1][:, j, 0:SEQ], sel, cum_s[:, 0:SEQ], start=True, stop=True)
                    sp = C("selpair")[0:HG, hp * P:(hp + 1) * P]
                    pe.matmul(acc[0][:, 0, 0:SEQ], sp, cum_s[:, 0:SEQ], start=True, stop=True)
                    for j in range(2):
                        h = 2 * hp + j
                        pe.matmul(acc[0][0:NS, 1, j * NS:(j + 1) * NS], C("sel")[0:HG, h * P:h * P + NS],
                                   cum_s[:, SEQ:T], start=True, stop=True)
                    m = pe.matmul(acc[0][:, 1, 2 * NS:3 * NS], sp, cum_s[:, SEQ:T], start=True, stop=True)
                    m.then_inc(sem["cum_spread"], 1)

                spread(0)
                for hp in range(GC):
                    pe.wait_ge(sem["seg_ready"], t.next("seg_ready", 2))
                    if hp < GC - 1:
                        spread(hp + 1)
                    if hp:
                        pe.wait_ge(sem["pair_read"], t.next("pair_read"))
                    pe.wait_ge(sem["decay_ready"], t.next("decay_ready"))
                    d = decays[hp % 2]
                    for c in range(NB):
                        for j in range(2):
                            h = 2 * hp + j
                            pe.matmul(bank[0][j * HEAD_DIM:(j + 1) * HEAD_DIM, c * P:(c + 1) * P],
                                       xdt[:, c, h * HEAD_DIM:(h + 1) * HEAD_DIM], toks(d[j], c),
                                       start=True, stop=True)
                    for c in range(1, NB):
                        pe.matmul(bank[1][:, c * P:(c + 1) * P], st_p[:, c - 1, hp * P:(hp + 1) * P],
                                   toks(fm[:, GC + 1, :], c), start=True, stop=True)
                    for j in range(2):
                        h = 2 * hp + j
                        pe.matmul(bank[2][j * HEAD_DIM:(j + 1) * HEAD_DIM, 0:NS],
                                   xdt[0:NS, NB, h * HEAD_DIM:(h + 1) * HEAD_DIM], d[j][0:NS, SEQ:T],
                                   start=True, stop=True)
                    for b in range(DEC_BATCH):
                        at = SEQ + b * DEC_SEQ
                        m = pe.matmul(bank[3][:, b * DEC_SEQ:(b + 1) * DEC_SEQ], st_s[:, b, hp * P:(hp + 1) * P],
                                       fm[:, GC + 1, at:at + DEC_SEQ], start=True, stop=True)
                    m.then_inc(sem["y_ready"], 1)
                pe.wait_ge(sem["pair_read"], t.next("pair_read"))
                for hp in range(GC):
                    pe.wait_ge(sem["sq_ready"], t.next("sq_ready"))
                    for half in range(2):
                        m = pe.matmul(bank[half][:, 0:HT], C("ones"), sq[hp][:, half * HT:(half + 1) * HT],
                                       start=hp == 0, stop=hp == GC - 1)
                    m.then_inc(sem["sq_summed"], 1)
                for b in range(DEC_BATCH):
                    if b >= 2:
                        pe.wait_ge(sem["adds_read"], t.next("adds_read"))
                    m = pe.matmul(bank[2 + b % 2][:, :], b_mask[:, b, :], xw[0:NS, NB, :], start=True, stop=True)
                    m.then_inc(sem["adds_ready"], 1)
                pe.wait_ge(sem["adds_read"], t.next("adds_read", 2))
                pe.wait_ge(sem["var_ready"], t.next("var_ready"))

            pe.wait_ge(sem["stage_over"], t.next("stage_over"))
            at_slot[0] = START["latents"]
            for i in range(6):
                project(i % 2, lambda c: X[:, c, :])
            pe.wait_ge(sem["squares_ready"], t.next("squares_ready", 3))
            rms(a_sq[0:3], "cq_summed")
            pe.wait_ge(sem["kr_ready"], t.next("kr_ready"))
            for half in range(2):
                m = pe.matmul(bank[half][:, 0:HT], C("fold"), q_r[:, half * HT:(half + 1) * HT], start=True,
                        stop=True)
            m.then_inc(sem["kr_folded"], 1)
            pe.wait_ge(sem["squares_ready"], t.next("squares_ready", 2))
            pe.wait_ge(sem["var_ready"], t.next("var_ready"))
            rms(a_sq[3:5], "ckv_summed")
            pe.wait_ge(sem["latents_ready"], t.next("latents_ready"))
            for c in range(2):
                m = pe.transpose(bank[0][0:NS, c * P:(c + 1) * P], ckv[:, c, SEQ:T], C("ident"))
            m.then_inc(sem["new_turned"], 1)
            pe.wait_ge(sem["new_read"], t.next("new_read"))
            t.skip("var_ready")
            with t.loop("heads_pe", MLA_HEADS):
                at_slot[0] = START["heads"]
                w = next_block()
                for p, off in ((0, 0), (1, P)):
                    pe.wait_ge(sem[f"acc{p}_free"], t.next(f"acc{p}_free"))
                    for half in range(2):
                        for c in range(3):
                            m = pe.matmul(acc[p][:, half, 0:HT], w[:, c * 256 + off:c * 256 + off + P],
                                           cq[:, c, half * HT:(half + 1) * HT], start=c == 0, stop=c == 2)
                            if (p, half, c) == (0, 0, 0):
                                m.then_inc(sem["blocks_begun"], 1)
                    m.then_inc(sem[f"acc{p}_ready"], 1)
                pe.wait_ge(sem["acc0_free"], t.value("acc0_free") + 1)
                pe.wait_ge(sem["acc1_free"], t.value("acc1_free") + 1)
                pe.wait_ge(sem["head_read"], t.next("head_read"))
                for c in range(2):
                    pe.matmul(bank[0][:, c * NS:(c + 1) * NS], w[:, 768 + c * P:768 + (c + 1) * P], q_n[:, SEQ:T],
                               start=True, stop=True)
                m = pe.matmul(bank[0][:, 2 * NS:3 * NS], C("fold"), q_r[:, SEQ:T],
                               start=True, stop=True)
                m.then_inc(sem["q_lat_ready"], 1)
                w = next_block()
                for c in range(2):
                    m = pe.matmul(bank[1][:, :], w[:, c * P:(c + 1) * P], ckv[:, c, 0:SEQ], start=c == 0, stop=c == 1)
                    if c == 0:
                        m.then_inc(sem["blocks_begun"], 1)
                m.then_inc(sem["k_ready"], 1)
                for b in range(NB):
                    for c in range(2):
                        m = pe.matmul(bank[2][:, b * P:(b + 1) * P], ckv[:, c, b * P:(b + 1) * P],
                                       w[:, 256 + c * P:256 + (c + 1) * P], start=c == 0, stop=c == 1)
                m.then_inc(sem["v_ready"], 1)
                pe.wait_ge(sem["kv_read"], t.next("kv_read", 2))
                pe.wait_ge(sem["q_lat_read"], t.next("q_lat_read"))

                def turn(qb):
                    pe.wait_ge(sem["prob_ready"], t.next("prob_ready"))
                    for b in range(qb + 1):
                        m = pe.transpose(bank[1 + qb % 2][:, b * P:(b + 1) * P], prob[qb % 2][:, b * P:(b + 1) * P],
                                          C("ident"))
                    m.then_inc(sem["prob_turned"], 1)

                for qb in range(NB):
                    n = (qb + 1) * P
                    s = bank[3 * (qb % 2)]
                    if qb >= 2:
                        pe.wait_ge(sem["exp_ready"], t.next("exp_ready"))
                    pe.matmul(s[:, 0:n], q_n[:, qb * P:n], k_n[:, 0:n], start=True, stop=False)
                    m = pe.matmul(s[:, 0:n], q_r[:, qb * P:n], krope[:, 0:n], start=False, stop=True)
                    m.then_inc(sem["scores_ready"], 1)
                    if qb >= 1:
                        if qb >= 3:
                            pe.wait_ge(sem["turned_out"], t.next("turned_out"))
                        turn(qb - 1)
                pe.wait_ge(sem["turned_out"], t.next("turned_out"))
                turn(NB - 1)
                pe.wait_ge(sem["turned_out"], t.next("turned_out", 2))
                pe.wait_ge(sem["exp_ready"], t.next("exp_ready", 2))
                for b in range(NB):
                    m = pe.matmul(bank[0][:, b * P:SEQ], v_tm[:, b, :], prob_t[:, b, b * P:SEQ],
                                   start=b == 0, stop=b == NB - 1, skip_group_check=True)
                m.then_inc(sem["head_out"], 1)

            pe.wait_ge(sem["stage_over"], t.next("stage_over"))
            t.skip("head_read")
            with t.loop("merge_b_pe", KC):
                at_slot[0] = START["merge_b"]
                pe.wait_ge(sem["batch_q_ready"], t.next("batch_q_ready"))
                for kq in range(4):
                    pe.wait_ge(sem[f"keys_in_slot{kq}"], t.next(f"keys_in_slot{kq}", 4 * 16))
                    if kq == 3:
                        pe.wait_ge(sem["o_lat_ready"], t.next("o_lat_ready"))
                    kv = keys[kq].rearrange("p (g n) -> p g n", g=4)
                    out = bank[kq][0:NS, :].rearrange("p (g h n) -> p g h n", g=4, h=2)
                    for h in range(2):
                        pe.matmul(out[:, :, h, :], q_rot_b[:, h, :], kv[:, :, 2 * PAGE:KEYS_W], start=h == 0,
                                   stop=False, skip_group_check=True)
                    for c in range(2):
                        m = pe.matmul(bank[kq][0:NS, :], q_lat_b[:, c, :], kv[:, :, c * PAGE:(c + 1) * PAGE],
                                       start=False, stop=c == 1, skip_group_check=True)
                    m.then_inc(sem["keys_used"], 1)
                pe.wait_ge(sem[f"acc{0}_free"], t.next(f"acc{0}_free"))
                for c in range(2):
                    pe.matmul(acc[0][0:NS, 0, 0:NS], q_lat_b[:, c, :], ckv[:, c, SEQ:T], start=c == 0, stop=False)
                m = pe.matmul(acc[0][0:NS, 0, 0:NS], q_rot_b[:, 0, :], krope[:, SEQ:T], start=False, stop=True)
                m.then_inc(sem["acc0_ready"], 1)
                project(1, lambda c: BR[:, c, :], 2)
                pe.wait_ge(sem["exp_ready"], t.next("exp_ready"))
                pe.matmul(bank[1][:, 0:NS], s_prob[:, 0:PAGE], ident32, start=True, stop=True)
                for g in range(1, N_PAGES):
                    pe.transpose(bank[1][:, g * NS:(g + 1) * NS], s_prob[:, g * PAGE:(g + 1) * PAGE], ident32)
                m = pe.transpose(bank[2][0:NS, 0:NS], s_prob[:, N_PAGES * PAGE:], ident32)
                m.then_inc(sem["prob_turned"], 1)
                pe.wait_ge(sem[f"acc{0}_free"], t.next(f"acc{0}_free"))
                w = next_block()
                for half in range(2):
                    if half:
                        pe.wait_ge(sem["turned_out"], t.next("turned_out", 2))
                        out = bank[3][0:NS, 0:KV_LORA]
                        for kq in range(4):
                            pe.wait_ge(sem[f"rows_in_slot{kq}"], t.next(f"rows_in_slot{kq}", 4 * 16))
                            for i in range(4):
                                m = pe.matmul(out, s_prob_t[:, kq * 4 + i, :],
                                               rows[kq][:, i * KV_LORA:(i + 1) * KV_LORA],
                                               start=kq == 0 and i == 0, stop=False)
                            m.then_inc(sem["rows_used"], 1)
                        m = pe.matmul(out, s_prob_n, ckv_new, start=False, stop=True)
                        m.then_inc(sem["lat_ready"], 1)
                    for c in range(KC):
                        m = pe.matmul(acc[0][:, half, 0:HT], w[:, c * P:(c + 1) * P],
                                       X[:, c, half * HT:(half + 1) * HT], start=c == 0, stop=c == KC - 1)
                        if half == 0 and c == 0:
                            m.then_inc(sem["blocks_begun"], 1)
                m.then_inc(sem["acc0_ready"], 1)
                pe.wait_ge(sem["lat_read"], t.next("lat_read"))
                for c in range(2):
                    m = pe.matmul(bank[3][:, KV_LORA + c * NS:KV_LORA + (c + 1) * NS], o_lat[:, c * P:(c + 1) * P],
                                   ident32, start=True, stop=True)
                m.then_inc(sem["lat_turned"], 1)
            pe.wait_ge(sem["o_lat_ready"], t.next("o_lat_ready"))
            at_slot[0] = START["values"]
            for w4 in range(2):
                w = next_block()
                for hh in range(4):
                    h = w4 * 4 + hh
                    for c in range(2):
                        m = pe.matmul(bank[2][:, h * NS:(h + 1) * NS], w[:, c * 512 + hh * P:c * 512 + (hh + 1) * P],
                                       o_lat_t[:, c, h, :], start=c == 0, stop=c == 1)
                        if hh == 0 and c == 0:
                            m.then_inc(sem["blocks_begun"], 1)
            m.then_inc(sem["sample_out"], 1)

            merge("merge_a", AT)

            pe.wait_ge(sem["stage_over"], t.next("stage_over"))
            pe.wait_ge(sem["mem_loaded"], t.next("mem_loaded", 16))
            with t.loop("mem_k_pe", 4):
                at_slot[0] = START["mem_k"]
                for p in range(2):
                    project(p, lambda c: mem[:, c, :], width=P)
            at_slot[0] = START["mem_v"]
            for nn in range(2):
                pe.wait_ge(sem[f"acc{nn}_free"], t.next(f"acc{nn}_free"))
                for b in range(4):
                    w = next_block()
                    for c in range(2):
                        for mb in range(2):
                            m = pe.matmul(acc[nn][:, mb, :], mem[:, b * 2 + c, mb * P:(mb + 1) * P],
                                           w[:, c * 512:(c + 1) * 512], start=b == 0 and c == 0, stop=b == 3 and c == 1)
                            if c == 0 and mb == 0:
                                m.then_inc(sem["blocks_begun"], 1)
                m.then_inc(sem[f"acc{nn}_ready"], 1)
            with t.loop("mem_heads_pe", MEM_HEADS):
                at_slot[0] = START["mq"]
                for p in range(2):
                    project(p, lambda c: X[:, c, :])
                pe.wait_ge(sem["acc0_free"], t.value("acc0_free") + 1)
                pe.wait_ge(sem["acc1_free"], t.value("acc1_free") + 1)
                pe.wait_ge(sem["kv_head_ready"], t.next("kv_head_ready"))
                for qb in range(NB):
                    if qb >= 2:
                        pe.wait_ge(sem["exp_ready"], t.next("exp_ready"))
                    for c in range(2):
                        m = pe.matmul(bank[qb % 2][:, 0:N_MEM], q_h[:, c, qb * P:(qb + 1) * P], k_h[:, c, :],
                                       start=c == 0, stop=c == 1)
                    m.then_inc(sem["scores_ready"], 1)
                    for q in ([qb - 1] if 1 <= qb < NB - 1 else [NB - 2, NB - 1] if qb == NB - 1 else []):
                        if q >= 2:
                            pe.wait_ge(sem["turned_out"], t.next("turned_out"))
                        pe.wait_ge(sem["prob_ready"], t.next("prob_ready"))
                        for b in range(2):
                            m = pe.transpose(bank[2 + q % 2][:, b * P:(b + 1) * P], m_prob[q % 2][:,
                                    b * P:(b + 1) * P],
                                              C("ident"))
                        m.then_inc(sem["prob_turned"], 1)
                pe.wait_ge(sem["turned_out"], t.next("turned_out", 2))
                pe.wait_ge(sem["exp_ready"], t.next("exp_ready", 2))
                for c in range(2):
                    for b in range(2):
                        m = pe.matmul(bank[c][:, :], v_h[:, b, c * P:(c + 1) * P], m_prob_t[:, b, :],
                                       start=b == 0, stop=b == 1)
                m.then_inc(sem["head_out"], 1)
                pe.wait_ge(sem["head_read"], t.next("head_read"))
            with t.loop("sample_m_pe", DEC_BATCH // 2):
                for j in range(2):
                    pe.wait_ge(sem[f"mem_k{j}_loaded"], t.next(f"mem_k{j}_loaded", 16))
                    pe.wait_ge(sem["q_b_ready"], t.next("q_b_ready"))
                    for h in range(MEM_HEADS):
                        for c in range(2):
                            m = pe.matmul(bank[j][h * NS:(h + 1) * NS, 0:N_MEM], q_b[j][:, 2 * h + c, :],
                                           mem_k[j][:, 2 * h + c, :], start=c == 0, stop=c == 1)
                    m.then_inc(sem["scores_ready"], 1)
            pe.wait_ge(sem["prob_ready"], t.next("prob_ready"))
            for b in range(2):
                m = pe.transpose(bank[2][:, b * P:(b + 1) * P], m_scores[:, b * P:(b + 1) * P], C("ident"))
            m.then_inc(sem["prob_turned"], 1)
            pe.wait_ge(sem["turned_out"], t.next("turned_out"))
            with t.loop("sample_mv_pe", DEC_BATCH // 2):
                for j in range(2):
                    pe.wait_ge(sem[f"mem_v{j}_loaded"], t.next(f"mem_v{j}_loaded", 16))
                    pe.wait_ge(sem["q_b_ready"], t.next("q_b_ready"))
                    for h in range(MEM_HEADS):
                        for b in range(2):
                            m = pe.matmul(bank[j][h * NS:(h + 1) * NS, 0:MEM_DIM], q_b[j][:, b * MEM_HEADS + h, :],
                                           mem_v[j][:, b, h * MEM_DIM:(h + 1) * MEM_DIM], start=b == 0, stop=b == 1)
                    m.then_inc(sem["head_out"], 1)
            pe.wait_ge(sem["o_m_ready"], t.next("o_m_ready"))
            for c in range(2):
                m = pe.transpose(bank[2][:, c * P:(c + 1) * P], o_m[:, c * P:(c + 1) * P], C("ident"))
            m.then_inc(sem["sample_out"], 1)

            merge("merge_m", BR)

            pe.wait_ge(sem["stage_over"], t.next("stage_over"))
            with t.loop("out_pe", KC // 4):
                for p in range(4):
                    project_parts(p % 2, MG_H, MG_L)
            norm()
            pe.wait_ge(sem["normed"], t.next("normed", KC))
            for half in range(2):
                with t.loop("up_pe", HALF_F // 4):
                    for p in range(4):
                        project_parts(p % 2, X_H, X_L)
                pe.wait_ge(sem["hidden_ready"], t.next("hidden_ready"))
                with t.loop("down_pe", KC // 2):
                    for p in range(2):
                        project_parts(p, hid_h, hid_l, 2)
            norm()


def lay_out(a):
    def tiles(w):
        k, n = w.shape
        return w.reshape(k // BLOCK, KC, P, n // P, P).transpose(3, 0, 2, 1, 4).reshape(n // P, k // BLOCK, P, BLOCK)
    w_in = a["w_in"]
    sizes = (Q_LORA, KV_LORA, ROPE, D_INNER, CONV_DIM, SSM_HEADS, MEM_HEADS * MEM_DIM, 3 * D_MODEL)
    cq, ckv, kr, z, xbc, dt, mq, gates = np.split(w_in, np.cumsum(sizes)[:-1], axis=1)
    order = [c for g in range(GROUPS) for c in [*range(g * GC, g * GC + GC), D_INNER // P + g, D_INNER // P + GROUPS + g]]
    blocks = []
    add = lambda x: blocks.extend(x.reshape(-1, P, BLOCK))
    dtp = np.zeros((D_MODEL, P), np.float32); dtp[:, :SSM_HEADS] = dt
    add(tiles(dtp))
    tx, tz = tiles(xbc), tiles(z)
    for g in range(GROUPS):
        add(tx[order[g * QC:(g + 1) * QC]])
        add(tz[g * GC:(g + 1) * GC])
    tg = tiles(gates)
    branches = {"b": (1, tiles(a["w_o_ssm"])), "a": (0, tiles(a["w_o_mla"])), "m": (2, tiles(a["w_o_mem"]))}
    def merge(name):
        i, w = branches[name]
        for j in range(KC):
            for block in (w[j], tg[i * KC + j]) if name == "b" else (tg[i * KC + j], w[j]):
                add(block)
    add(tiles(cq)); add(tiles(ckv))
    swap = np.r_[ROPE // 2:ROPE, 0:ROPE // 2]
    add(tiles(np.concatenate([kr, kr[:, swap]], 1)))
    uq, uk, uv = a["w_uq"], a["w_uk"], a["w_uv"]
    for h in range(MLA_HEADS):
        q = np.concatenate([uq[:, h, :NOPE], uq[:, h, NOPE:], uq[:, h, NOPE:][:, swap]], 1).reshape(3, P, 256)
        add(np.concatenate([q.transpose(1, 0, 2).reshape(P, 768), uk[:, h, :].T], 1))
        kh = uk[:, h, :].reshape(2, P, P).transpose(1, 0, 2).reshape(P, 256)
        vh = uv[:, h, :].reshape(2, P, P).transpose(1, 0, 2).reshape(P, 256)
        add(np.concatenate([kh, vh, np.zeros((P, 512), np.float32)], 1))
    merge("b")
    for w4 in range(2):
        add(uv[:, w4 * 4:w4 * 4 + 4].reshape(2, P, 4 * P).transpose(1, 0, 2).reshape(P, BLOCK))
    merge("a")
    add(tiles(a["w_mem_k"].reshape(D_MODEL, -1)))
    mv = a["w_mem_v"].reshape(4, 2, P, 2, 512)
    add(mv.transpose(3, 0, 2, 1, 4).reshape(8, P, BLOCK))
    add(tiles(mq))
    merge("m")
    add(tiles(a["w_out"])); up, down = tiles(a["w_up"]), tiles(a["w_down"])
    for half in range(2):
        add(up[half * FC // 2:(half + 1) * FC // 2])
        add(down[:, half * 2:(half + 1) * 2])
    assert len(blocks) == sum(n * b for _, n, b in PHASES)
    x = np.concatenate([a["x_prompt"][0], a["x_sample"].reshape(NS, D_MODEL)])
    x_t = x.T.reshape(KC, P, T).transpose(1, 0, 2)
    vec = np.zeros((P, VW), np.float32)
    def put(name, v):
        at, n = _V[name]
        vec[:v.shape[0], at:at + n] = v.reshape(v.shape[0], n)
    cols = lambda v: v.reshape(-1, P).T
    put("qg", cols(a["q_norm_g"])); put("kvg", cols(a["kv_norm_g"]))
    cw = a["conv_w"].reshape(CONV_W, NC, P)[:, order]
    put("convw", cw.transpose(2, 1, 0)); put("convb", a["conv_b"].reshape(NC, P)[order].T)
    put("dskip", cols(np.repeat(a["d_skip"], HEAD_DIM))); put("ssmg", cols(a["ssm_norm_g"]))
    for n, m in (("bgate", "b_gate"), ("ln1g", "ln1_g"), ("ln1b", "ln1_b"), ("bup", "b_up"), ("bdown", "b_down"),
                 ("ln2g", "ln2_g"), ("ln2b", "ln2_b")):
        put(n, cols(a[m]))
    put("dtb", a["dt_bias"][:, None]); put("alog", a["a_log"][:, None])
    cs = a["state_conv"].reshape(DEC_BATCH, 3, NC, P)[:, :, order].transpose(3, 2, 0, 1)
    ss = a["state_ssm"].reshape(DEC_BATCH, GROUPS, GW, D_STATE).transpose(1, 3, 0, 2)
    ckv_rows = a["cache_ckv"]
    ckv_cols = ckv_rows.reshape(N_POOL, PAGE, 2, P).transpose(0, 3, 2, 1).reshape(N_POOL, P, KV_LORA)
    rot = a["cache_krope"].reshape(N_POOL, 2, PAGE // 2, ROPE).transpose(0, 1, 3, 2).reshape(N_POOL, P, PAGE // 2)
    mem_t = a["mem_prompt"][0].T.reshape(KC, P, N_MEM).transpose(1, 0, 2)
    memk = a["cache_mem_k"].reshape(DEC_BATCH, N_MEM, 8, P).transpose(0, 3, 2, 1)
    memv = a["cache_mem_v"].reshape(DEC_BATCH, 2, P, 1024).transpose(0, 2, 1, 3)
    return dict(stream=np.stack(blocks), x_t=x_t, mem_t=mem_t, const=constants(), vec=vec, conv_state=cs, ssm_state=ss,
                pages=a["page_table"].reshape(1, -1).astype(np.int32), ckv_rows=ckv_rows,
                page_cols=np.concatenate([ckv_cols, rot], 2), memk_cols=memk, memv_rows=memv), order


def kernel(**inputs):
    import concourse.bacc as bacc
    from concourse import mybir
    from concourse.bass_utils import run_bass_kernel_spmd
    a = {k: np.asarray(v) for k, v in inputs.items()}
    ins, order = lay_out(a)
    nc = bacc.Bacc("TRN2", target_bir_lowering=False, num_devices=1)
    arrays, d = {}, {}
    for name, v in ins.items():
        v = np.ascontiguousarray(v)
        arrays["in_" + name] = v
        d[name] = nc.dram_tensor("in_" + name, v.shape, mybir.dt.from_np(v.dtype), kind="ExternalInput").ap()
    outs = {"y": (P, KC, T), "ckv": (P, 2, T), "krope": (ROPE, T), "mem_k": (P, 8, N_MEM), "mem_v": (P, 2, 1024),
            "ssm_p": (GROUPS, P, GW), "ssm_s": (GROUPS, P, DEC_BATCH, GW), "conv": (P, NC, 27)}
    o = {n: nc.dram_tensor("out_" + n, s, mybir.dt.float32, kind="ExternalOutput").ap() for n, s in outs.items()}
    program(nc, o=o, **d)
    r = run_bass_kernel_spmd(nc, [arrays], core_ids=[0]).results[0]
    back = np.argsort(order)
    def tokens(x):
        x = x.transpose(2, 1, 0).reshape(T, -1)
        return x[None, :SEQ], x[SEQ:].reshape(DEC_BATCH, DEC_SEQ, -1)
    y_p, y_s = tokens(r["out_y"])
    ckv_p, ckv_s = tokens(r["out_ckv"])
    kr_p, kr_s = tokens(r["out_krope"][:, None, :])
    mem_k = r["out_mem_k"].transpose(2, 1, 0).reshape(1, N_MEM, MEM_HEADS, MEM_DIM)
    mem_v = r["out_mem_v"].transpose(1, 0, 2).reshape(1, N_MEM, MEM_HEADS, MEM_DIM)
    ssm_p = r["out_ssm_p"].transpose(0, 2, 1).reshape(1, SSM_HEADS, HEAD_DIM, D_STATE)
    ssm_s = r["out_ssm_s"].transpose(2, 0, 3, 1).reshape(DEC_BATCH, SSM_HEADS, HEAD_DIM, D_STATE)
    conv = r["out_conv"][:, back]
    conv_p = conv[:, :, 0:3].transpose(2, 1, 0).reshape(1, 3, CONV_DIM)
    conv_s = conv[:, :, 3:].reshape(P, NC, DEC_BATCH, 3).transpose(2, 3, 1, 0).reshape(DEC_BATCH, 3, CONV_DIM)
    return (y_p, y_s, ckv_p, kr_p, mem_k, mem_v, ssm_p, conv_p, ckv_s, kr_s, ssm_s, conv_s)
```
